# Optimizing a Trainium2 kernel written in Bass

```python
import math
import jax, jax.numpy as jnp
from jax import lax
import numpy as np

D_MODEL = 1024
BATCH = 1
SEQ = 128
DEPTH = 2
DEC_BATCH = 1
DEC_SEQ = 256
PAST_LEN = 128

GRID_W = 64
N_LAYERS_AB = (DEPTH + 1) // 2
N_LAYERS_C = DEPTH // 2
EPS = 1e-6
LRU_WIDTH = D_MODEL
LRU_BLOCKS = 8
LRU_C = 8.0
CONV_W = 4
CONV_PAD = (2, 1)
GDN_HEADS = 8
GDN_DK = 128
GDN_DV = 128
GDN_QKV = 2 * GDN_HEADS * GDN_DK + GDN_HEADS * GDN_DV
GDN_CHUNK = 64
GLA_HEADS = 4
GLA_DK = D_MODEL // 2 // GLA_HEADS
GLA_DV = D_MODEL // GLA_HEADS
GLA_RANK = 16
GLA_TAU = 16.0
GLA_CHUNK = 32
N_EXPERTS = 16
N_GROUPS = 4
TOP_K = 2
D_EXPERT = 512
AB_IN = 2 * LRU_WIDTH + GDN_QKV + GDN_HEADS * GDN_DV + 4 * GDN_HEADS
AB_MIX = LRU_WIDTH + GDN_HEADS * GDN_DV
C_IN = 2 * GLA_HEADS * GLA_DK + 2 * GLA_HEADS * GLA_DV + 2 * GLA_RANK
C_MIX = GLA_HEADS * GLA_DV

kernel_name = "hybrid_rglru_gdn_gla_moe_prefix_diffusion_step"

F32 = jnp.float32

def _split(x, sizes):
    return jnp.split(x, np.cumsum(sizes)[:-1].tolist(), axis=-1)

def _rms_norm(x, g):
    xf = x.astype(F32)
    y = xf * lax.rsqrt(jnp.mean(xf * xf, axis=-1, keepdims=True) + EPS)
    return (y * g.astype(F32)).astype(x.dtype)

def _gated_rms_norm(o, z, g):
    B, T, H, V = o.shape
    y = o * lax.rsqrt(jnp.mean(o * o, axis=-1, keepdims=True) + EPS) * g.astype(F32)
    return (y.reshape(B, T, H * V) * jax.nn.silu(z.astype(F32))).astype(z.dtype)

def _l2norm(x):
    xf = x.astype(F32)
    return xf * lax.rsqrt(jnp.sum(xf * xf, axis=-1, keepdims=True) + EPS)

def _dwconv(x, w, b):
    C = x.shape[-1]
    y = lax.conv_general_dilated(x, w[:, None, :].astype(x.dtype), window_strides=(1,), padding=[CONV_PAD],
                                 dimension_numbers=('NWC', 'WIO', 'NWC'), feature_group_count=C)
    return y + b.astype(x.dtype)

def _lin_combine(e1, e2):
    a1, b1 = e1
    a2, b2 = e2
    return a1 * a2, a2 * b1 + b2

def _rglru_scan(x, h0, wa, ba, wx, bx, lam):
    B, T, W = x.shape
    xf = x.astype(F32)
    xb = xf.reshape(B, T, LRU_BLOCKS, W // LRU_BLOCKS)
    r = jax.nn.sigmoid(jnp.einsum('btni,nij->btnj', xb, wa.astype(F32)).reshape(B, T, W) + ba.astype(F32))
    ig = jax.nn.sigmoid(jnp.einsum('btni,nij->btnj', xb, wx.astype(F32)).reshape(B, T, W) + bx.astype(F32))
    log_a = -LRU_C * r * jax.nn.softplus(-lam.astype(F32))
    a = jnp.exp(log_a)
    b = jnp.sqrt(-jnp.expm1(2.0 * log_a)) * ig * xf
    b = b.at[:, 0].add(a[:, 0] * h0.astype(F32))
    _, h = lax.associative_scan(_lin_combine, (a, b), axis=1)
    return h

def _gated_delta_rule(q, k, v, g, beta, s0):
    B, T, H, _ = q.shape
    C = GDN_CHUNK
    N = T // C
    chunk = lambda t: t.astype(F32).reshape(B, N, C, *t.shape[2:])
    q, k, v, g, beta = chunk(q), chunk(k), chunk(v), chunk(g), chunk(beta)
    gc = jnp.cumsum(g, axis=2)
    idx = jnp.arange(C)
    causal = idx[:, None] >= idx[None, :]
    strict = idx[:, None] > idx[None, :]
    gh = jnp.moveaxis(gc, 3, 2)
    diff = gh[..., :, None] - gh[..., None, :]
    decay = jnp.where(causal, jnp.exp(jnp.where(causal, diff, 0.0)), 0.0)
    kb = k * beta[..., None]
    A = jnp.where(strict, jnp.einsum('bnihk,bnjhk->bnhij', kb, k) * decay, 0.0)
    eye = jnp.broadcast_to(jnp.eye(C, dtype=F32), A.shape)
    tmat = lax.linalg.triangular_solve(eye + A, eye, left_side=True, lower=True, unit_diagonal=True)
    u = jnp.einsum('bnhij,bnjhv->bnihv', tmat, v * beta[..., None])
    w = jnp.einsum('bnhij,bnjhk->bnihk', tmat, kb * jnp.exp(gc)[..., None])
    qk = jnp.einsum('bnihk,bnjhk->bnhij', q, k) * decay

    def step(s, xs):
        q_c, k_c, u_c, w_c, gc_c, qk_c = xs
        v_new = u_c - jnp.einsum('bihk,bhkv->bihv', w_c, s)
        o = (jnp.einsum('bihk,bhkv->bihv', q_c * jnp.exp(gc_c)[..., None], s)
             + jnp.einsum('bhij,bjhv->bihv', qk_c, v_new))
        g_last = gc_c[:, -1]
        k_dec = k_c * jnp.exp(g_last[:, None] - gc_c)[..., None]
        s = s * jnp.exp(g_last)[..., None, None] + jnp.einsum('bihk,bihv->bhkv', k_dec, v_new)
        return s, o

    xs = tuple(jnp.moveaxis(t, 1, 0) for t in (q, k, u, w, gc, qk))
    s, o = lax.scan(step, s0.astype(F32), xs)
    return jnp.moveaxis(o, 0, 1).reshape(B, T, H, -1), s

def _gla_chunked(q, k, v, glog, s0):
    B, T, H, _ = q.shape
    C = GLA_CHUNK
    N = T // C
    chunk = lambda t: t.astype(F32).reshape(B, N, C, *t.shape[2:])
    q, k, v, glog = chunk(q), chunk(k), chunk(v), chunk(glog)
    gc = jnp.cumsum(glog, axis=2)
    idx = jnp.arange(C)
    mask = (idx[:, None] >= idx[None, :])[:, :, None, None]
    diff = gc[:, :, :, None] - gc[:, :, None, :]
    decay = jnp.where(mask, jnp.exp(jnp.where(mask, diff, 0.0)), 0.0)
    A = jnp.einsum('bnihk,bnjhk,bnijhk->bnhij', q, k, decay)

    def step(s, xs):
        q_c, k_c, v_c, gc_c, a_c = xs
        o = (jnp.einsum('bihk,bhkv->bihv', q_c * jnp.exp(gc_c), s)
             + jnp.einsum('bhij,bjhv->bihv', a_c, v_c))
        g_last = gc_c[:, -1]
        k_dec = k_c * jnp.exp(g_last[:, None] - gc_c)
        s = s * jnp.exp(g_last)[..., None] + jnp.einsum('bihk,bihv->bhkv', k_dec, v_c)
        return s, o

    xs = tuple(jnp.moveaxis(t, 1, 0) for t in (q, k, v, gc, A))
    s, o = lax.scan(step, s0.astype(F32), xs)
    return jnp.moveaxis(o, 0, 1).reshape(B, T, H, -1), s

def _rev(t):
    return jnp.flip(t, 1)

def _mixer_ab(h, lru_h0, gdn_s0, with_state, w_in, lru_conv_w, lru_conv_b, lru_wa, lru_ba, lru_wx, lru_bx,
              lru_lam, gdn_conv_w, gdn_conv_b, gdn_a_log, gdn_dt_bias, gdn_norm_g, w_out):
    B, T, _ = h.shape
    H = GDN_HEADS
    y_br, x_br, qkv, z, a_raw, b_raw = _split(h @ w_in, [LRU_WIDTH, LRU_WIDTH, GDN_QKV, H * GDN_DV, 2 * H, 2 * H])
    xc = _dwconv(x_br, lru_conv_w, lru_conv_b)
    h_f = _rglru_scan(xc, lru_h0[:, 0], lru_wa[0], lru_ba[0], lru_wx[0], lru_bx[0], lru_lam[0])
    h_b = _rev(_rglru_scan(_rev(xc), lru_h0[:, 1], lru_wa[1], lru_ba[1], lru_wx[1], lru_bx[1], lru_lam[1]))
    lru_out = (jax.nn.gelu(y_br.astype(F32)) * (h_f + h_b)).astype(h.dtype)
    qkv = jax.nn.silu(_dwconv(qkv, gdn_conv_w, gdn_conv_b))
    q, k, v = _split(qkv, [H * GDN_DK, H * GDN_DK, H * GDN_DV])
    q = _l2norm(q.reshape(B, T, H, GDN_DK)) * (GDN_DK ** -0.5)
    k = _l2norm(k.reshape(B, T, H, GDN_DK))
    v = v.reshape(B, T, H, GDN_DV).astype(F32)
    g = -jnp.exp(gdn_a_log.astype(F32)) * jax.nn.softplus(a_raw.astype(F32).reshape(B, T, 2, H)
                                                          + gdn_dt_bias.astype(F32))
    beta = jax.nn.sigmoid(b_raw.astype(F32).reshape(B, T, 2, H))
    o_f, s_f = _gated_delta_rule(q, k, v, g[:, :, 0], beta[:, :, 0], gdn_s0[:, 0])
    o_b, s_b = _gated_delta_rule(_rev(q), _rev(k), _rev(v), _rev(g[:, :, 1]), _rev(beta[:, :, 1]), gdn_s0[:, 1])
    gdn_out = _gated_rms_norm(o_f + _rev(o_b), z, gdn_norm_g)
    out = jnp.concatenate([lru_out, gdn_out], axis=-1) @ w_out
    if with_state:
        lru_state = jnp.stack([h_f[:, -1], h_b[:, 0]], axis=1)
        gdn_state = jnp.stack([s_f, s_b], axis=1)
        return out, lru_state, gdn_state
    return out

def _mixer_c(h, s0, with_state, w_in, w2, b2, norm_g, w_out):
    B, T, _ = h.shape
    H = GLA_HEADS
    q, k, v, gz, lr = _split(h @ w_in, [H * GLA_DK, H * GLA_DK, H * GLA_DV, H * GLA_DV, 2 * GLA_RANK])
    q = q.astype(F32).reshape(B, T, H, GLA_DK) * (GLA_DK ** -0.5)
    k = k.astype(F32).reshape(B, T, H, GLA_DK)
    v = v.astype(F32).reshape(B, T, H, GLA_DV)
    glog = jax.nn.log_sigmoid(jnp.einsum('btdr,drk->btdk', lr.astype(F32).reshape(B, T, 2, GLA_RANK), w2.astype(F32))
                              + b2.astype(F32)) / GLA_TAU
    glog = glog.reshape(B, T, 2, H, GLA_DK)
    o_f, s_f = _gla_chunked(q, k, v, glog[:, :, 0], s0[:, 0])
    o_b, s_b = _gla_chunked(_rev(q), _rev(k), _rev(v), _rev(glog[:, :, 1]), s0[:, 1])
    out = _gated_rms_norm(o_f + _rev(o_b), gz, norm_g) @ w_out
    if with_state:
        return out, jnp.stack([s_f, s_b], axis=1)
    return out

def _moe(h, router_w, router_b, w_gate, w_up, w_down):
    s = jax.nn.sigmoid(jnp.einsum('btd,de->bte', h.astype(F32), router_w.astype(F32)))
    sel = s + router_b.astype(F32)
    grouped = sel.reshape(*sel.shape[:-1], N_GROUPS, N_EXPERTS // N_GROUPS)
    group_score = jnp.sum(lax.top_k(grouped, TOP_K)[0], axis=-1)
    g_best = jnp.argmax(group_score, axis=-1)
    in_group = (jnp.arange(N_EXPERTS) // (N_EXPERTS // N_GROUPS)) == g_best[..., None]
    _, top_idx = lax.top_k(jnp.where(in_group, sel, -jnp.inf), TOP_K)
    top_w = jnp.take_along_axis(s, top_idx, axis=-1)
    top_w = top_w / jnp.sum(top_w, axis=-1, keepdims=True)
    gates = jnp.sum(jax.nn.one_hot(top_idx, N_EXPERTS, dtype=F32) * top_w[..., None], axis=-2)
    hid = jax.nn.silu(jnp.einsum('btd,edf->btef', h, w_gate)) * jnp.einsum('btd,edf->btef', h, w_up)
    hid = hid * gates[..., None].astype(h.dtype)
    return jnp.einsum('btef,efd->btd', hid, w_down)

def _to_col_major(x):
    B, T, D = x.shape
    rows = T // GRID_W
    return x.reshape(B, rows, GRID_W, D).transpose(0, 2, 1, 3).reshape(B, T, D)

def _to_row_major(x):
    B, T, D = x.shape
    rows = T // GRID_W
    return x.reshape(B, GRID_W, rows, D).transpose(0, 2, 1, 3).reshape(B, T, D)

def setup_inputs(seed: int = 0) -> dict:
    key = jax.random.key(seed)
    ks = iter(jax.random.split(key, 48))
    nrm = lambda shape, scale: scale * jax.random.normal(next(ks), shape, F32)
    uni = lambda shape, lo, hi: jax.random.uniform(next(ks), shape, F32, lo, hi)
    D = D_MODEL
    bw = LRU_WIDTH // LRU_BLOCKS
    p = uni((N_LAYERS_AB, 2, LRU_WIDTH), 0.9, 0.999) ** (1.0 / LRU_C)
    dt = jnp.exp(uni((N_LAYERS_AB, 2, GDN_HEADS), math.log(1e-3), math.log(1e-1)))
    return {
        "x_prompt": nrm((BATCH, SEQ, D), 1.0),
        "x_sample": nrm((DEC_BATCH, DEC_SEQ, D), 1.0),
        "state_lru": nrm((DEC_BATCH, N_LAYERS_AB, 2, LRU_WIDTH), 0.5),
        "state_gdn": nrm((DEC_BATCH, N_LAYERS_AB, 2, GDN_HEADS, GDN_DK, GDN_DV), 0.1),
        "state_gla": nrm((DEC_BATCH, N_LAYERS_C, 2, GLA_HEADS, GLA_DK, GLA_DV), 0.1),
        "c": nrm((DEC_BATCH, D), 1.0),
        "c_ctx": nrm((D,), 1.0),
        "ada_w": nrm((DEPTH, D, 6 * D), 0.5 * D ** -0.5),
        "ada_b": nrm((DEPTH, 6 * D), 0.01),
        "norm1_g": 1.0 + nrm((DEPTH, D), 0.01),
        "norm2_g": 1.0 + nrm((DEPTH, D), 0.01),
        "final_norm_g": 1.0 + nrm((D,), 0.01),
        "ab_w_in": nrm((N_LAYERS_AB, D, AB_IN), D ** -0.5),
        "lru_conv_w": nrm((N_LAYERS_AB, CONV_W, LRU_WIDTH), CONV_W ** -0.5),
        "lru_conv_b": nrm((N_LAYERS_AB, LRU_WIDTH), 0.01),
        "lru_wa": nrm((N_LAYERS_AB, 2, LRU_BLOCKS, bw, bw), bw ** -0.5),
        "lru_ba": nrm((N_LAYERS_AB, 2, LRU_WIDTH), 0.01),
        "lru_wx": nrm((N_LAYERS_AB, 2, LRU_BLOCKS, bw, bw), bw ** -0.5),
        "lru_bx": nrm((N_LAYERS_AB, 2, LRU_WIDTH), 0.01),
        "lru_lam": jnp.log(p) - jnp.log1p(-p),
        "gdn_conv_w": nrm((N_LAYERS_AB, CONV_W, GDN_QKV), CONV_W ** -0.5),
        "gdn_conv_b": nrm((N_LAYERS_AB, GDN_QKV), 0.01),
        "gdn_a_log": jnp.log(uni((N_LAYERS_AB, 2, GDN_HEADS), 1.0, 16.0)),
        "gdn_dt_bias": dt + jnp.log(-jnp.expm1(-dt)),
        "gdn_norm_g": 1.0 + nrm((N_LAYERS_AB, GDN_DV), 0.01),
        "ab_w_out": nrm((N_LAYERS_AB, AB_MIX, D), AB_MIX ** -0.5),
        "gla_w_in": nrm((N_LAYERS_C, D, C_IN), D ** -0.5),
        "gla_w2": nrm((N_LAYERS_C, 2, GLA_RANK, GLA_HEADS * GLA_DK), GLA_RANK ** -0.5),
        "gla_b2": nrm((N_LAYERS_C, 2, GLA_HEADS * GLA_DK), 0.1),
        "gla_norm_g": 1.0 + nrm((N_LAYERS_C, GLA_DV), 0.01),
        "gla_w_out": nrm((N_LAYERS_C, C_MIX, D), C_MIX ** -0.5),
        "router_w": nrm((D, N_EXPERTS), D ** -0.5),
        "router_b": nrm((N_EXPERTS,), 0.01),
        "moe_w_gate": nrm((DEPTH, N_EXPERTS, D, D_EXPERT), D ** -0.5),
        "moe_w_up": nrm((DEPTH, N_EXPERTS, D, D_EXPERT), D ** -0.5),
        "moe_w_down": nrm((DEPTH, N_EXPERTS, D_EXPERT, D), D_EXPERT ** -0.5),
    }

def reference(x_prompt, x_sample, state_lru, state_gdn, state_gla, c, c_ctx, ada_w, ada_b, norm1_g, norm2_g,
              final_norm_g, ab_w_in, lru_conv_w, lru_conv_b, lru_wa, lru_ba, lru_wx, lru_bx, lru_lam, gdn_conv_w,
              gdn_conv_b, gdn_a_log, gdn_dt_bias, gdn_norm_g, ab_w_out, gla_w_in, gla_w2, gla_b2, gla_norm_g,
              gla_w_out, router_w, router_b, moe_w_gate, moe_w_up, moe_w_down):
    xp, xs = x_prompt, x_sample
    bp = xp.shape[0]
    new_lru, new_gdn, new_gla = [], [], []
    for i in range(DEPTH):
        j = i // 2
        mod_p = (jax.nn.silu(c_ctx) @ ada_w[i] + ada_b[i])[None, None, :]
        mod_s = (jax.nn.silu(c) @ ada_w[i] + ada_b[i])[:, None, :]
        sh1p, sc1p, g1p, sh2p, sc2p, g2p = jnp.split(mod_p, 6, axis=-1)
        sh1s, sc1s, g1s, sh2s, sc2s, g2s = jnp.split(mod_s, 6, axis=-1)
        hp = _rms_norm(xp, norm1_g[i]) * (1.0 + sc1p) + sh1p
        hs = _rms_norm(xs, norm1_g[i]) * (1.0 + sc1s) + sh1s
        if i % 2 == 0:
            ab = (ab_w_in[j], lru_conv_w[j], lru_conv_b[j], lru_wa[j], lru_ba[j], lru_wx[j], lru_bx[j], lru_lam[j],
                  gdn_conv_w[j], gdn_conv_b[j], gdn_a_log[j], gdn_dt_bias[j], gdn_norm_g[j], ab_w_out[j])
            zero_lru = jnp.zeros((bp, 2, LRU_WIDTH), F32)
            zero_gdn = jnp.zeros((bp, 2, GDN_HEADS, GDN_DK, GDN_DV), F32)
            op, lru_st, gdn_st = _mixer_ab(hp, zero_lru, zero_gdn, True, *ab)
            os_ = _mixer_ab(hs, state_lru[:, j], state_gdn[:, j], False, *ab)
            new_lru.append(lru_st)
            new_gdn.append(gdn_st)
        else:
            cp = (gla_w_in[j], gla_w2[j], gla_b2[j], gla_norm_g[j], gla_w_out[j])
            zero_gla = jnp.zeros((bp, 2, GLA_HEADS, GLA_DK, GLA_DV), F32)
            op, gla_st = _mixer_c(hp, zero_gla, True, *cp)
            os_ = _to_row_major(_mixer_c(_to_col_major(hs), state_gla[:, j], False, *cp))
            new_gla.append(gla_st)
        xp = xp + g1p * op
        xs = xs + g1s * os_
        hp = _rms_norm(xp, norm2_g[i]) * (1.0 + sc2p) + sh2p
        hs = _rms_norm(xs, norm2_g[i]) * (1.0 + sc2s) + sh2s
        xp = xp + g2p * _moe(hp, router_w, router_b, moe_w_gate[i], moe_w_up[i], moe_w_down[i])
        xs = xs + g2s * _moe(hs, router_w, router_b, moe_w_gate[i], moe_w_up[i], moe_w_down[i])
    y_prompt = _rms_norm(xp, final_norm_g)
    y_sample = _rms_norm(xs, final_norm_g)
    return (y_prompt, y_sample, jnp.stack(new_lru, axis=1), jnp.stack(new_gdn, axis=1), jnp.stack(new_gla, axis=1))


_drawn_inputs = setup_inputs


def setup_inputs(seed=0):
    import zlib

    import numpy as np

    out = dict(_drawn_inputs(seed))
    spreads = {}
    factors = {'state_gla': 64.0,
     'norm1_g': 2.959,
     'final_norm_g': 28.438,
     'lru_ba': 35.596,
     'lru_bx': 28.065,
     'gdn_conv_b': 4.335,
     'gdn_norm_g': 22.967,
     'gla_norm_g': 60.208,
     'norm2_g': 4.719,
     'lru_conv_b': 3.278,
     'router_b': 2.674}
    for name, (base, spread) in spreads.items():
        noise = np.random.default_rng([zlib.crc32(name.encode()), seed]).standard_normal(out[name].shape)
        drawn = base * np.exp(spread * noise) if base else spread * noise
        out[name] = __import__('jax').numpy.asarray(drawn.astype(out[name].dtype))
    for name, factor in factors.items():
        out[name] = (out[name] * factor).astype(out[name].dtype)
    return out
```

```python
import concourse.bass as bass
from concourse import mybir
from contextlib import ExitStack
import numpy as np

P = 128
D = 1024
KD = D // P
T_PROMPT, T_SAMPLE = 128, 256
T = T_PROMPT + T_SAMPLE
NT = T // P
SEGS = ((0, 0, T_PROMPT), (1, T_PROMPT, T_SAMPLE))
GRID_W = 64
EPS = 1e-6
CONV_W = 4
H = 4
HG = 2
DK = 128
E, DE = 16, 512
GLA_H, GLA_V = 4, 256
SUB = 32
SLOT = 2048
RING = 6
LEVELS = 7
CLAMP = 60.0
BIG = 1.0e30
SMALL = 960

_V = [("c", 16), ("ada_b", 96), ("n1", 16), ("n2", 16), ("nf", 8), ("lcw", 32), ("lcb", 8), ("lba", 16),
      ("lbx", 16), ("lam", 16), ("gcw", 96), ("gcb", 24), ("gng", 1), ("h0", 16), ("glb", 8), ("glg", 2),
      ("rb", 16), ("arow", 1), ("trow", 1)]
_C = [("ident", 128), ("ones", 128), ("neg_strict", 256), ("neg_incl", 256), ("pair", 256),
      ("lev", 768), ("esel", 1024), ("ehead", 32), ("sgn", 1), ("bwd", 1), ("eps", 1), ("neg1", 1), ("i16", 16),
      ("i4", 4)]


def columns(table):
    at, out = 0, {}
    for name, n in table:
        out[name] = (at, at + n)
        at += n
    return out, at


VC, NV = columns(_V)
CC, NCONST = columns(_C)


def constants():
    c = np.zeros((P, NCONST), np.float32)

    def put(name, a):
        c[:a.shape[0], CC[name][0]:CC[name][0] + a.shape[1]] = a

    j, i = np.arange(P)[:, None], np.arange(P)[None, :]
    put("ident", np.eye(P))
    put("ones", np.ones((P, P)))
    put("neg_strict", np.where(np.concatenate([j < i, j > i], 1), 0.0, -30000.0))
    put("neg_incl", np.where(np.concatenate([j <= i, j >= i], 1), 0.0, -30000.0))
    put("pair", np.concatenate([(i % 2 == 1) & (j == i - 1), (i % 2 == 0) & (j == i + 1)], 1).astype(np.float32))
    lev = np.zeros((P, 2, LEVELS - 1, 64))
    for d in range(2):
        for n in range(1, LEVELS):
            b = 2 ** n
            for col in range(64):
                first = (col // b) * 2 * b + (0 if d == 0 else b)
                lev[first:first + b, d, n - 1, col] = 1.0
    put("lev", lev.reshape(P, -1))
    es = np.zeros((8, 8, P))
    es[np.arange(8), np.arange(8)] = 1.0
    put("esel", es.reshape(8, -1))
    eh = np.zeros((P, H, 8))
    for h in range(H):
        eh[:, h, h] = eh[:, h, H + h] = 1.0
    put("ehead", eh.reshape(P, -1))
    put("sgn", np.repeat([1.0, -1.0], 64)[:, None])
    put("bwd", (np.arange(8) >= 4).astype(np.float32)[:, None])
    put("eps", np.full((P, 1), EPS))
    put("neg1", np.full((P, 1), -1.0))
    put("i16", np.tile(np.arange(16.0) - 1024.0, (P, 1)))
    put("i4", np.tile(np.arange(4.0) - 1024.0, (P, 1)))
    return c


PHASES = [("ada0", 24), ("ab", 24), ("ada1", 24), ("about", 8), ("moe0", 96), ("gla", 12), ("glaout", 4),
          ("moe1", 96)]
UNIT0, _n = {}, 0
for _name, _units in PHASES:
    UNIT0[_name] = _n
    _n += _units
N_UNITS = _n


def slot_bases():
    count, out = [0] * (2 * RING), {}
    for name, units in PHASES:
        out[name] = list(count)
        ring = 2 * RING if name.startswith("moe") else RING
        for u in range(units):
            count[u % ring] += 1
    return out


BASE = slot_bases()


def build(nc, ws, vec, const, x_in, rw_in, tail_in, tail2_in, w2_in, lruw_in, s_gdn, s_gla, y_out, st_lru, st_gdn,
          st_gla):
    F32 = mybir.dt.float32
    ALU = mybir.AluOpType
    ACT = mybir.ActivationFunctionType
    AX = mybir.AxisListType

    ctx = ExitStack()
    with ctx:
        def sb(name, shape):
            return ctx.enter_context(nc.sbuf_tensor(name, shape, F32))

        def sem(name):
            return ctx.enter_context(nc.semaphore(name))

        bank = [ctx.enter_context(nc.psum_tensor(f"bank{i}", [P, 512], F32)) for i in range(8)]

        xT = sb("xT", [P, KD, T])
        hT = sb("hT", [P, KD, T])
        mix = sb("mix", [P, 2 * KD, T])
        ring = sb("ring", [P, RING, SLOT])
        vecs = sb("vecs", [P, NV])
        cst = sb("cst", [P, NCONST])
        rw = sb("rw", [P, KD, E])
        small = sb("small", [P, SMALL])
        WORK = 24190
        work = sb("work", [P, WORK])

        def v(name, a=0, b=None):
            s, e = VC[name]
            return vecs[:, s + a:(e if b is None else s + b)]

        def cc(name, a=0, b=None, rows=P):
            s, e = CC[name]
            return cst[0:rows, s + a:(e if b is None else s + b)]

        ident, ones = cc("ident"), cc("ones")

        def carve(tile, start=0):
            at = [start]

            def take(n, *shape, rows=P):
                a = tile[0:rows, at[0]:at[0] + n]
                at[0] += n
                if len(shape) == 2:
                    return a.rearrange("p (a b) -> p a b", b=shape[1])
                if len(shape) == 3:
                    return a.rearrange("p (a b c) -> p a b c", b=shape[1], c=shape[2])
                if len(shape) == 4:
                    return a.rearrange("p (a b c d) -> p a b c d", b=shape[1], c=shape[2], d=shape[3])
                return a
            take.at = at
            return take

        tk = carve(small)
        cs = tk(16, 8, 2)
        mod = [tk(96, 48, 2) for _ in range(2)]
        gain = tk(16, 8, 2)
        sp = tk(16, 8, 2)
        nsp4 = tk(16, 8, 2)
        psp4 = tk(16, 8, 2)
        hba = tk(16, 8, 2)
        hbx = tk(16, 8, 2)
        z1, z2, z3, z4 = tk(16), tk(16), tk(16), tk(16)
        gp = tk(32, 4, 4, 2)
        gpx = tk(88)
        lru_st = tk(16, 8, 2)
        lnrow = tk(2)
        rstd = tk(T)
        assert tk.at[0] <= SMALL, tk.at

        slots = [ring[:, s, :] for s in range(RING)] + [work[:, s * SLOT:(s + 1) * SLOT] for s in range(RING)]
        normed, squares = mix[:, 0:KD, :], mix[:, KD:2 * KD, :]

        tk = carve(work)
        qT, kT = tk(H * T, H, T), tk(H * T, H, T)
        kTok, vTok = tk(H * T, NT, H, P), tk(H * T, NT, H, P)
        oT = tk(H * T, H, T)
        S = tk(2 * H * P, 2, H, P)
        gcR, lbR = tk(HG * T, HG, T, rows=8), tk(HG * T, HG, T, rows=8)
        glR = tk(HG * NT, HG, NT, rows=8)
        negC, rowA, rowQ, rowK, lbS = (tk(T, rows=8) for _ in range(5))
        cols = tk(4 * NT * 8, 4, NT, 8)
        ecols = tk(4 * NT * 8, 4, NT, 8)
        egl = tk(8 * NT, 8, NT)
        shared = tk.at[0]
        xc = tk(4 * T, 4, T)
        pad = [tk(390) for _ in range(2)]
        acc = tk(387)
        cv = [tk(T) for _ in range(2)]
        vT = [tk(T) for _ in range(2)]
        sqb = [tk(T) for _ in range(2)]
        gy = [tk(T) for _ in range(2)]
        rt, it_, aa, th = (tk(2 * T, 2, T) for _ in range(4))
        hf, hb = tk(T), tk(T)
        lruw = tk(2 * 512, 2, 4, P)
        assert tk.at[0] <= WORK, tk.at
        tk.at[0] = shared
        Gs, Qs = tk(NT * H * P, NT, H, P), tk(NT * H * P, NT, H, P)
        quad = []
        for _ in range(2):
            q = {n: tk(H * P, H, P) for n in ("N", "QK", "qe", "L", "U", "Tm", "kdec", "vb")}
            q["Ys"] = tk(H * 64, H, 64)
            quad.append(q)
        assert tk.at[0] <= WORK, tk.at
        mrow = work[0:2, 0:1536]
        tk.at[0] = shared
        tw = tk(KD * P, KD, P)
        tu, tv_, tabs = tk(T), tk(T), tk(T)
        psR = tk(HG * T, HG, T, rows=8)
        pt = tk(HG * T, HG, T, rows=8)
        gR = tk(HG * T, HG, T, rows=8)
        arow = tk(1)
        assert tk.at[0] <= WORK, tk.at

        tk = carve(work, RING * SLOT)
        rt_s, rt_sel, rt_m, rt_a, rt_b, rt_o1, rt_o2, gates_ = (tk(48, 3, 16) for _ in range(8))
        rt_mx, rt_mn = tk(24, 12, 2), tk(24, 12, 2)
        rt_t, rt_u, rt_g, rt_h = (tk(12) for _ in range(4))
        rt_k = tk(3)
        sg, hid, hidT = ([tk(DE) for _ in range(2)] for _ in range(3))
        assert tk.at[0] <= WORK, tk.at
        accf = mix[:, 0:KD, :].rearrange("p a b -> p (a b)").rearrange("p (t d) -> p t d", t=NT)

        tk = carve(work)
        gabs, gmin = tk(8 * T, 8, T), tk(8 * T, 8, T)
        gch = tk(2 * T, 2, T)
        gq, gk = tk(T), tk(T)
        gv = tk(NT * GLA_V, NT, GLA_V)
        go = tk(2 * T, 2, T)
        gsq = tk(2 * T, 2, T)
        gS = tk(2 * GLA_V, 2, GLA_V)
        incl = tk(2 * P, 2, P)
        glp = []
        for _ in range(2):
            glp.append({"ex": tk(512, 4, P), "qx": tk(P, 4, SUB), "qe": tk(P), "kd": tk(P), "kdT": tk(P), "AT": tk(P),
                        "egl": tk(1)})
        tw2, w2sb, lrT = tk(KD * P, KD, P), tk(512, rows=64), tk(T)
        grstd = tk(T)
        assert tk.at[0] <= WORK, tk.at

        const_loaded = sem("const_loaded")
        x_loaded = sem("x_loaded")
        group_start = sem("group_start")
        tail_loaded = sem("tail_loaded")
        slots_started = sem("slots_started")
        prep = sem("prep")
        prep_exp = sem("prep_exp")
        mod_read = sem("mod_read")
        mod_rows = sem("mod_rows")
        mod_turned = sem("mod_turned")
        mod_done = sem("mod_done")
        lru_prep = sem("lru_prep")
        sq_done = sem("sq_done")
        ms_done = sem("ms_done")
        ln_done = sem("ln_done")
        rstd_done = sem("rstd_done")
        normed_done = sem("normed_done")
        h_ready = sem("h_ready")
        x_ready = sem("x_ready")
        tail_done = sem("tail_done")
        tail_act = sem("tail_act")
        rows_ready = sem("rows_ready")
        proj_done = sem("proj_done")
        proj_read = sem("proj_read")
        conv_step = sem("conv_step")
        conv_done = sem("conv_done")
        silu_done = sem("silu_done")
        gates_done = sem("gates_done")
        lru_tanh = sem("lru_tanh")
        lru_mid = sem("lru_mid")
        lru_sqrt = sem("lru_sqrt")
        lru_u = sem("lru_u")
        lru_done = sem("lru_done")
        lru_b = sem("lru_b")
        sq_pool = sem("sq_pool")
        ss_done = sem("ss_done")
        lnr_done = sem("lnr_done")
        rows_dve = sem("rows_dve")
        tr_done = sem("tr_done")
        tr_read = sem("tr_read")
        y_mixed = sem("y_mixed")
        half_act = sem("half_act")
        half_dve = sem("half_dve")
        half_pool = sem("half_pool")
        lruw0_loaded = sem("lruw0_loaded")
        lruw1_loaded = sem("lruw1_loaded")
        gram_done = sem("gram_done")
        gram_read = sem("gram_read")
        cols_done = sem("cols_done")
        cols_copied = sem("cols_copied")
        cols_exp = sem("cols_exp")
        bc_done = sem("bc_done")
        arg_done = sem("arg_done")
        exp_done = sem("exp_done")
        n_done = sem("n_done")
        n_tr = sem("n_tr")
        l_done = sem("l_done")
        u_init = sem("u_init")
        u_tr = sem("u_tr")
        t_done = sem("t_done")
        quad_pool = sem("quad_pool")
        y_done = sem("y_done")
        y_masked = sem("y_masked")
        du_done = sem("du_done")
        u_done = sem("u_done")
        ks_done = sem("ks_done")
        r_done = sem("r_done")
        vnew_done = sem("vnew_done")
        v_read = sem("v_read")
        o_done = sem("o_done")
        o_read = sem("o_read")
        ds_done = sem("ds_done")
        s_done = sem("s_done")
        state_loaded = sem("state_loaded")
        state_saved = sem("state_saved")
        osq = sem("osq")
        oms = sem("oms")
        orstd = sem("orstd")
        omix = sem("omix")
        group_done = sem("group_done")
        out_done = sem("out_done")
        out_read = sem("out_read")
        router_done = sem("router_done")
        router_sig = sem("router_sig")
        gate_done = sem("gate_done")
        up_done = sem("up_done")
        sg_done = sem("sg_done")
        hid_done = sem("hid_done")
        htr_done = sem("htr_done")
        hidT_done = sem("hidT_done")
        down_done = sem("down_done")
        acc_done = sem("acc_done")
        acc_tr = sem("acc_tr")
        acc_added = sem("acc_added")
        tail2_loaded = sem("tail2_loaded")
        glr_done = sem("glr_done")
        glr_copied = sem("glr_copied")
        gpre_done = sem("gpre_done")
        gpre_act = sem("gpre_act")
        gpre_dve = sem("gpre_dve")
        gexp = sem("gexp")
        gproj_done = sem("gproj_done")
        gproj_read = sem("gproj_read")
        ghead = sem("ghead")
        gargs = sem("gargs")
        gexps = sem("gexps")
        gmul = sem("gmul")
        gA_done = sem("gA_done")
        gA_read = sem("gA_read")
        gkd_tr = sem("gkd_tr")
        gkd_done = sem("gkd_done")
        go_done = sem("go_done")
        go_read = sem("go_read")
        gds_done = sem("gds_done")
        gs_done = sem("gs_done")
        gs_saved = sem("gs_saved")
        gs_loaded = sem("gs_loaded")
        gosq = sem("gosq")
        goms = sem("goms")
        gorstd = sem("gorstd")
        gomix = sem("gomix")
        gfin = sem("gfin")
        y_ready = sem("y_ready")
        stored = sem("stored")
        loaded = [sem(f"slot{i}_loaded") for i in range(2 * RING)]
        free = [sem(f"slot{i}_free") for i in range(2 * RING)]
        block = ctx.enter_context(nc.Block())

        def step_counter(eng, signal, per=0):
            n = [0]

            def link(ins, base=0):
                n[0] += 1
                ins.then_inc(signal, 1)
                eng.wait_ge(signal, base + n[0])
            link.n = n
            return link

        def bc3(a, n):
            return a.unsqueeze(2).to_broadcast([a.shape[0], a.shape[1], n])

        def bcm(a, n):
            return a.unsqueeze(1).to_broadcast([a.shape[0], n, a.shape[1]])

        @block.sync
        def _(sp):
            sp.dma_start(vecs[:], vec).then_inc(const_loaded, 16)
            sp.dma_start(cst[:], const).then_inc(const_loaded, 16)
            sp.dma_start(rw[:], rw_in).then_inc(const_loaded, 16)
            sp.dma_start(xT[:], x_in).then_inc(x_loaded, 16)
            sp.dma_start(tw, tail_in).then_inc(tail_loaded, 16)
            sp.wait_ge(slots_started, 1)

            def stream(phase, rounds, n_slots, step):
                if rounds > 1:
                    with sp.Fori(0, rounds) as r:
                        for i in range(n_slots):
                            sp.wait_ge(free[i], r + (BASE[phase][i] + 1))
                            sp.dma_start(slots[i], ws[r * step + (UNIT0[phase] + i)]).then_inc(loaded[i], 16)
                else:
                    for i in range(n_slots):
                        sp.wait_ge(free[i % RING], BASE[phase][i % RING] + 1 + i // RING)
                        sp.dma_start(slots[i % RING], ws[UNIT0[phase] + i]).then_inc(loaded[i % RING], 16)

            stream("ada0", 4, RING, RING)
            with sp.Fori(0, HG) as g:
                for i in range(12):
                    n = i % RING
                    sp.wait_ge(free[n], g * 2 + (BASE["ab"][n] + 1 + i // RING))
                    sp.dma_start(slots[n], ws[g * 12 + (UNIT0["ab"] + i)]).then_inc(loaded[n], 16)
                for d in range(2):
                    sp.wait_ge(s_done, g * 4 + (d + 1))
                    sp.dma_start(st_gdn[g, d], S[:, d]).then_inc(state_saved, 16)
                sp.wait_ge(state_saved, g * 32 + 32)
                sp.dma_start(S, s_gdn[g]).then_inc(state_loaded, 16)
            stream("ada1", 4, RING, RING)
            stream("about", 1, 8, 0)

            def stream_experts(layer):
                phase = f"moe{layer}"
                for i in range(2 * RING):
                    if i == RING:
                        sp.wait_ge(x_ready, 2 * layer + 1)
                    sp.wait_ge(free[i], BASE[phase][i] + 1)
                    sp.dma_start(slots[i], ws[UNIT0[phase] + i]).then_inc(loaded[i], 16)
                with sp.Fori(1, E // 2) as r:
                    for i in range(2 * RING):
                        sp.wait_ge(free[i], r + (BASE[phase][i] + 1))
                        sp.dma_start(slots[i], ws[r * (2 * RING) + (UNIT0[phase] + i)]).then_inc(loaded[i], 16)

            sp.dma_start(st_lru, lru_st).then_inc(stored, 16)
            stream_experts(0)
            sp.wait_ge(x_ready, 2)
            sp.dma_start(tw2, tail2_in).then_inc(tail2_loaded, 16)
            sp.dma_start(w2sb, w2_in).then_inc(tail2_loaded, 16)
            with sp.Fori(0, 2) as r:
                for i in range(RING):
                    sp.wait_ge(free[i], r + (BASE["gla"][i] + 1))
                    sp.dma_start(slots[i], ws[r * RING + (UNIT0["gla"] + i)]).then_inc(loaded[i], 16)
                for hh in range(2):
                    sp.wait_ge(gs_done, r * 8 + (4 * hh + 2))
                    sp.dma_start(st_gla[r * 2 + hh], gS).then_inc(gs_saved, 16)
                    sp.wait_ge(gs_saved, r * 32 + (16 * hh + 16))
                    sp.dma_start(gS, s_gla[r * 2 + hh]).then_inc(gs_loaded, 16)
            stream("glaout", 1, 4, 0)
            stream_experts(1)
            sp.wait_ge(y_ready, 1)
            sp.dma_start(y_out, hT[:]).then_inc(stored, 16)
            sp.wait_ge(stored, 32)
            sp.wait_ge(gs_saved, 64)
            sp.wait_ge(state_saved, 64)

        @block.tensor
        def _(pe):
            mm, tr = pe.matmul, pe.transpose
            for i in range(2 * RING):
                pe.sem_inc(free[i], 1)
            pe.sem_inc(slots_started, 1)
            pe.wait_ge(const_loaded, 48)
            pe.wait_ge(prep_exp, 1)

            def ada(layer):
                phase = f"ada{layer}"
                with pe.Fori(0, 4) as r:
                    for i in range(RING):
                        pe.wait_ge(loaded[i], r * 16 + 16 * (BASE[phase][i] + 1))
                        w = slots[i].rearrange("p (m k c) -> p m k c", m=2, k=KD)
                        for k in range(KD):
                            last = mm(bank[i // 2][0:2, (i % 2) * 256:(i % 2) * 256 + 256], cs[:, k, :], w[:, :, k, :],
                                      start=(k == 0), stop=(k == KD - 1))
                        last.then_inc(free[i], 1)
                    pe.wait_ge(mod_rows, r + (4 * layer + 1))
                    for m in range(2 * RING):
                        last = mm(bank[7][:, 2 * m:2 * m + 2], mrow[:, m * P:(m + 1) * P], ident[0:2, 0:2],
                                  start=True, stop=True)
                    last.then_inc(mod_turned, 1)
                    pe.wait_ge(mod_read, r + (4 * layer + 1))

            def mean_square(n, slot_free=None):
                pe.wait_ge(sq_done, n + 1)
                for k in range(KD):
                    last = mm(bank[6][:, 0:T], ones, squares[:, k, :], start=(k == 0), stop=(k == KD - 1))
                    if k == 0 and slot_free is not None:
                        last.then_inc(slot_free, 1)
                last.then_inc(ms_done, 1)

            ada(0)
            mean_square(0)
            pe.wait_ge(h_ready, 1)
            pe.wait_ge(mod_done, 1)
            pe.wait_ge(tail_loaded, 16)
            for k in range(KD):
                last = mm(bank[7][:, 0:T], tw[:, k, :], hT[:, k, :], start=(k == 0), stop=(k == KD - 1))
            last.then_inc(tail_done, 1)

            with pe.Fori(0, HG) as g:
                def gates(i):
                    pe.wait_ge(conv_done, g * 16 + (i + 1))
                    pe.wait_ge((lruw0_loaded, lruw1_loaded)[i % 2], g * 32 + 16 * (i // 2 + 1))
                    if i:
                        pe.wait_ge(lru_tanh, g * 4 + i)
                    for n in range(4):
                        last = mm(bank[2 + n][:, 0:T], lruw[:, i % 2, n, :], xc[:, i, :], start=True, stop=True)
                    last.then_inc(gates_done, 1)

                def squares_sum(j):
                    pe.wait_ge(sq_pool, g * 8 + (j + 1))
                    if j == 4:
                        pe.wait_ge(lnr_done, g * 2 + 1)
                    if j == 0:
                        pe.wait_ge(rows_ready, 1)
                    mm(bank[7][0:8, 0:T], cc("ehead", 8 * (j % 4), 8 * (j % 4) + 8), sqb[j % 2],
                       start=(j % 4 == 0), stop=(j % 4 == 3)).then_inc(ss_done, 1)

                def to_tokens(j):
                    pe.wait_ge(silu_done, g * 12 + (4 + j + 1))
                    if j:
                        pe.wait_ge(tr_read, g * 8 + j)
                    src = kT[:, j, :] if j < 4 else vT[j % 2]
                    for t in range(NT):
                        last = tr(bank[6][:, t * P:(t + 1) * P], src[:, t * P:(t + 1) * P], ident)
                    last.then_inc(tr_done, 1)

                for b in range(24):
                    n = (b // 2) % RING
                    if b % 2 == 0:
                        pe.wait_ge(loaded[n], g * 32 + 16 * (BASE["ab"][n] + 1 + b // (2 * RING)))
                    pe.wait_ge(proj_read, g * 24 + (b + 1))
                    w = slots[n].rearrange("p (m k c) -> p m k c", m=2, k=KD)
                    for k in range(KD):
                        last = mm(bank[b % 2][:, 0:T], w[:, b % 2, k, :], hT[:, k, :], start=(k == 0),
                                  stop=(k == KD - 1))
                        if k == 0 and b % 2 == 0 and b:
                            last.then_inc(free[(b // 2 - 1) % RING], 1)
                    last.then_inc(proj_done, 1)
                    if 2 <= b < 6:
                        gates(b - 2)
                    if 6 <= b < 14:
                        squares_sum(b - 6)
                    if 10 <= b < 18:
                        to_tokens(b - 10)

                pe.wait_ge(half_act, g + 1)
                pe.wait_ge(half_dve, g + 1)
                for c in range(NT):
                    for n, x in enumerate((kT, qT)):
                        for h in range(H):
                            last = mm(bank[2 * c + n][:, h * P:(h + 1) * P], kT[:, h, c * P:(c + 1) * P],
                                      x[:, h, c * P:(c + 1) * P], start=True, stop=True)
                            if c + n + h == 0:
                                last.then_inc(free[RING - 1], 1)
                        last.then_inc(gram_done, 1)
                for n, row in enumerate((negC, lbS, rowA, rowK)):
                    for c in range(NT):
                        src = row[:, c * P:(c + 1) * P]
                        last = tr(bank[6][:, (n * NT + c) * 8:(n * NT + c) * 8 + 8], src, ident[0:8, 0:8])
                for r in range(8):
                    last = mm(bank[7][:, r * NT:(r + 1) * NT], cc("esel", r * P, (r + 1) * P, rows=8),
                              glR[:, g, :], start=True, stop=True)
                last.then_inc(cols_done, 1)
                pe.wait_ge(gram_read, g * 6 + 6)
                pe.wait_ge(cols_exp, g + 1)

                for stp in range(NT):
                    chunk = (stp, (0, 2, 1)[stp])
                    q0 = stp * 2
                    both = [(x, chunk[x], quad[x], bank[3 * x:3 * x + 3]) for x in range(2)]
                    for x, c, q, bk in both:
                        if stp:
                            pe.wait_ge(o_read, g * 6 + (q0 - 2 + x + 1))
                            pe.wait_ge(s_done, g * 4 + (2 * (stp - 1) + x + 1)) if stp < 3 else None
                        for n, row in enumerate((rowA, rowQ)):
                            for h in range(H):
                                last = mm(bk[n][:, h * P:(h + 1) * P],
                                          cc("esel", (4 * x + h) * P, (4 * x + h + 1) * P, rows=8),
                                          row[:, c * P:(c + 1) * P], start=True, stop=True)
                        last.then_inc(bc_done, 1)
                    for x, c, q, bk in both:
                        pe.wait_ge(n_done, g * 6 + (q0 + x + 1))
                        for h in range(H):
                            last = tr(bk[2][:, h * P:(h + 1) * P], q["N"][:, h, :], ident)
                        last.then_inc(n_tr, 1)
                    for lv in range(LEVELS):
                        for x, c, q, bk in both:
                            if lv:
                                b = 2 ** lv
                                pe.wait_ge(u_done, g * 42 + (q0 * 7 + 2 * (lv - 1) + x + 1))
                                if lv == 1:
                                    pe.wait_ge(l_done, g * 6 + (q0 + x + 1))
                                uv = q["U"].rearrange("p h (q t b) -> p h q t b", t=2, b=b)[:, :, :, 1 - x, :]
                                for h in range(H):
                                    last = mm(bk[1][:, h * 64:(h + 1) * 64].rearrange("p (q b) -> p q b", b=b),
                                              q["L"][:, h, :], uv[:, h], start=True, stop=True)
                                last.then_inc(y_done, 1)
                            else:
                                pe.wait_ge(u_done, g * 42 + (q0 * 7 + x + 1))
                            if lv < LEVELS - 1 and lv == 0:
                                pass
                        for x, c, q, bk in both:
                            if lv == 0:
                                for h in range(H):
                                    last = tr(bk[0][:, h * P:(h + 1) * P], q["U"][:, h, :], ident)
                                last.then_inc(u_tr, 1)
                                continue
                            b = 2 ** lv
                            pe.wait_ge(t_done, g * 36 + (q0 * 6 + 2 * (lv - 1) + x + 1))
                            pe.wait_ge(y_masked, g * 36 + (q0 * 6 + 2 * (lv - 1) + x + 1))
                            for h in range(H):
                                last = mm(bk[2][:, h * 64:(h + 1) * 64], q["Tm"][:, h, :], q["Ys"][:, h, :],
                                          start=True, stop=True)
                            last.then_inc(du_done, 1)
                        if 1 <= lv < LEVELS - 1:
                            for x, c, q, bk in both:
                                pe.wait_ge(u_done, g * 42 + (q0 * 7 + 2 * lv + x + 1))
                                for h in range(H):
                                    last = tr(bk[0][:, h * P:(h + 1) * P], q["U"][:, h, :], ident)
                                last.then_inc(u_tr, 1)
                    for x, c, q, bk in both:
                        if stp:
                            if stp == 1 and x == 0:
                                pe.wait_ge(state_loaded, g * 16 + 16)
                            for h in range(H):
                                last = mm(bank[6 + x][:, h * P:(h + 1) * P], kT[:, h, c * P:(c + 1) * P],
                                          S[:, x, h, :], start=True, stop=True)
                            last.then_inc(ks_done, 1)
                    for x, c, q, bk in both:
                        pe.wait_ge(u_done, g * 42 + (q0 * 7 + 12 + x + 1))
                        pe.wait_ge(quad_pool, g * 6 + (q0 + x + 1))
                        if stp:
                            pe.wait_ge(r_done, g * 4 + (q0 - 2 + x + 1))
                        R = q["Tm"] if stp else q["vb"]
                        for h in range(H):
                            last = mm(bk[1][:, h * P:(h + 1) * P], q["U"][:, h, :], R[:, h, :], start=True,
                                      stop=True)
                        last.then_inc(vnew_done, 1)
                    for x, c, q, bk in both:
                        pe.wait_ge(v_read, g * 6 + (q0 + x + 1))
                        for h in range(H):
                            dst = bk[2][:, h * P:(h + 1) * P]
                            if stp:
                                mm(dst, S[:, x, h, :], q["qe"][:, h, :], start=True, stop=False)
                            last = mm(dst, q["L"][:, h, :], q["QK"][:, h, :], start=not stp, stop=True)
                        last.then_inc(o_done, 1)
                        if stp < 2:
                            for h in range(H):
                                last = mm(bk[0][:, h * P:(h + 1) * P], q["kdec"][:, h, :], q["L"][:, h, :],
                                          start=True, stop=True)
                            last.then_inc(ds_done, 1)
                pe.wait_ge(osq, g + 1)
                for h in range(H):
                    last = mm(bank[h][:, 0:T], ones, kT[:, h, :], start=True, stop=True)
                last.then_inc(oms, 1)
                pe.wait_ge(group_done, g * 1 + 1)

            ada(1)
            pe.wait_ge(omix, HG)
            for m in range(KD):
                n = m % RING
                pe.wait_ge(loaded[n], 16 * (BASE["about"][n] + 1 + m // RING))
                if m >= 2:
                    pe.wait_ge(out_read, m - 1)
                w = slots[n].rearrange("p (k c) -> p k c", k=2 * KD)
                for k in range(2 * KD):
                    last = mm(bank[m % 2][:, 0:T], w[:, k, :], mix[:, k, :], start=(k == 0), stop=(k == 2 * KD - 1))
                    if k == 0 and m:
                        last.then_inc(free[(m - 1) % RING], 1)
                last.then_inc(out_done, 1)
            mean_square(1, free[(KD - 1) % RING])


            def experts(layer):
                phase, o = f"moe{layer}", 48 * layer
                pe.wait_ge(h_ready, 2 * layer + 2)
                for t in range(NT):
                    for k in range(KD):
                        last = mm(bank[7][:, t * E:(t + 1) * E], hT[:, k, t * P:(t + 1) * P], rw[:, k, :],
                                  start=(k == 0), stop=(k == KD - 1))
                last.then_inc(router_done, 1)
                with pe.Fori(0, E // 2) as ep:
                    def turn(n):
                        pe.wait_ge(hid_done, ep * 6 + (o + n + 1))
                        for j in range(DE // P):
                            last = tr(bank[4][:, j * P:(j + 1) * P], hid[n % 2][:, j * P:(j + 1) * P], ident)
                        last.then_inc(htr_done, 1)

                    def down(n):
                        so, t = n // 3 * RING, n % 3
                        if t == 0:
                            for i in (4, 5):
                                pe.wait_ge(loaded[so + i], ep * 16 + 16 * (BASE[phase][so + i] + 1))
                        pe.wait_ge(hidT_done, ep * 6 + (o + n + 1))
                        pe.wait_ge(acc_done, ep * 6 + (49 * layer + n + 1))
                        for half in range(2):
                            for j in range(DE // P):
                                w = slots[so + 4 + j // 2].rearrange("p (k d) -> p k d", k=2)
                                last = mm(bank[5 + half][:], hidT[n % 2][:, j * P:(j + 1) * P],
                                          w[:, j % 2, half * 512:(half + 1) * 512], start=(j == 0), stop=(j == 3))
                                if half == 1 and j == 1 and t == 2:
                                    last.then_inc(free[so + 4], 1)
                        last.then_inc(down_done, 1)

                    for n in range(6):
                        so, t = n // 3 * RING, n % 3
                        for kind, (bk, done) in enumerate(((n % 2, gate_done), (2 + n % 2, up_done))):
                            for k in range(KD):
                                i = so + 2 * kind + k // 4
                                if t == 0 and k % 4 == 0:
                                    pe.wait_ge(loaded[i], ep * 16 + 16 * (BASE[phase][i] + 1))
                                w = slots[i].rearrange("p (k f) -> p k f", k=4)
                                last = mm(bank[bk][:], hT[:, k, t * P:(t + 1) * P], w[:, k % 4, :],
                                          start=(k == 0), stop=(k == KD - 1))
                                if t == 2 and k == 3:
                                    last.then_inc(free[i], 1)
                                if t == 2 and kind == 1 and k == 0:
                                    last.then_inc(free[so + 1], 1)
                            last.then_inc(done, 1)
                            if n and kind == 0:
                                turn(n - 1)
                            if n and kind == 1:
                                down(n - 1)
                    turn(5)
                    down(5)
                pe.wait_ge(acc_done, 49 * layer + 49)
                for n in range(2 * NT):
                    if n >= 2:
                        pe.wait_ge(acc_added, 6 * layer + n - 1)
                    for j in range(4):
                        m = n % 2 * 4 + j
                        last = tr(bank[n % 2][:, j * P:(j + 1) * P], accf[:, n // 2, m * P:(m + 1) * P], ident)
                    last.then_inc(acc_tr, 1)

            def gla():
                pe.wait_ge(h_ready, 3)
                pe.wait_ge(tail2_loaded, 32)
                for k in range(KD):
                    last = mm(bank[7][:, 0:T], tw2[:, k, :], hT[:, k, :], start=(k == 0), stop=(k == KD - 1))
                last.then_inc(glr_done, 1)
                pe.wait_ge(glr_copied, 1)
                for n in range(8):
                    if n >= 4:
                        pe.wait_ge(gpre_act, n - 3)
                        pe.wait_ge(gpre_dve, n - 3)
                    d, h = n // 4, n % 4
                    mm(bank[n % 4][:, 0:T], w2sb[32 * d:32 * d + 32, h * P:(h + 1) * P], lrT[32 * d:32 * d + 32, :],
                       start=True, stop=True).then_inc(gpre_done, 1)
                pe.wait_ge(gpre_act, 8)
                pe.wait_ge(gpre_dve, 8)
                with pe.Fori(0, 2) as g:
                    for hh in range(2):
                        so = 3 * hh
                        for i in range(2):
                            pe.wait_ge(loaded[so + i], g * 16 + 16 * (BASE["gla"][so + i] + 1))
                            w = slots[so + i].rearrange("p (m k c) -> p m k c", m=2, k=KD)
                            for m in range(2):
                                for k in range(KD):
                                    last = mm(bank[2 * i + m][:, 0:T], w[:, m, k, :], hT[:, k, :], start=(k == 0),
                                              stop=(k == KD - 1))
                                    if i == 1 and m == 0 and k == 0:
                                        last.then_inc(free[so], 1)
                                last.then_inc(gproj_done, 1)
                        pe.wait_ge(loaded[so + 2], g * 16 + 16 * (BASE["gla"][so + 2] + 1))
                        w = slots[so + 2].rearrange("p (k c) -> p k c", k=KD)
                        for t in range(NT):
                            for k in range(KD):
                                last = mm(bank[4 + t // 2][:, t % 2 * 256:t % 2 * 256 + 256],
                                          hT[:, k, t * P:(t + 1) * P], w[:, k, :], start=(k == 0), stop=(k == KD - 1))
                                if t == 0 and k == 0:
                                    last.then_inc(free[so + 1], 1)
                        last.then_inc(gproj_done, 1)
                        pe.wait_ge(gproj_read, g * 10 + (5 * hh + 5))
                        pe.sem_inc(free[so + 2], 1)
                        for stp in range(NT):
                            chunk = (stp, (0, 2, 1)[stp])
                            q0 = 6 * hh + 2 * stp
                            for d in range(2):
                                b, bk = glp[d], bank[d::2]
                                pe.wait_ge(gmul, g * 12 + (q0 + d + 1))
                                for i in range(4):
                                    last = mm(bk[0][:, i * SUB:(i + 1) * SUB], b["ex"][:, i, :], b["qx"][:, i, :],
                                              start=True, stop=True)
                                last.then_inc(gA_done, 1)
                                tr(bk[1][:, 0:P], b["kd"], ident).then_inc(gkd_tr, 1)
                            for d in range(2):
                                b, bk, c = glp[d], bank[d::2], chunk[d]
                                pe.wait_ge(gA_read, g * 12 + (q0 + d + 1))
                                if stp == 1 and d == 0:
                                    pe.wait_ge(gs_loaded, g * 32 + (16 * hh + 16))
                                if stp == 2:
                                    pe.wait_ge(gs_done, g * 8 + (4 * hh + 2 + d + 1))
                                for j in range(2):
                                    dst = bk[2][:, j * P:(j + 1) * P]
                                    if stp:
                                        mm(dst, gS[:, d, j * P:(j + 1) * P], b["qe"], start=True, stop=False)
                                    last = mm(dst, gv[:, c, j * P:(j + 1) * P], b["AT"], start=not stp, stop=True)
                                last.then_inc(go_done, 1)
                                if stp < 2:
                                    pe.wait_ge(gkd_done, g * 8 + (4 * hh + 2 * stp + d + 1))
                                    mm(bk[3][:, 0:GLA_V], b["kdT"], gv[:, c, :], start=True, stop=True)\
                                        .then_inc(gds_done, 1)
                        pe.wait_ge(gosq, g * 2 + (hh + 1))
                        for j in range(2):
                            last = mm(bank[0][:, 0:T], ones, gsq[:, j, :], start=(j == 0), stop=(j == 1))
                        last.then_inc(goms, 1)
                        pe.wait_ge(gorstd, g * 2 + (hh + 1))
                pe.wait_ge(gomix, 4)
                for m in range(KD):
                    n = m // 2
                    if m % 2 == 0:
                        pe.wait_ge(loaded[n], 16 * (BASE["glaout"][n] + 1))
                    if m >= 2:
                        pe.wait_ge(out_read, KD + m - 1)
                    w = slots[n].rearrange("p (m k c) -> p m k c", m=2, k=KD)
                    for k in range(KD):
                        last = mm(bank[m % 2][:, 0:T], w[:, m % 2, k, :], mix[:, k, :], start=(k == 0),
                                  stop=(k == KD - 1))
                        if k == 0 and m % 2 == 0 and m:
                            last.then_inc(free[n - 1], 1)
                    last.then_inc(out_done, 1)

            experts(0)
            mean_square(2)
            gla()
            mean_square(3, free[3])
            experts(1)
            mean_square(4)

        @block.scalar
        def _(act):
            A = act.activation
            act.wait_ge(const_loaded, 48)
            A(cs.rearrange("p a b -> p (a b)"), v("c"), ACT.Silu).then_inc(prep_exp, 1)
            A(z2, v("lam"), ACT.Abs).then_inc(prep_exp, 1)
            act.wait_ge(prep_exp, 2)
            A(z1, z2, ACT.Exp, scale=-1.0).then_inc(prep_exp, 1)
            A(hba.rearrange("p a b -> p (a b)"), v("lba"), ACT.Copy, scale=0.5).then_inc(prep_exp, 1)
            A(hbx.rearrange("p a b -> p (a b)"), v("lbx"), ACT.Copy, scale=0.5).then_inc(prep_exp, 1)

            def norm(n):
                if n == 0:
                    act.wait_ge(x_loaded, 16)
                else:
                    act.wait_ge(x_ready, n)
                A(squares, xT[:], ACT.Square).then_inc(sq_done, 1)
                act.wait_ge(ms_done, n + 1)
                A(rstd, bank[6][:, 0:T], ACT.Ln, scale=1.0 / D, bias=cc("eps")).then_inc(ln_done, 1)
                act.wait_ge(ln_done, (1, 4, 5, 10, 11)[n])
                A(rstd, rstd, ACT.Exp, scale=-0.5).then_inc(rstd_done, 1)

            norm(0)
            link = step_counter(act, tail_act)
            link(A(arow, v("arow"), ACT.Exp))
            act.wait_ge(tail_done, 1)
            link(A(tu, bank[7][:, 0:T], ACT.Identity, scale=cc("sgn"), bias=v("trow")))
            link(A(tabs, tu, ACT.Abs))
            link(A(tabs, tabs, ACT.Exp, scale=-1.0))
            link(A(tabs, tabs, ACT.Ln, bias=1.0))
            act.sem_inc(proj_read, 2)

            with act.Fori(0, HG) as g:
                def load_gate_weights(i):
                    if i >= 2:
                        act.wait_ge(gates_done, g * 4 + (i - 1))
                    act.dma_start(lruw[:, i % 2], lruw_in[g * 4 + i])\
                        .then_inc((lruw0_loaded, lruw1_loaded)[i % 2], 16)

                def lru_gates(i):
                    act.wait_ge(gates_done, g * 4 + (i + 1))
                    if i:
                        act.wait_ge(lru_done, g * 4 + i)
                    for d in range(2):
                        A(rt[:, d, :], bank[2 + 2 * d][:, 0:T], ACT.Tanh, scale=0.5, bias=hba4(i, d, "a"))
                    for d in range(2):
                        last = A(it_[:, d, :], bank[3 + 2 * d][:, 0:T], ACT.Tanh, scale=0.5, bias=hba4(i, d, "x"))
                    last.then_inc(lru_tanh, 1)
                    act.wait_ge(lru_tanh, g * 4 + (i + 1))
                    for d in range(2):
                        n4 = gp[:, 0, i, d:d + 1]
                        A(aa[:, d, :], rt[:, d, :], ACT.Exp, scale=n4, bias=n4)
                    for d in range(2):
                        p4 = gp[:, 1, i, d:d + 1]
                        last = A(th[:, d, :], rt[:, d, :], ACT.Tanh, scale=p4, bias=p4)
                    last.then_inc(lru_mid, 1)

                def hba4(i, d, kind):
                    return gp[:, 2 if kind == "a" else 3, i, d:d + 1]

                act.wait_ge(group_start, g + 1)
                load_gate_weights(0)
                load_gate_weights(1)
                for b in range(28):
                    if b < 24:
                        act.wait_ge(proj_done, g * 24 + (b + 1))
                        src = bank[b % 2][:, 0:T]
                        if b < 16:
                            if b >= 2:
                                act.wait_ge(conv_done, g * 16 + (b - 1))
                            A(pad[b % 2][:, 2:2 + T_PROMPT], src[:, 0:T_PROMPT], ACT.Copy)
                            A(pad[b % 2][:, 133:133 + T_SAMPLE], src[:, T_PROMPT:T], ACT.Copy)\
                                .then_inc(proj_read, 1)
                        elif b < 20:
                            A(mix[:, g * 4 + (KD + b - 16), :], src, ACT.Silu).then_inc(proj_read, 1)
                        else:
                            if b >= 22:
                                act.wait_ge(y_mixed, g * 4 + (b - 21))
                            A(gy[b % 2], src, ACT.Gelu_apprx_tanh).then_inc(proj_read, 1)
                    if 5 <= b < 17:
                        n = b - 5
                        act.wait_ge(conv_done, g * 16 + (b - 1 + 1))
                        if n >= 10:
                            act.wait_ge(tr_done, g * 8 + (n - 4 - 2 + 1))
                        dst = qT[:, n, :] if n < 4 else kT[:, n - 4, :] if n < 8 else vT[n % 2]
                        A(dst, cv[(b - 1) % 2], ACT.Silu).then_inc(silu_done, 1)
                    if 4 <= b < 8:
                        act.wait_ge(lru_u, g * 4 + (b - 3))
                        A(rt, th, ACT.Sqrt, scale=0.25).then_inc(lru_sqrt, 1)
                    if 3 <= b < 7:
                        lru_gates(b - 3)
                        if b - 3 + 2 < 4:
                            load_gate_weights(b - 3 + 2)
                    if b == 10:
                        act.wait_ge(ss_done, g * 8 + 4)
                        A(rowQ, bank[7][0:8, 0:T], ACT.Ln, bias=cc("eps", rows=8)).then_inc(lnr_done, 1)
                    if b == 14:
                        act.wait_ge(ss_done, g * 8 + 8)
                        A(rowK, bank[7][0:8, 0:T], ACT.Ln, bias=cc("eps", rows=8)).then_inc(lnr_done, 1)
                act.wait_ge(silu_done, g * 12 + 12)
                act.wait_ge(proj_read, g * 24 + 26)
                act.sem_inc(half_act, 1)

                for c in range(NT):
                    for n, dst in enumerate((Gs, Qs)):
                        act.wait_ge(gram_done, g * 6 + (2 * c + n + 1))
                        if c == 0 and n == 0:
                            act.wait_ge(half_dve, g + 1)
                            act.wait_ge(half_pool, g + 1)
                        A(dst[:, c].rearrange("p h t -> p (h t)"), bank[2 * c + n][:], ACT.Copy)\
                            .then_inc(gram_read, 1)
                act.wait_ge(cols_copied, g + 1)
                A(ecols[:, 1:4].rearrange("p a b c -> p (a b c)"), cols[:, 1:4].rearrange("p a b c -> p (a b c)"),
                  ACT.Exp)
                A(egl.rearrange("p a b -> p (a b)"), bank[7][:, 0:8 * NT], ACT.Exp).then_inc(cols_exp, 1)
                for stp in range(NT):
                    q0 = stp * 2
                    for x in range(2):
                        q, bk = quad[x], bank[3 * x:3 * x + 3]
                        act.wait_ge(arg_done, g * 6 + (q0 + x + 1))
                        A(q["N"], q["N"], ACT.Exp)
                        A(q["QK"], q["QK"], ACT.Exp)
                        A(q["qe"].rearrange("p a b -> p (a b)"), bk[1][:], ACT.Exp).then_inc(exp_done, 1)
                    for x in range(2):
                        q, bk = quad[x], bank[3 * x:3 * x + 3]
                        act.wait_ge(n_tr, g * 6 + (q0 + x + 1))
                        A(q["L"].rearrange("p a b -> p (a b)"), bk[2][:], ACT.Copy).then_inc(l_done, 1)
                    for lv in range(LEVELS - 1):
                        for x in range(2):
                            q, bk = quad[x], bank[3 * x:3 * x + 3]
                            act.wait_ge(u_tr, g * 36 + (q0 * 6 + 2 * lv + x + 1))
                            A(q["Tm"].rearrange("p a b -> p (a b)"), bk[0][:], ACT.Copy).then_inc(t_done, 1)
                    for x in range(2):
                        q, bk = quad[x], bank[3 * x:3 * x + 3]
                        act.wait_ge(vnew_done, g * 6 + (q0 + x + 1))
                        A(q["L"].rearrange("p a b -> p (a b)"), bk[1][:], ACT.Copy).then_inc(v_read, 1)
                act.wait_ge(oms, g + 1)
                for h in range(H):
                    last = A(qT[:, h, :], bank[h][:, 0:T], ACT.Ln, scale=1.0 / DK, bias=cc("eps"))
                last.then_inc(ln_done, 1)
                act.wait_ge(ln_done, g + 2)
                A(qT, qT, ACT.Exp, scale=-0.5).then_inc(orstd, 1)
            norm(1)


            def experts(layer):
                o = 48 * layer
                act.wait_ge(router_done, layer + 1)
                A(rt_s.rearrange("p a b -> p (a b)"), bank[7][:, 0:NT * E], ACT.Sigmoid).then_inc(router_sig, 1)
                with act.Fori(0, E // 2) as ep:
                    def turned(n):
                        act.wait_ge(htr_done, ep * 6 + (o + n + 1))
                        A(hidT[n % 2], bank[4][:], ACT.Copy).then_inc(hidT_done, 1)

                    for n in range(6):
                        act.wait_ge(gate_done, ep * 6 + (o + n + 1))
                        A(sg[n % 2], bank[n % 2][:], ACT.Silu).then_inc(sg_done, 1)
                        if n:
                            turned(n - 1)
                    turned(5)

            def gla():
                act.wait_ge(glr_done, 1)
                A(lrT, bank[7][:, 0:T], ACT.Copy).then_inc(glr_copied, 1)
                for n in range(8):
                    act.wait_ge(gpre_done, n + 1)
                    A(gabs[:, n, :], bank[n % 4][:, 0:T], ACT.Abs, bias=v("glb", n, n + 1)).then_inc(gpre_act, 1)
                act.wait_ge(gpre_act, 8)
                A(gabs, gabs, ACT.Exp, scale=-1.0).then_inc(gexp, 1)
                act.wait_ge(gexp, 1)
                A(gabs, gabs, ACT.Ln, bias=1.0).then_inc(gexp, 1)
                with act.Fori(0, 2) as g:
                    for hh in range(2):
                        n0 = 5 * hh
                        act.wait_ge(gproj_done, g * 10 + (n0 + 1))
                        if hh == 0:
                            act.wait_ge(ghead, g * 2 + 1)
                        A(gq, bank[0][:, 0:T], ACT.Copy, scale=DK ** -0.5).then_inc(gproj_read, 1)
                        act.wait_ge(gproj_done, g * 10 + (n0 + 2))
                        A(gk, bank[1][:, 0:T], ACT.Copy).then_inc(gproj_read, 1)
                        for j in range(2):
                            act.wait_ge(gproj_done, g * 10 + (n0 + 3 + j))
                            A(mix[:, g * 4 + (2 * hh + j), :], bank[2 + j][:, 0:T], ACT.Silu).then_inc(gproj_read, 1)
                        act.wait_ge(gproj_done, g * 10 + (n0 + 5))
                        A(gv[:, 0:2].rearrange("p a b -> p (a b)"), bank[4][:], ACT.Copy)
                        A(gv[:, 2], bank[5][:, 0:GLA_V], ACT.Copy).then_inc(gproj_read, 1)
                        for stp in range(NT):
                            chunk = (stp, (0, 2, 1)[stp])
                            q0 = 6 * hh + 2 * stp
                            for d in range(2):
                                b, c = glp[d], chunk[d]
                                gc = gch[:, d, c * P:(c + 1) * P]
                                gl = gc[:, P - 1:P] if d == 0 else gc[:, 0:1]
                                act.wait_ge(gargs, g * 24 + (2 * (q0 + d) + 2))
                                A(b["ex"], b["ex"], ACT.Exp, scale=-1.0)
                                A(b["qx"], b["qx"], ACT.Exp)
                                A(b["qe"], gc, ACT.Exp)
                                A(b["egl"], gl, ACT.Exp)
                                A(b["kd"], gc, ACT.Exp, scale=-1.0, bias=gl).then_inc(gexps, 1)
                            if stp < 2:
                                for d in range(2):
                                    act.wait_ge(gkd_tr, g * 12 + (q0 + d + 1))
                                    A(glp[d]["kdT"], bank[d::2][1][:, 0:P], ACT.Copy).then_inc(gkd_done, 1)
                        act.wait_ge(goms, g * 2 + (hh + 1))
                        A(grstd, bank[0][:, 0:T], ACT.Ln, scale=1.0 / GLA_V, bias=cc("eps")).then_inc(ln_done, 1)
                        act.wait_ge(ln_done, g * 2 + (hh + 6))
                        A(grstd, grstd, ACT.Exp, scale=-0.5).then_inc(gorstd, 1)

            experts(0)
            norm(2)
            gla()
            norm(3)
            experts(1)
            norm(4)

        @block.gpsimd
        def _(pool):
            TT = pool.tensor_tensor
            pool.wait_ge(rows_ready, 1)
            with pool.Fori(0, HG) as g:
                pool.wait_ge(group_start, g + 1)
                for j in range(8):
                    pool.wait_ge(silu_done, g * 12 + (j + 1))
                    if j >= 2:
                        pool.wait_ge(ss_done, g * 8 + (j - 1))
                    src = qT[:, j, :] if j < 4 else kT[:, j - 4, :]
                    TT(sqb[j % 2], src, src, ALU.mult).then_inc(sq_pool, 1)
                pool.wait_ge(sq_pool, g * 8 + 8)
                pool.sem_inc(half_pool, 1)
                pool.wait_ge(cols_exp, g + 1)
                for stp in range(NT):
                    chunk = (stp, (0, 2, 1)[stp])
                    q0 = stp * 2
                    for x in range(2):
                        q, c = quad[x], chunk[x]
                        if stp:
                            pool.wait_ge(o_read, g * 6 + (q0 - 2 + x + 1))
                            pool.wait_ge(s_done, g * 4 + (q0 - 2 + x + 1))
                        TT(q["kdec"], kTok[:, c], bc3(ecols[:, 3, c, 4 * x:4 * x + 4], P), ALU.mult)
                        TT(q["vb"], vTok[:, c], bc3(ecols[:, 1, c, 4 * x:4 * x + 4], P), ALU.mult)
                        pool.wait_ge(exp_done, g * 6 + (q0 + x + 1))
                        TT(q["QK"], q["QK"], Qs[:, c], ALU.mult)
                        TT(q["qe"], q["qe"], qT[:, :, c * P:(c + 1) * P], ALU.mult).then_inc(quad_pool, 1)
                pool.wait_ge(quad_pool, g * 6 + 6)

            with pool.Fori(0, 2) as g:
                for hh in range(2):
                    pool.wait_ge(gproj_read, g * 10 + (5 * hh + 5))
                    for stp in range(NT):
                        chunk = (stp, (0, 2, 1)[stp])
                        q0 = 6 * hh + 2 * stp
                        for d in range(2):
                            b, sl = glp[d], slice(chunk[d] * P, (chunk[d] + 1) * P)
                            pool.wait_ge(gexps, g * 12 + (q0 + d + 1))
                            TT(b["ex"], b["ex"], bcm(gk[:, sl], 4), ALU.mult)
                            TT(b["qx"].rearrange("p a b -> p (a b)"), b["qx"].rearrange("p a b -> p (a b)"), gq[:, sl],
                               ALU.mult)
                            TT(b["qe"], b["qe"], gq[:, sl], ALU.mult)
                            TT(b["kd"], b["kd"], gk[:, sl], ALU.mult).then_inc(gmul, 1)

        @block.vector
        def _(dve):
            V = nc.vector
            TT, TS, STT = V.tensor_tensor, V.tensor_scalar, V.scalar_tensor_tensor
            dve.wait_ge(const_loaded, 48)
            link = line = step_counter(dve, prep)
            dve.wait_ge(prep_exp, 5)
            link(TS(z3, z1, 2.0, None, ALU.add))
            link(V.reciprocal(z4, z3))
            link(TT(z2, z1, z4, ALU.mult))
            link(TT(z3, z2, z2, ALU.mult))
            link(TS(z4, z3, 1.0 / 15, 1.0 / 13, ALU.mult, ALU.add))
            for m in (11, 9, 7, 5, 3, 1):
                link(TT(z4, z4, z3, ALU.mult))
                link(TS(z4, z4, 1.0 / m, None, ALU.add))
            link(TT(z4, z4, z2, ALU.mult))
            link(TS(z4, z4, 2.0, None, ALU.mult))
            link(TS(z3, v("lam"), -1.0, 0.0, ALU.mult, ALU.max))
            spf = sp.rearrange("p a b -> p (a b)")
            link(TT(spf, z4, z3, ALU.add))
            link(TS(nsp4.rearrange("p a b -> p (a b)"), spf, -4.0, None, ALU.mult))
            link(TS(psp4.rearrange("p a b -> p (a b)"), spf, 4.0, None, ALU.mult))
            dve.sem_inc(lru_prep, 1)

            def copy_of(dst, src):
                return TT(dst, src, src, ALU.max)

            def modulation(layer):
                phase, last_slot = f"ada{layer}", RING - 1
                with dve.Fori(0, 4) as r:
                    dve.wait_ge(free[last_slot], r + (BASE[phase][last_slot] + 2))
                    for n in range(3):
                        last = V.tensor_copy(mrow[:, n * 512:(n + 1) * 512], bank[n][0:2, :])
                    last.then_inc(mod_rows, 1)
                    dve.wait_ge(mod_turned, r + (4 * layer + 1))
                    TT(mod[layer][:, bass.ds(r * 12, 12), :], bank[7][:, 0:24].rearrange("p (a b) -> p a b", b=2),
                       bc3(vecs[:, bass.ds(r * 12 + (VC["ada_b"][0] + 48 * layer), 12)], 2), ALU.add)\
                        .then_inc(mod_read, 1)
                dve.wait_ge(mod_read, 4 * layer + 4)
                dve.sem_inc(mod_done, 1)

            def norm(n, permuted=False):
                layer, second = n // 2, n % 2
                dve.wait_ge(rstd_done, n + 1)
                m = mod[layer]
                sc, sh = m[:, 24 * second + 8:24 * second + 16, :], m[:, 24 * second:24 * second + 8, :]
                gn = v("n2" if second else "n1", 8 * layer, 8 * layer + 8)
                TS(gain, sc, 1.0, None, ALU.add).then_inc(normed_done, 1)
                dve.wait_ge(normed_done, 3 * n + 1)
                TT(gain, gain, bc3(gn, 2), ALU.mult).then_inc(normed_done, 1)
                TT(normed, xT[:], bcm(rstd, KD), ALU.mult).then_inc(normed_done, 1)
                dve.wait_ge(normed_done, 3 * n + 3)
                for k in range(KD):
                    for q, t0, tn in SEGS:
                        src, dst = normed[:, k, t0:t0 + tn], hT[:, k, t0:t0 + tn]
                        if permuted and q:
                            src = src.rearrange("p (r w) -> p w r", w=GRID_W)
                            dst = dst.rearrange("p (w r) -> p w r", w=GRID_W)
                        last = TS(dst, src, gain[:, k, q:q + 1], sh[:, k, q:q + 1], ALU.mult, ALU.add)
                last.then_inc(h_ready, 1)

            modulation(0)
            dve.wait_ge(mod_done, 1)
            norm(0)
            dve.wait_ge(tail_act, 5)
            link(STT(tv_, tu, 0.0, tabs, ALU.max, ALU.add))
            link(TS(tv_, tv_, arow, -1.0, ALU.mult, ALU.mult))
            for g in range(HG):
                V.tensor_copy(gR[:, g, :], tv_[32 * g:32 * g + 8, :])
                link(V.tensor_copy(lbR[:, g, :], tv_[64 + 32 * g:64 + 32 * g + 8, :]))
            for g in range(HG):
                for c in range(NT):
                    sl = slice(c * P, (c + 1) * P)
                    link(V.tensor_tensor_scan(psR[:, g, sl], cc("ones", rows=8), gR[:, g, sl], 0.0, ALU.mult,
                                              ALU.add))
            for g in range(HG):
                p3 = psR[:, g, :].rearrange("p (c t) -> p c t", t=P)
                g3 = gR[:, g, :].rearrange("p (c t) -> p c t", t=P)
                t3 = pt[:, g, :].rearrange("p (c t) -> p c t", t=P)
                link(V.tensor_copy(glR[:, g, :], p3[:, :, P - 1]))
                link(TT(t3, g3, bc3(glR[:, g, :], P), ALU.add))
                link(STT(pt[:, g, :], psR[:, g, :], -2.0, pt[:, g, :], ALU.mult, ALU.add))
                link(STT(gcR[:, g, :], pt[:, g, :], cc("bwd", rows=8), psR[:, g, :], ALU.mult, ALU.add))
            dve.sem_inc(rows_ready, 1)

            with dve.Fori(0, HG) as g:
                for n, src in enumerate((nsp4, psp4, hba, hbx)):
                    V.tensor_copy(gp[:, n], src[:, bass.ds(g * 4, 4), :])
                V.tensor_copy(gpx[:, 0:16], vecs[:, bass.ds(g * 16 + VC["lcw"][0], 16)])
                V.tensor_copy(gpx[:, 16:20], vecs[:, bass.ds(g * 4 + VC["lcb"][0], 4)])
                for n in range(3):
                    V.tensor_copy(gpx[:, 20 + 16 * n:36 + 16 * n],
                                  vecs[:, bass.ds(g * 16 + (VC["gcw"][0] + 32 * n), 16)])
                    V.tensor_copy(gpx[:, 68 + 4 * n:72 + 4 * n],
                                  vecs[:, bass.ds(g * 4 + (VC["gcb"][0] + 8 * n), 4)])
                V.tensor_copy(gpx[:, 80:88], vecs[:, bass.ds(g * 8 + VC["h0"][0], 8)])
                for n in range(2):
                    V.memset(pad[n][:, 0:2], 0.0)
                    V.memset(pad[n][:, 130:133], 0.0)
                    last = V.memset(pad[n][:, 389:390], 0.0)
                last.then_inc(group_start, 1)
                dve.wait_ge(group_start, g + 1)

                link = step_counter(dve, conv_step)
                CONV = 3 * 16
                state = [0]

                def conv(b):
                    kind, i = b // 4, b % 4
                    w = gpx[:, 4 * i:4 * i + 4] if kind == 0 else \
                        gpx[:, 20 + 16 * (kind - 1) + 4 * i:24 + 16 * (kind - 1) + 4 * i]
                    bias = gpx[:, 16 + i:17 + i] if kind == 0 else gpx[:, 64 + 4 * kind + i:65 + 4 * kind + i]
                    x, dst = pad[b % 2], (xc[:, i, :] if kind == 0 else cv[b % 2])
                    dve.wait_ge(proj_read, g * 24 + (b + 3))
                    link(TS(acc, x[:, 0:387], w[:, 0:1], bias, ALU.mult, ALU.add), g * CONV)
                    for n in range(1, 3):
                        link(STT(acc, x[:, n:n + 387], w[:, n:n + 1], acc, ALU.mult, ALU.add), g * CONV)
                    if b >= 6:
                        dve.wait_ge(silu_done, g * 12 + (b - 6 + 1))
                    STT(dst[:, 0:T_PROMPT], x[:, 3:3 + T_PROMPT], w[:, 3:4], acc[:, 0:T_PROMPT], ALU.mult, ALU.add)
                    STT(dst[:, T_PROMPT:T], x[:, 134:134 + T_SAMPLE], w[:, 3:4], acc[:, 131:387], ALU.mult,
                        ALU.add).then_inc(conv_done, 1)
                    dve.wait_ge(conv_done, g * 16 + (b + 1))

                def lru_factors(i):
                    dve.wait_ge(lru_mid, g * 4 + (i + 1))
                    TT(rt, aa, aa, ALU.mult).then_inc(lru_b, 1)
                    STT(it_, it_, 1.0, xc[:, i, :].unsqueeze(1).to_broadcast([P, 2, T]), ALU.add, ALU.mult)
                    dve.wait_ge(lru_b, g * 24 + (6 * i + 1))
                    STT(th, rt, 1.0, th, ALU.add, ALU.mult).then_inc(lru_u, 1)

                def lru_scan(i):
                    dve.wait_ge(lru_sqrt, g * 4 + (i + 1))
                    TT(it_, it_, rt, ALU.mult).then_inc(lru_b, 1)
                    dve.wait_ge(lru_b, g * 24 + (6 * i + 2))
                    scan = V.tensor_tensor_scan
                    h0f, h0b = gpx[:, 80 + 2 * i:81 + 2 * i], gpx[:, 81 + 2 * i:82 + 2 * i]
                    scan(hf[:, 0:128], aa[:, 0, 0:128], it_[:, 0, 0:128], 0.0, ALU.mult, ALU.add)
                    scan(hf[:, 128:T], aa[:, 0, 128:T], it_[:, 0, 128:T], h0f, ALU.mult, ALU.add)
                    scan(hb[:, 0:128][:, ::-1], aa[:, 1, 0:128][:, ::-1], it_[:, 1, 0:128][:, ::-1], 0.0, ALU.mult,
                         ALU.add)
                    scan(hb[:, 128:T][:, ::-1], aa[:, 1, 128:T][:, ::-1], it_[:, 1, 128:T][:, ::-1], h0b,
                         ALU.mult, ALU.add).then_inc(lru_b, 1)
                    dve.wait_ge(lru_b, g * 24 + (6 * i + 3))
                    copy_of(lru_st[:, bass.ds(g * 4 + i, 1), 0], hf[:, 127:128]).then_inc(lru_b, 1)
                    copy_of(lru_st[:, bass.ds(g * 4 + i, 1), 1], hb[:, 0:1]).then_inc(lru_b, 1)
                    TT(mix[:, g * 4 + i, :], hf, hb, ALU.add).then_inc(lru_b, 1)
                    dve.wait_ge(lru_b, g * 24 + (6 * i + 6))
                    dve.sem_inc(lru_done, 1)

                for b in range(26):
                    if 11 <= b < 19:
                        j = b - 11
                        dve.wait_ge(tr_done, g * 8 + (j + 1))
                        dst = (kTok if j < 4 else vTok)[:, :, j % 4, :]
                        V.tensor_copy(dst, bank[6][:, 0:T].rearrange("p (c t) -> p c t", t=P))\
                            .then_inc(tr_read, 1)
                    if b < 16:
                        conv(b)
                    if 4 <= b < 8:
                        lru_scan(b - 4)
                    if 3 <= b < 7:
                        lru_factors(b - 3)
                    if b >= 22:
                        i = b - 22
                        dve.wait_ge(proj_read, g * 24 + (20 + i + 3))
                        m = mix[:, g * 4 + i, :]
                        TT(m, m, gy[i % 2], ALU.mult).then_inc(y_mixed, 1)
                link = step_counter(dve, rows_dve)
                RW = 7
                dve.wait_ge(lnr_done, g * 2 + 2)
                gc = gcR[:, g, :]
                link(STT(negC, rowK, -0.5, gc, ALU.mult, ALU.subtract), g * RW)
                link(STT(rowA, rowK, -0.5, gc, ALU.mult, ALU.add), g * RW)
                link(TT(rowA, rowA, lbR[:, g, :], ALU.add), g * RW)
                link(STT(rowQ, rowQ, -0.5, gc, ALU.mult, ALU.add), g * RW)
                link(TS(rowQ, rowQ, float(np.log(DK ** -0.5)), None, ALU.add), g * RW)
                link(TT(rowK.rearrange("p (c t) -> p c t", t=P), negC.rearrange("p (c t) -> p c t", t=P),
                        bc3(glR[:, g, :], P), ALU.add), g * RW)
                link(copy_of(lbS, lbR[:, g, :]), g * RW)
                assert link.n[0] == RW
                dve.wait_ge(y_mixed, g * 4 + 4)
                dve.wait_ge(tr_read, g * 8 + 8)
                dve.sem_inc(half_dve, 1)

                dve.wait_ge(cols_done, g + 1)
                V.tensor_copy(cols.rearrange("p a b c -> p (a b c)"), bank[6][:, 0:4 * NT * 8])\
                    .then_inc(cols_copied, 1)
                dve.wait_ge(cols_exp, g + 1)
                dve.wait_ge(cols_copied, g + 1)
                dve.wait_ge(gram_read, g * 6 + 6)
                TS(ecols[:, 2].rearrange("p a b -> p (a b)"), ecols[:, 2].rearrange("p a b -> p (a b)"), -1.0, None,
                   ALU.mult)
                for stp in range(NT):
                    chunk = (stp, (0, 2, 1)[stp])
                    q0 = stp * 2
                    both = [(x, chunk[x], quad[x], bank[3 * x:3 * x + 3]) for x in range(2)]
                    for x, c, q, bk in both:
                        dve.wait_ge(bc_done, g * 6 + (q0 + x + 1))
                        for h in range(H):
                            nc_ = cols[:, 0, c, 4 * x + h:4 * x + h + 1]
                            STT(q["N"][:, h, :], bk[0][:, h * P:(h + 1) * P], nc_,
                                cc("neg_strict", x * P, x * P + P), ALU.add, ALU.add)
                            last = STT(q["QK"][:, h, :], bk[1][:, h * P:(h + 1) * P], nc_,
                                       cc("neg_incl", x * P, x * P + P), ALU.add, ALU.add)
                        last.then_inc(arg_done, 1)
                    for x, c, q, bk in both:
                        dve.wait_ge(exp_done, g * 6 + (q0 + x + 1))
                        TT(q["N"], q["N"], Gs[:, c], ALU.mult).then_inc(n_done, 1)
                        dve.wait_ge(n_done, g * 6 + (q0 + x + 1))
                        TT(q["U"], q["N"], bcm(cc("pair", x * P, x * P + P), H), ALU.mult).then_inc(u_init, 1)
                        dve.wait_ge(u_init, g * 6 + (q0 + x + 1))
                        TT(q["U"], bcm(ident, H), q["U"], ALU.subtract).then_inc(u_done, 1)
                    for lv in range(1, LEVELS):
                        b = 2 ** lv
                        n0 = q0 * 6 + 2 * (lv - 1)
                        for x, c, q, bk in both:
                            dve.wait_ge(y_done, g * 36 + (n0 + x + 1))
                            mk = cc("lev", x * 384 + (lv - 1) * 64, x * 384 + lv * 64)
                            TT(q["Ys"], bk[1][:, 0:256].rearrange("p (h c) -> p h c", h=H), bcm(mk, H), ALU.mult)\
                                .then_inc(y_masked, 1)
                        for x, c, q, bk in both:
                            dve.wait_ge(du_done, g * 36 + (n0 + x + 1))
                            uv = q["U"].rearrange("p h (q t b) -> p h q t b", t=2, b=b)[:, :, :, 1 - x, :]
                            TT(uv, uv, bk[2][:, 0:256].rearrange("p (h q b) -> p h q b", h=H, b=b), ALU.subtract)\
                                .then_inc(u_done, 1)
                    for x, c, q, bk in both:
                        if stp:
                            dve.wait_ge(ks_done, g * 4 + (q0 - 2 + x + 1))
                            dve.wait_ge(quad_pool, g * 6 + (q0 + x + 1))
                            for h in range(H):
                                last = STT(q["Tm"][:, h, :], bank[6 + x][:, h * P:(h + 1) * P],
                                           ecols[:, 2, c, 4 * x + h:4 * x + h + 1], q["vb"][:, h, :], ALU.mult,
                                           ALU.add)
                            last.then_inc(r_done, 1)
                    for x, c, q, bk in both:
                        dve.wait_ge(o_done, g * 6 + (q0 + x + 1))
                        o = oT[:, :, c * P:(c + 1) * P]
                        first = stp + x == 0 or stp == 1
                        po = bk[2][:].rearrange("p (h t) -> p h t", h=H)
                        if first:
                            V.tensor_copy(o, po).then_inc(o_read, 1)
                        else:
                            TT(o, o, po, ALU.add).then_inc(o_read, 1)
                        dve.wait_ge(o_read, g * 6 + (q0 + x + 1))
                        if stp < 2:
                            dve.wait_ge(ds_done, g * 4 + (q0 + x + 1))
                            if stp == 0:
                                V.tensor_copy(S[:, x].rearrange("p a b -> p (a b)"), bk[0][:]).then_inc(s_done, 1)
                            else:
                                for h in range(H):
                                    last = STT(S[:, x, h, :], S[:, x, h, :], egl[:, 4 * x + h, c:c + 1],
                                               bk[0][:, h * P:(h + 1) * P], ALU.mult, ALU.add)
                                last.then_inc(s_done, 1)
                TT(kT, oT, oT, ALU.mult).then_inc(osq, 1)
                dve.wait_ge(orstd, g + 1)
                STT(oT, oT, v("gng"), qT, ALU.mult, ALU.mult).then_inc(group_done, 1)
                dve.wait_ge(group_done, g + 1)
                m = mix[:, bass.ds(g * 4 + KD, 4), :]
                TT(m, m, oT, ALU.mult).then_inc(omix, 1)
                dve.wait_ge(omix, g + 1)

            modulation(1)
            dve.wait_ge(mod_done, 2)
            for m in range(KD):
                dve.wait_ge(out_done, m + 1)
                for q, t0, tn in SEGS:
                    xs = xT[:, m, t0:t0 + tn]
                    last = STT(xs, bank[m % 2][:, t0:t0 + tn], mod[0][:, 16 + m, q:q + 1], xs, ALU.mult, ALU.add)
                last.then_inc(out_read, 1)
            dve.wait_ge(out_read, KD)
            dve.sem_inc(x_ready, 1)
            norm(1)

            def route(layer):
                L = line
                flat = lambda a: a.rearrange("p a b -> p (a b)")
                dve.wait_ge(router_sig, layer + 1)
                L(TT(rt_sel, rt_s, bcm(v("rb"), NT), ALU.add))
                four = flat(rt_sel).rearrange("p (g e) -> p g e", e=4)
                L(TT(rt_mx, four[:, :, 0::2], four[:, :, 1::2], ALU.max))
                L(TT(rt_mn, four[:, :, 0::2], four[:, :, 1::2], ALU.min))
                L(TT(rt_t, rt_mx[:, :, 0], rt_mx[:, :, 1], ALU.max))
                L(TT(rt_u, rt_mx[:, :, 0], rt_mx[:, :, 1], ALU.min))
                L(TT(rt_g, rt_mn[:, :, 0], rt_mn[:, :, 1], ALU.max))
                L(TT(rt_u, rt_u, rt_g, ALU.max))
                L(TT(rt_t, rt_t, rt_u, ALU.add))
                g3 = lambda a: a.rearrange("p (t g) -> p t g", g=4)
                L(V.tensor_reduce(rt_k, g3(rt_t), AX.X, ALU.max))
                L(TT(g3(rt_g), g3(rt_t), bc3(rt_k, 4), ALU.is_ge))
                L(TT(g3(rt_g), g3(rt_g), bcm(cc("i4"), NT), ALU.mult))
                L(V.tensor_reduce(rt_k, g3(rt_g), AX.X, ALU.min))
                L(TT(g3(rt_h), bc3(rt_k, 4), bcm(cc("i4"), NT), ALU.is_equal))
                member = rt_h.unsqueeze(2).to_broadcast([P, 12, 4])
                m4 = flat(rt_m).rearrange("p (g e) -> p g e", e=4)
                L(TT(m4, four, member, ALU.mult))
                L(TS(rt_u, rt_h, BIG, -BIG, ALU.mult, ALU.add))
                L(TT(m4, m4, rt_u.unsqueeze(2).to_broadcast([P, 12, 4]), ALU.add))
                for first, hot in ((True, rt_o1), (False, rt_o2)):
                    L(V.tensor_reduce(rt_k, rt_m, AX.X, ALU.max))
                    L(TT(rt_a, rt_m, bc3(rt_k, E), ALU.is_ge))
                    L(TT(rt_a, rt_a, bcm(cc("i16"), NT), ALU.mult))
                    L(V.tensor_reduce(rt_k, rt_a, AX.X, ALU.min))
                    L(TT(hot, bc3(rt_k, E), bcm(cc("i16"), NT), ALU.is_equal))
                    if first:
                        L(STT(flat(rt_m), flat(hot), -2.0 * BIG, flat(rt_m), ALU.mult, ALU.add))
                L(TT(rt_a, rt_o1, rt_o2, ALU.add))
                L(TT(rt_a, rt_a, rt_s, ALU.mult))
                L(V.tensor_reduce(rt_k, rt_a, AX.X, ALU.add))
                L(V.reciprocal(rt_k, rt_k))
                L(TT(gates_, rt_a, bc3(rt_k, E), ALU.mult))

            def experts(layer):
                o = 48 * layer
                dve.wait_ge(h_ready, 2 * layer + 2)
                V.memset(mix[:, 0:KD, :], 0.0).then_inc(acc_done, 1)
                dve.wait_ge(acc_done, 49 * layer + 1)
                route(layer)
                with dve.Fori(0, E // 2) as ep:
                    def add(n):
                        t = n % 3
                        dve.wait_ge(down_done, ep * 6 + (o + n + 1))
                        if t == 2:
                            dve.sem_inc(free[n // 3 * RING + 5], 1)
                        for half in range(2):
                            a = accf[:, t, half * 512:(half + 1) * 512]
                            last = TT(a, a, bank[5 + half][:], ALU.add)
                        last.then_inc(acc_done, 1)

                    for n in range(6):
                        dve.wait_ge(sg_done, ep * 6 + (o + n + 1))
                        dve.wait_ge(up_done, ep * 6 + (o + n + 1))
                        STT(hid[n % 2], bank[2 + n % 2][:], gates_[:, n % 3, bass.ds(ep * 2 + n // 3, 1)], sg[n % 2],
                            ALU.mult, ALU.mult).then_inc(hid_done, 1)
                        if n == 2 or n == 5:
                            dve.sem_inc(free[n // 3 * RING + 3], 1)
                        if n:
                            add(n - 1)
                    add(5)
                for n in range(2 * NT):
                    dve.wait_ge(acc_tr, 6 * layer + n + 1)
                    t, q = n // 2, min(n // 2, 1)
                    for j in range(4):
                        m = n % 2 * 4 + j
                        xs = xT[:, m, t * P:(t + 1) * P]
                        last = STT(xs, bank[n % 2][:, j * P:(j + 1) * P], mod[layer][:, 40 + m, q:q + 1], xs, ALU.mult,
                                   ALU.add)
                    last.then_inc(acc_added, 1)
                dve.wait_ge(acc_added, 6 * layer + 6)
                dve.sem_inc(x_ready, 1)

            def gla():
                TS(incl, cc("neg_incl").rearrange("p (a b) -> p a b", a=2), -1.0, None, ALU.is_ge)
                for n in range(8):
                    dve.wait_ge(gpre_act, n + 1)
                    TS(gmin[:, n, :], bank[n % 4][:, 0:T], v("glb", n, n + 1), 0.0, ALU.add, ALU.min)\
                        .then_inc(gpre_dve, 1)
                dve.wait_ge(gexp, 2)
                dve.wait_ge(gpre_dve, 8)
                link = line
                link(TT(gmin, gmin, gabs, ALU.subtract))
                link(TS(gmin, gmin, 1.0 / 16.0, None, ALU.mult))
                for n in range(8):
                    for c in range(NT):
                        src, dst = gmin[:, n, c * P:(c + 1) * P], gabs[:, n, c * P:(c + 1) * P]
                        if n >= 4:
                            src, dst = src[:, ::-1], dst[:, ::-1]
                        last = V.tensor_tensor_scan(dst, ones, src, 0.0, ALU.mult, ALU.add)
                link(last)
                with dve.Fori(0, 2) as g:
                    for hh in range(2):
                        for d in range(2):
                            last = copy_of(gch[:, d, :], gabs[:, g * 2 + (4 * d + hh), :])
                        last.then_inc(ghead, 1)
                        dve.wait_ge(ghead, g * 2 + (hh + 1))
                        for stp in range(NT):
                            chunk = (stp, (0, 2, 1)[stp])
                            q0 = 6 * hh + 2 * stp
                            for d in range(2):
                                b, c = glp[d], chunk[d]
                                gc = gch[:, d, c * P:(c + 1) * P]
                                ref = gc[:, SUB // 2 - 1 + d::SUB]
                                TT(b["qx"], gc.rearrange("p (i t) -> p i t", t=SUB), bc3(ref, SUB), ALU.subtract)
                                TT(b["ex"], bcm(gc, 4), bc3(ref, P), ALU.subtract).then_inc(gargs, 1)
                                dve.wait_ge(gargs, g * 24 + (2 * (q0 + d) + 1))
                                TS(b["ex"], b["ex"], -CLAMP, None, ALU.max).then_inc(gargs, 1)
                            for d in range(2):
                                dve.wait_ge(gA_done, g * 12 + (q0 + d + 1))
                                TT(glp[d]["AT"], bank[d][:, 0:P], incl[:, d, :], ALU.mult).then_inc(gA_read, 1)
                            for d in range(2):
                                b, c = glp[d], chunk[d]
                                dve.wait_ge(go_done, g * 12 + (q0 + d + 1))
                                o = go[:, :, c * P:(c + 1) * P]
                                po = bank[4 + d][:, 0:2 * P].rearrange("p (j t) -> p j t", j=2)
                                if stp + d == 0 or stp == 1:
                                    V.tensor_copy(o, po).then_inc(go_read, 1)
                                else:
                                    TT(o, o, po, ALU.add).then_inc(go_read, 1)
                                dve.wait_ge(go_read, g * 12 + (q0 + d + 1))
                                if stp < 2:
                                    dve.wait_ge(gds_done, g * 8 + (4 * hh + 2 * stp + d + 1))
                                    if stp == 0:
                                        V.tensor_copy(gS[:, d, :], bank[6 + d][:, 0:GLA_V]).then_inc(gs_done, 1)
                                    else:
                                        STT(gS[:, d, :], gS[:, d, :], b["egl"], bank[6 + d][:, 0:GLA_V], ALU.mult,
                                            ALU.add).then_inc(gs_done, 1)
                        TT(gsq, go, go, ALU.mult).then_inc(gosq, 1)
                        dve.wait_ge(gorstd, g * 2 + (hh + 1))
                        for j in range(2):
                            last = STT(go[:, j, :], go[:, j, :], v("glg", j, j + 1), grstd, ALU.mult, ALU.mult)
                        last.then_inc(gfin, 1)
                        dve.wait_ge(gfin, g * 2 + (hh + 1))
                        m = mix[:, bass.ds(g * 4 + 2 * hh, 2), :]
                        TT(m, m, go, ALU.mult).then_inc(gomix, 1)
                        dve.wait_ge(gomix, g * 2 + (hh + 1))
                for m in range(KD):
                    dve.wait_ge(out_done, KD + m + 1)
                    for q, t0, tn in SEGS:
                        xs, ps = xT[:, m, t0:t0 + tn], bank[m % 2][:, t0:t0 + tn]
                        if q:
                            xs = xs.rearrange("p (r w) -> p w r", w=GRID_W)
                            ps = ps.rearrange("p (w r) -> p w r", w=GRID_W)
                        last = STT(xs, ps, mod[1][:, 16 + m, q:q + 1], xs, ALU.mult, ALU.add)
                    last.then_inc(out_read, 1)
                dve.wait_ge(out_read, 2 * KD)
                dve.sem_inc(x_ready, 1)

            experts(0)
            norm(2, permuted=True)
            gla()
            norm(3)
            experts(1)
            dve.wait_ge(rstd_done, 5)
            TT(normed, xT[:], bcm(rstd, KD), ALU.mult).then_inc(normed_done, 1)
            dve.wait_ge(normed_done, 13)
            for k in range(KD):
                last = TS(hT[:, k, :], normed[:, k, :], v("nf", k, k + 1), None, ALU.mult)
            last.then_inc(y_ready, 1)


def kernel(**inputs):
    import concourse.bacc as bacc
    from concourse.bass_utils import run_bass_kernel_spmd

    a = {k: np.asarray(x) for k, x in inputs.items()}

    def feat(x):
        x = np.moveaxis(x, -1, 0)
        return x.reshape(x.shape[0] // P, P, *x.shape[1:]).swapaxes(0, 1)

    def units_cols(w):
        n = w.shape[1]
        return w.reshape(KD, P, n // 256, 2, P).transpose(2, 1, 3, 0, 4).reshape(n // 256, P, SLOT)

    w_in = a["ab_w_in"][0]
    cols_of = {"y": 0, "x": 1024, "q": 2048, "k": 3072, "v": 4096, "z": 5120}
    ab = [units_cols(w_in[:, cols_of[n] + 512 * g:cols_of[n] + 512 * g + 512]) for g in range(HG) for n in "xqkvzy"]
    about = a["ab_w_out"][0].reshape(2 * KD, P, KD, P).transpose(2, 1, 0, 3).reshape(KD, P, SLOT)

    def moe(i):
        out = []
        for e in range(E):
            for w in (a["moe_w_gate"], a["moe_w_up"]):
                out.append(w[i, e].reshape(2, 4, P, DE).transpose(0, 2, 1, 3).reshape(2, P, SLOT))
            out.append(a["moe_w_down"][i, e].reshape(2, 2, P, D).transpose(0, 2, 1, 3).reshape(2, P, SLOT))
        return out

    gw = a["gla_w_in"][0]
    gla = []
    for h in range(GLA_H):
        gla.append(units_cols(np.concatenate([gw[:, 128 * h:128 * h + 128], gw[:, 512 + 128 * h:640 + 128 * h]], 1)))
        gla.append(units_cols(gw[:, 2048 + 256 * h:2304 + 256 * h]))
        gla.append(gw[:, 1024 + 256 * h:1280 + 256 * h].reshape(KD, P, 256).transpose(1, 0, 2).reshape(1, P, SLOT))
    parts = {"ada0": [units_cols(a["ada_w"][0])], "ab": ab, "ada1": [units_cols(a["ada_w"][1])], "about": [about],
             "moe0": moe(0), "gla": gla, "glaout": [units_cols(a["gla_w_out"][0])], "moe1": moe(1)}
    ws = np.concatenate([u for name, _ in PHASES for u in parts[name]])
    assert ws.shape == (N_UNITS, P, SLOT), ws.shape

    x = np.concatenate([a["x_prompt"][0], a["x_sample"][0]])
    xT = np.ascontiguousarray(feat(x))
    vec = np.zeros((P, NV), np.float32)

    def put(name, val):
        s, e = VC[name]
        vec[:val.shape[0], s:e] = val.reshape(val.shape[0], -1)

    put("c", feat(np.stack([a["c_ctx"], a["c"][0]])))
    put("ada_b", feat(a["ada_b"]).swapaxes(1, 2))
    put("n1", feat(a["norm1_g"]).swapaxes(1, 2))
    put("n2", feat(a["norm2_g"]).swapaxes(1, 2))
    put("nf", feat(a["final_norm_g"]))
    put("lcw", feat(a["lru_conv_w"][0]))
    put("lcb", feat(a["lru_conv_b"][0]))
    put("lba", feat(a["lru_ba"][0]))
    put("lbx", feat(a["lru_bx"][0]))
    put("lam", feat(a["lru_lam"][0]))
    put("gcw", feat(a["gdn_conv_w"][0]))
    put("gcb", feat(a["gdn_conv_b"][0]))
    put("gng", a["gdn_norm_g"][0][:, None])
    put("h0", feat(a["state_lru"][0, 0]))
    put("glb", feat(a["gla_b2"][0]).swapaxes(1, 2))
    put("glg", feat(a["gla_norm_g"][0]))
    put("rb", np.broadcast_to(a["router_b"], (P, E)))
    rows = np.zeros((2, 4, 32), np.float32)
    for g in range(HG):
        for n, name in enumerate(("gdn_a_log", "gdn_dt_bias")):
            rows[n, g, 0:8] = a[name][0][:, 4 * g:4 * g + 4].reshape(8)
    put("arow", rows[0].reshape(P, 1))
    put("trow", rows[1].reshape(P, 1))

    tail = np.zeros((D, 4, 32), np.float32)
    for n, off in enumerate((6144, 6160)):
        part = w_in[:, off:off + 16].reshape(D, 2, HG, H)
        for g in range(HG):
            tail[:, 2 * n + g, 0:8] = part[:, :, g, :].reshape(D, 8)
    tail = tail.reshape(KD, P, P).transpose(1, 0, 2)
    tail2 = np.zeros((D, 4, 32), np.float32)
    tail2[:, 0:2, 0:16] = gw[:, 3072:3104].reshape(D, 2, 16)
    tail2 = tail2.reshape(KD, P, P).transpose(1, 0, 2)
    w2 = np.zeros((2, 32, 512), np.float32)
    w2[:, 0:16] = a["gla_w2"][0]
    lruw = np.stack([a["lru_wa"][0, 0], a["lru_wx"][0, 0], a["lru_wa"][0, 1], a["lru_wx"][0, 1]])
    lruw = lruw.transpose(1, 2, 0, 3)
    s_gdn = a["state_gdn"][0, 0].reshape(2, HG, H, DK, P).transpose(1, 3, 0, 2, 4)
    s_gla = a["state_gla"][0, 0].reshape(2, GLA_H, DK, GLA_V).transpose(1, 2, 0, 3)
    arrays = {"ws": ws, "vec": vec, "const": constants(), "x_in": xT, "rw_in": feat(a["router_w"].T).swapaxes(1, 1),
              "tail_in": tail, "tail2_in": tail2, "w2_in": w2.reshape(64, 512), "lruw_in": lruw, "s_gdn": s_gdn,
              "s_gla": s_gla}
    arrays = {k: np.ascontiguousarray(x, dtype=np.float32) for k, x in arrays.items()}
    outs = {"y_out": (P, KD, T), "st_lru": (P, 8, 2), "st_gdn": (HG, 2, P, H, P), "st_gla": (GLA_H, P, 2, GLA_V)}
    nc = bacc.Bacc("TRN2", target_bir_lowering=False, num_devices=1)
    args = {k: nc.dram_tensor(k, x.shape, mybir.dt.float32, kind="ExternalInput").ap() for k, x in arrays.items()}
    st = {k: nc.dram_tensor(k, sh, mybir.dt.float32, kind="ExternalOutput").ap() for k, sh in outs.items()}
    build(nc, *args.values(), *[st[k] for k in ("y_out", "st_lru", "st_gdn", "st_gla")])
    r = run_bass_kernel_spmd(nc, [arrays], core_ids=[0]).results[0]
    y = r["y_out"].transpose(2, 1, 0).reshape(T, D)
    return (y[None, 0:T_PROMPT], y[None, T_PROMPT:],
            r["st_lru"].transpose(2, 1, 0).reshape(1, 1, 2, D),
            r["st_gdn"].transpose(1, 0, 3, 2, 4).reshape(1, 1, 2, HG * H, DK, P),
            r["st_gla"].transpose(2, 0, 1, 3).reshape(1, 1, 2, GLA_H, DK, GLA_V))
```

```python
import concourse.bass as bass
from concourse import mybir
from contextlib import ExitStack
import numpy as np

P = 128
D = 1024
KD = D // P
T_PROMPT, T_SAMPLE = 128, 256
T = T_PROMPT + T_SAMPLE
NT = T // P
SEGS = ((0, 0, T_PROMPT), (1, T_PROMPT, T_SAMPLE))
GRID_W = 64
EPS = 1e-6
CONV_W = 4
H = 4
HG = 2
DK = 128
E, DE = 16, 512
GLA_H, GLA_V = 4, 256
SUB = 32
SLOT = 2048
RING = 6
LEVELS = 7
CLAMP = 60.0
COMBINE = (2, 3, 7, 0)
LRU_GATES = tuple(range(3, 11, 2))
LRU_SCANS = tuple(b + 1 for b in LRU_GATES)
BIG = 1.0e30
SMALL = 956
CAP = P

_V = [("c", 16), ("ada_b", 96), ("n1", 16), ("n2", 16), ("nf", 8), ("lcw", 32), ("lcb", 8), ("lba", 16),
      ("lbx", 16), ("lam", 16), ("gcw", 96), ("gcb", 24), ("gng", 1), ("h0", 16), ("glb", 8), ("glg", 2),
      ("rb", 16), ("arow", 1), ("trow", 1)]
_C = [("ident", 128), ("ones", 128), ("neg_strict", 256), ("neg_incl", 256), ("pair", 256),
      ("lev", 768), ("esel", 1024), ("ehead", 32), ("sgn", 1), ("bwd", 1), ("eps", 1), ("neg1", 1), ("i16", 16),
      ("i4", 4)]


def columns(table):
    at, out = 0, {}
    for name, n in table:
        out[name] = (at, at + n)
        at += n
    return out, at


VC, NV = columns(_V)
CC, NCONST = columns(_C)


def constants():
    c = np.zeros((P, NCONST), np.float32)

    def put(name, a):
        c[:a.shape[0], CC[name][0]:CC[name][0] + a.shape[1]] = a

    j, i = np.arange(P)[:, None], np.arange(P)[None, :]
    put("ident", np.eye(P))
    put("ones", np.ones((P, P)))
    put("neg_strict", np.where(np.concatenate([j < i, j > i], 1), 0.0, -30000.0))
    put("neg_incl", np.where(np.concatenate([j <= i, j >= i], 1), 0.0, -30000.0))
    put("pair", np.concatenate([(i % 2 == 1) & (j == i - 1), (i % 2 == 0) & (j == i + 1)], 1).astype(np.float32))
    lev = np.zeros((P, 2, LEVELS - 1, 64))
    for d in range(2):
        for n in range(1, LEVELS):
            b = 2 ** n
            for col in range(64):
                first = (col // b) * 2 * b + (0 if d == 0 else b)
                lev[first:first + b, d, n - 1, col] = 1.0
    put("lev", lev.reshape(P, -1))
    es = np.zeros((8, 8, P))
    es[np.arange(8), np.arange(8)] = 1.0
    put("esel", es.reshape(8, -1))
    eh = np.zeros((P, H, 8))
    for h in range(H):
        eh[:, h, h] = eh[:, h, H + h] = 1.0
    put("ehead", eh.reshape(P, -1))
    put("sgn", np.repeat([1.0, -1.0], 64)[:, None])
    put("bwd", (np.arange(8) >= 4).astype(np.float32)[:, None])
    put("eps", np.full((P, 1), EPS))
    put("neg1", np.full((P, 1), -1.0))
    put("i16", np.tile(np.arange(16.0) - 1024.0, (P, 1)))
    put("i4", np.tile(np.arange(4.0) - 1024.0, (P, 1)))
    return c


PHASES = [("ada0", 24), ("ab", 48), ("about", 8), ("moe0", 96), ("gla", 12), ("glaout", 4),
          ("moe1", 96)]
UNIT0, _n = {}, 0
for _name, _units in PHASES:
    UNIT0[_name] = _n
    _n += _units
N_UNITS = _n


def slot_bases():
    count, out = [0] * (2 * RING), {}
    for name, units in PHASES:
        out[name] = list(count)
        ring = 2 * RING if name.startswith("moe") else RING
        for u in range(units):
            count[u % ring] += 1
    return out


BASE = slot_bases()


def build(nc, ws, vec, const, x_in, rw_in, tail_in, tail2_in, w2_in, lruw_in, s_gdn, s_gla, y_out, st_lru, st_gdn,
          st_gla):
    F32 = mybir.dt.float32
    ALU = mybir.AluOpType
    ACT = mybir.ActivationFunctionType
    AX = mybir.AxisListType

    ctx = ExitStack()
    with ctx:
        def sb(name, shape):
            return ctx.enter_context(nc.sbuf_tensor(name, shape, F32))

        def sem(name):
            return ctx.enter_context(nc.semaphore(name))

        bank = [ctx.enter_context(nc.psum_tensor(f"bank{i}", [P, 512], F32)) for i in range(8)]

        xT = sb("xT", [P, KD, T])
        hT = sb("hT", [P, KD, T])
        mix = sb("mix", [P, 2 * KD, T])
        ring = sb("ring", [P, RING, SLOT])
        vecs = sb("vecs", [P, NV])
        cst = sb("cst", [P, NCONST])
        rw = sb("rw", [P, KD, E])
        small = sb("small", [P, SMALL])
        WORK = 24190
        flag = ctx.enter_context(nc.sbuf_tensor("flag", [P, 4], mybir.dt.int32))
        work = sb("work", [P, WORK])

        def v(name, a=0, b=None):
            s, e = VC[name]
            return vecs[:, s + a:(e if b is None else s + b)]

        def cc(name, a=0, b=None, rows=P):
            s, e = CC[name]
            return cst[0:rows, s + a:(e if b is None else s + b)]

        ident, ones = cc("ident"), cc("ones")

        def carve(tile, start=0):
            at = [start]

            def take(n, *shape, rows=P):
                a = tile[0:rows, at[0]:at[0] + n]
                at[0] += n
                if len(shape) == 2:
                    return a.rearrange("p (a b) -> p a b", b=shape[1])
                if len(shape) == 3:
                    return a.rearrange("p (a b c) -> p a b c", b=shape[1], c=shape[2])
                if len(shape) == 4:
                    return a.rearrange("p (a b c d) -> p a b c d", b=shape[1], c=shape[2], d=shape[3])
                return a
            take.at = at
            return take

        tk = carve(small)
        cs = tk(16, 8, 2)
        mod = [tk(96, 48, 2) for _ in range(2)]
        gain = tk(16, 8, 2)
        sp = tk(16, 8, 2)
        nsp4 = tk(16, 8, 2)
        psp4 = tk(16, 8, 2)
        hba = tk(16, 8, 2)
        hbx = tk(16, 8, 2)
        z1, z2, z3, z4 = tk(16), tk(16), tk(16), tk(16)
        gp = tk(32, 4, 4, 2)
        gpx = tk(88)
        lru_st = tk(16, 8, 2)
        lnrow = tk(2)
        rstd = tk(T)
        assert tk.at[0] <= SMALL, tk.at

        slots = [ring[:, s, :] for s in range(RING)] + [work[:, s * SLOT:(s + 1) * SLOT] for s in range(RING)]
        normed, squares = mix[:, 0:KD, :], hT[:]

        tk = carve(work)
        qT, kT = tk(H * T, H, T), tk(H * T, H, T)
        kTok, vTok = tk(H * T, NT, H, P), tk(H * T, NT, H, P)
        oT = tk(H * T, H, T)
        S = tk(2 * H * P, 2, H, P)
        gcR, lbR = tk(HG * T, HG, T, rows=8), tk(HG * T, HG, T, rows=8)
        glR = tk(HG * NT, HG, NT, rows=8)
        mrow1 = work[32:34, tk.at[0]:tk.at[0] + 1024]
        negC, rowA, rowQ, rowK, lbS = (tk(T, rows=8) for _ in range(5))
        cols = tk(4 * NT * 8, 4, NT, 8)
        ecols = tk(4 * NT * 8, 4, NT, 8)
        egl = tk(8 * NT, 8, NT)
        shared = tk.at[0]
        xc = tk(4 * T, 4, T)
        pad = [tk(390) for _ in range(2)]
        acc = tk(387)
        cv = [tk(T) for _ in range(2)]
        vT = [tk(T) for _ in range(2)]
        sqb = [tk(T) for _ in range(2)]
        gy = [tk(T) for _ in range(2)]
        rt, it_, aa, th = (tk(2 * T, 2, T) for _ in range(4))
        hf, hb = tk(T), tk(T)
        lruw = tk(2 * 512, 2, 4, P)
        assert tk.at[0] <= WORK, tk.at
        tk.at[0] = shared
        Gs, Qs = tk(NT * H * P, NT, H, P), tk(NT * H * P, NT, H, P)
        quad = []
        for _ in range(2):
            q = {n: tk(H * P, H, P) for n in ("N", "QK", "qe", "L", "U", "Tm", "kdec", "vb")}
            q["Ys"] = tk(H * 64, H, 64)
            quad.append(q)
        assert tk.at[0] <= WORK, tk.at
        mrow = [work[0:2, n * 1536:(n + 1) * 1536] for n in range(2)]
        tk.at[0] = shared
        tw = tk(KD * P, KD, P)
        tu, tv_, tabs = tk(T), tk(T), tk(T)
        psR = tk(HG * T, HG, T, rows=8)
        pt = tk(HG * T, HG, T, rows=8)
        gR = tk(HG * T, HG, T, rows=8)
        arow = tk(1)
        assert tk.at[0] <= WORK, tk.at

        tk = carve(work, RING * SLOT)
        rt_s, rt_sel, rt_m, rt_a, rt_b, rt_o1, rt_o2, gates_ = (tk(48, 3, 16) for _ in range(8))
        rt_mx, rt_mn = tk(24, 12, 2), tk(24, 12, 2)
        rt_t, rt_u, rt_g, rt_h = (tk(12) for _ in range(4))
        rt_k = tk(3)
        rank = tk(3 * (E + 1), NT, E + 1)
        upper, places = tk(P), tk(CAP)
        own = tk.at[0]
        sg, hid, hidT = ([tk(DE) for _ in range(2)] for _ in range(3))
        assert tk.at[0] <= WORK, tk.at
        tk.at[0] = own
        sel, gsel, selT = tk(NT * CAP, NT, CAP), tk(NT * CAP, NT, CAP), tk(T)
        xg = tk(KD * CAP, KD, CAP)
        sg1, hid1, hidT1, yo = tk(DE), tk(DE), tk(DE), tk(D)
        assert tk.at[0] <= WORK, tk.at
        htok = mix[:, KD:2 * KD, :].rearrange("p a b -> p (a b)").rearrange("p (t d) -> p t d", t=NT)
        accf = mix[:, 0:KD, :].rearrange("p a b -> p (a b)").rearrange("p (t d) -> p t d", t=NT)

        tk = carve(work)
        gabs, gmin = tk(8 * T, 8, T), tk(8 * T, 8, T)
        gch = tk(2 * T, 2, T)
        gq, gk = tk(T), tk(T)
        gv = tk(NT * GLA_V, NT, GLA_V)
        go = tk(2 * T, 2, T)
        gsq = tk(2 * T, 2, T)
        gS, gS2 = tk(2 * GLA_V, 2, GLA_V), tk(2 * GLA_V, 2, GLA_V)
        incl = tk(2 * P, 2, P)
        glp = []
        for _ in range(2 * NT):
            glp.append({"ex": tk(512, 4, P), "qx": tk(P, 4, SUB), "qe": tk(P), "kd": tk(P), "kdT": tk(P), "AT": tk(P),
                        "egl": tk(1)})
        tw2, w2sb, lrT = tk(KD * P, KD, P), tk(512, rows=64), tk(T)
        grstd = tk(T)
        assert tk.at[0] <= WORK, tk.at

        const_loaded = sem("const_loaded")
        x_loaded = sem("x_loaded")
        group_start = sem("group_start")
        tail_loaded = sem("tail_loaded")
        slots_started = sem("slots_started")
        prep = sem("prep")
        prep_exp = sem("prep_exp")
        mod_read = sem("mod_read")
        mod_turned = sem("mod_turned")
        mod_rows = sem("mod_rows")
        lru_prep = sem("lru_prep")
        sq_done = sem("sq_done")
        ms_done = sem("ms_done")
        ln_done = sem("ln_done")
        rstd_done = sem("rstd_done")
        normed_done = sem("normed_done")
        h_ready = sem("h_ready")
        x_ready = sem("x_ready")
        tail_done = sem("tail_done")
        tail_act = sem("tail_act")
        rows_ready = sem("rows_ready")
        proj_done = sem("proj_done")
        proj_read = sem("proj_read")
        conv_step = sem("conv_step")
        conv_done = sem("conv_done")
        silu_done = sem("silu_done")
        gates_done = sem("gates_done")
        lru_tanh = sem("lru_tanh")
        lru_mid = sem("lru_mid")
        lru_sqrt = sem("lru_sqrt")
        lru_u = sem("lru_u")
        lru_done = sem("lru_done")
        lru_b = sem("lru_b")
        sq_pool = sem("sq_pool")
        ss_done = sem("ss_done")
        lnr_done = sem("lnr_done")
        rows_dve = sem("rows_dve")
        tr_done = sem("tr_done")
        tr_read = sem("tr_read")
        y_mixed = sem("y_mixed")
        half_act = sem("half_act")
        half_dve = sem("half_dve")
        half_pool = sem("half_pool")
        lruw0_loaded = sem("lruw0_loaded")
        lruw1_loaded = sem("lruw1_loaded")
        gram_done = sem("gram_done")
        gram_read = sem("gram_read")
        cols_done = sem("cols_done")
        cols_copied = sem("cols_copied")
        cols_exp = sem("cols_exp")
        bc_done = sem("bc_done")
        arg_done = sem("arg_done")
        exp_done = sem("exp_done")
        n_done = sem("n_done")
        n_tr = sem("n_tr")
        l_done = sem("l_done")
        u_init = sem("u_init")
        u_tr = sem("u_tr")
        t_done = sem("t_done")
        quad_pool = sem("quad_pool")
        y_done = sem("y_done")
        y_masked = sem("y_masked")
        du_done = sem("du_done")
        u_done = sem("u_done")
        ks_done = sem("ks_done")
        r_done = sem("r_done")
        vnew_done = sem("vnew_done")
        v_read = sem("v_read")
        o_done = sem("o_done")
        o_read = sem("o_read")
        ds_done = sem("ds_done")
        s_done = sem("s_done")
        state_loaded = sem("state_loaded")
        state_saved = sem("state_saved")
        osq = sem("osq")
        oms = sem("oms")
        orstd = sem("orstd")
        omix = sem("omix")
        group_done = sem("group_done")
        out_done = sem("out_done")
        out_read = sem("out_read")
        router_done = sem("router_done")
        router_sig = sem("router_sig")
        gate_done = sem("gate_done")
        up_done = sem("up_done")
        sg_done = sem("sg_done")
        hid_done = sem("hid_done")
        htr_done = sem("htr_done")
        hidT_done = sem("hidT_done")
        down_done = sem("down_done")
        acc_done = sem("acc_done")
        acc_tr = sem("acc_tr")
        acc_added = sem("acc_added")
        tail2_loaded = sem("tail2_loaded")
        glr_done = sem("glr_done")
        glr_copied = sem("glr_copied")
        gpre_done = sem("gpre_done")
        gpre_act = sem("gpre_act")
        gpre_dve = sem("gpre_dve")
        gexp = sem("gexp")
        gproj_done = sem("gproj_done")
        gproj_read = sem("gproj_read")
        ghead = sem("ghead")
        gargs = sem("gargs")
        gexps = sem("gexps")
        gmul = sem("gmul")
        gA_done = sem("gA_done")
        gA_read = sem("gA_read")
        gkd_tr = sem("gkd_tr")
        gkd_done = sem("gkd_done")
        go_done = sem("go_done")
        go_read = sem("go_read")
        gds_done = sem("gds_done")
        gs_done = sem("gs_done")
        gs_saved = sem("gs_saved")
        gs_loaded = sem("gs_loaded")
        gosq = sem("gosq")
        goms = sem("goms")
        gorstd = sem("gorstd")
        gomix = sem("gomix")
        gfin = sem("gfin")
        y_ready = sem("y_ready")
        routed = sem("routed")
        sel_done = sem("sel_done")
        gathered = sem("gathered")
        gather_read = sem("gather_read")
        selT_read = sem("selT_read")
        y_read = sem("y_read")
        comb_done = sem("comb_done")
        comb_read = sem("comb_read")
        stored = sem("stored")
        loaded = [sem(f"slot{i}_loaded") for i in range(2 * RING)]
        free = [sem(f"slot{i}_free") for i in range(2 * RING)]
        block = ctx.enter_context(nc.Block())

        def step_counter(eng, signal):
            n = [0]

            def link(ins, base=0):
                n[0] += 1
                ins.then_inc(signal, 1)
                eng.wait_ge(signal, base + n[0])
            link.n = n
            return link

        def bc3(a, n):
            return a.unsqueeze(2).to_broadcast([a.shape[0], a.shape[1], n])

        def bcm(a, n):
            return a.unsqueeze(1).to_broadcast([a.shape[0], n, a.shape[1]])

        @block.sync
        def _(sp):
            sp.dma_start(vecs[:], vec).then_inc(const_loaded, 16)
            sp.dma_start(cst[:], const).then_inc(const_loaded, 16)
            sp.dma_start(rw[:], rw_in).then_inc(const_loaded, 16)
            sp.dma_start(xT[:], x_in).then_inc(x_loaded, 16)
            sp.dma_start(tw, tail_in).then_inc(tail_loaded, 16)
            sp.wait_ge(slots_started, 1)

            def stream(phase, rounds, n_slots, step):
                if rounds > 1:
                    with sp.Fori(0, rounds) as r:
                        for i in range(n_slots):
                            sp.wait_ge(free[i], r + (BASE[phase][i] + 1))
                            sp.dma_start(slots[i], ws[r * step + (UNIT0[phase] + i)]).then_inc(loaded[i], 16)
                else:
                    for i in range(n_slots):
                        sp.wait_ge(free[i % RING], BASE[phase][i % RING] + 1 + i // RING)
                        sp.dma_start(slots[i % RING], ws[UNIT0[phase] + i]).then_inc(loaded[i % RING], 16)

            stream("ada0", 4, RING, RING)
            with sp.Fori(0, HG) as g:
                def group_unit(i):
                    n = i % RING
                    sp.wait_ge(free[n], g * 4 + (BASE["ab"][n] + 1 + i // RING))
                    sp.dma_start(slots[n], ws[g * 24 + (UNIT0["ab"] + i)]).then_inc(loaded[n], 16)

                for i in range(18):
                    group_unit(i)
                for d in range(2):
                    sp.wait_ge(s_done, g * 4 + (d + 1))
                    sp.dma_start(st_gdn[g, d], S[:, d]).then_inc(state_saved, 16)
                sp.wait_ge(state_saved, g * 32 + 32)
                sp.dma_start(S, s_gdn[g]).then_inc(state_loaded, 16)
                for i in range(18, 24):
                    group_unit(i)
            stream("about", 1, 8, 0)

            def stream_experts(layer):
                phase = f"moe{layer}"
                for i in range(2 * RING):
                    if i == RING:
                        sp.wait_ge(x_ready, 2 * layer + 1)
                    sp.wait_ge(free[i], BASE[phase][i] + 1)
                    sp.dma_start(slots[i], ws[UNIT0[phase] + i]).then_inc(loaded[i], 16)
                with sp.Fori(1, E // 2) as r:
                    for i in range(2 * RING):
                        sp.wait_ge(free[i], r + (BASE[phase][i] + 1))
                        sp.dma_start(slots[i], ws[r * (2 * RING) + (UNIT0[phase] + i)]).then_inc(loaded[i], 16)

            sp.dma_start(st_lru, lru_st).then_inc(stored, 16)
            stream_experts(0)
            sp.wait_ge(x_ready, 2)
            sp.dma_start(tw2, tail2_in).then_inc(tail2_loaded, 16)
            sp.dma_start(w2sb, w2_in).then_inc(tail2_loaded, 16)
            sp.dma_start(gS2, s_gla[0]).then_inc(gs_loaded, 16)
            with sp.Fori(0, 2) as r:
                for i in range(RING):
                    sp.wait_ge(free[i], r + (BASE["gla"][i] + 1))
                    sp.dma_start(slots[i], ws[r * RING + (UNIT0["gla"] + i)]).then_inc(loaded[i], 16)
                for hh in range(2):
                    sp.wait_ge(gs_done, r * 8 + (4 * hh + 2))
                    sp.dma_start(st_gla[r * 2 + hh], gS).then_inc(gs_saved, 16)
            stream("glaout", 1, 4, 0)
            sp.wait_ge(gs_loaded, 16 * (GLA_H + 1))
            sp.wait_ge(gs_saved, 16 * (GLA_H + 1))
            stream_experts(1)
            for k in range(0, KD, 2):
                sp.wait_ge(y_ready, k // 2 + 1)
                sp.dma_start(y_out[:, k:k + 2, :], hT[:, k:k + 2, :]).then_inc(stored, 16)
            sp.wait_ge(stored, 16 + 16 * (KD // 2))
            sp.wait_ge(state_saved, 64)

        @block.tensor
        def _(pe):
            mm, tr = pe.matmul, pe.transpose
            for i in range(2 * RING):
                pe.sem_inc(free[i], 1)
            pe.sem_inc(slots_started, 1)
            pe.wait_ge(const_loaded, 48)
            pe.wait_ge(prep_exp, 1)

            def modulate(i, out, ks):
                w = slots[i].rearrange("p (m k c) -> p m k c", m=2, k=KD)
                for k in ks:
                    last = mm(out, cs[:, k, :], w[:, :, k, :], start=(k == 0), stop=(k == KD - 1))
                return last

            def turn_rows(out, rows, eye, n):
                for m in range(n):
                    last = mm(out[:, 2 * m:2 * m + 2], rows[:, m * P:(m + 1) * P], eye, start=True, stop=True)
                last.then_inc(mod_turned, 1)

            with pe.Fori(0, 2) as r:
                def turn(half):
                    pe.wait_ge(mod_rows, r * 2 + (half + 1))
                    pe.wait_ge(mod_read, r * 2 + (half + 1))
                    turn_rows(bank[7], mrow[half], ident[0:2, 0:2], 2 * RING)

                for half in range(2):
                    for i in range(RING):
                        pe.wait_ge(loaded[i], r * 32 + 16 * (BASE["ada0"][i] + 1 + half))
                        out = bank[3 * half + i // 2][0:2, (i % 2) * 256:(i % 2) * 256 + 256]
                        modulate(i, out, range(KD)).then_inc(free[i], 1)
                        if half == 1 and i == 2:
                            turn(0)
                turn(1)

            def mean_square(n, slot_free=None):
                for k in range(KD):
                    pe.wait_ge(sq_done, KD * n + k + 1)
                    last = mm(bank[6][:, 0:T], ones, squares[:, k, :], start=(k == 0), stop=(k == KD - 1))
                    if k == 0 and slot_free is not None:
                        last.then_inc(slot_free, 1)
                last.then_inc(ms_done, 1)

            mean_square(0)
            pe.wait_ge(h_ready, 1)
            pe.wait_ge(tail_loaded, 16)
            for k in range(KD):
                last = mm(bank[7][:, 0:T], tw[:, k, :], hT[:, k, :], start=(k == 0), stop=(k == KD - 1))
            last.then_inc(tail_done, 1)

            with pe.Fori(0, HG) as g:
                def gates(i):
                    pe.wait_ge(conv_done, g * 16 + (i + 1))
                    pe.wait_ge((lruw0_loaded, lruw1_loaded)[i % 2], g * 32 + 16 * (i // 2 + 1))
                    if i:
                        pe.wait_ge(lru_tanh, g * 4 + i)
                    for n in range(4):
                        last = mm(bank[2 + n][:, 0:T], lruw[:, i % 2, n, :], xc[:, i, :], start=True, stop=True)
                    last.then_inc(gates_done, 1)

                def squares_sum(j):
                    pe.wait_ge(sq_pool, g * 8 + (j + 1))
                    if j == 4:
                        pe.wait_ge(lnr_done, g * 2 + 1)
                    if j == 0:
                        pe.wait_ge(rows_ready, 1)
                    mm(bank[7][0:8, 0:T], cc("ehead", 8 * (j % 4), 8 * (j % 4) + 8), sqb[j % 2],
                       start=(j % 4 == 0), stop=(j % 4 == 3)).then_inc(ss_done, 1)

                def to_tokens(j):
                    pe.wait_ge(silu_done, g * 12 + (4 + j + 1))
                    if j:
                        pe.wait_ge(tr_read, g * 8 + j)
                    src = kT[:, j, :] if j < 4 else vT[j % 2]
                    for t in range(NT):
                        last = tr(bank[6][:, t * P:(t + 1) * P], src[:, t * P:(t + 1) * P], ident)
                    last.then_inc(tr_done, 1)

                for b in range(24):
                    n = (b // 2) % RING
                    if b % 2 == 0:
                        pe.wait_ge(loaded[n], g * 64 + 16 * (BASE["ab"][n] + 1 + b // (2 * RING)))
                    pe.wait_ge(proj_read, g * 24 + (b + 1))
                    w = slots[n].rearrange("p (m k c) -> p m k c", m=2, k=KD)
                    for k in range(KD):
                        last = mm(bank[b % 2][:, 0:T], w[:, b % 2, k, :], hT[:, k, :], start=(k == 0),
                                  stop=(k == KD - 1))
                        if k == 0 and b % 2 == 0 and b:
                            last.then_inc(free[(b // 2 - 1) % RING], 1)
                    last.then_inc(proj_done, 1)
                    if b + 1 in LRU_GATES:
                        gates(LRU_GATES.index(b + 1))
                    if 6 <= b < 14:
                        squares_sum(b - 6)
                    if 10 <= b < 18:
                        to_tokens(b - 10)

                pe.wait_ge(half_act, g + 1)
                pe.wait_ge(half_dve, g + 1)
                for c in range(NT):
                    for n, x in enumerate((kT, qT)):
                        for h in range(H):
                            last = mm(bank[2 * c + n][:, h * P:(h + 1) * P], kT[:, h, c * P:(c + 1) * P],
                                      x[:, h, c * P:(c + 1) * P], start=True, stop=True)
                            if c + n + h == 0:
                                last.then_inc(free[RING - 1], 1)
                        last.then_inc(gram_done, 1)
                for n, row in enumerate((negC, lbS, rowA, rowK)):
                    for c in range(NT):
                        src = row[:, c * P:(c + 1) * P]
                        last = tr(bank[6][:, (n * NT + c) * 8:(n * NT + c) * 8 + 8], src, ident[0:8, 0:8])
                for r in range(8):
                    last = mm(bank[7][:, r * NT:(r + 1) * NT], cc("esel", r * P, (r + 1) * P, rows=8),
                              glR[:, g, :], start=True, stop=True)
                last.then_inc(cols_done, 1)
                pe.wait_ge(gram_read, g * 6 + 6)
                pe.wait_ge(cols_exp, g + 1)

                def modulate_next(stp, lv, half):
                    if 1 <= lv <= 4:
                        i = 12 + 4 * stp + lv - 1
                        n = i % RING
                        if half == 0:
                            pe.wait_ge(loaded[n], g * 64 + 16 * (BASE["ab"][n] + 1 + i // RING))
                        out = bank[6 + (lv - 1) // 2][0:2, (lv - 1) % 2 * 256:(lv - 1) % 2 * 256 + 256]
                        last = modulate(n, out, range(4 * half, 4 * half + 4))
                        if half == 1:
                            last.then_inc(free[n], 1)
                    if lv == 6 and half == 0:
                        pe.wait_ge(mod_rows, g * 3 + (4 + stp + 1))
                        turn_rows(bank[6], mrow1, ident[32:34, 32:34], 8)

                for stp in range(NT):
                    chunk = (stp, (0, 2, 1)[stp])
                    q0 = stp * 2
                    both = [(x, chunk[x], quad[x], bank[3 * x:3 * x + 3]) for x in range(2)]
                    for x, c, q, bk in both:
                        if stp:
                            pe.wait_ge(o_read, g * 6 + (q0 - 2 + x + 1))
                            pe.wait_ge(s_done, g * 4 + (2 * (stp - 1) + x + 1))
                        for n, row in enumerate((rowA, rowQ)):
                            for h in range(H):
                                last = mm(bk[n][:, h * P:(h + 1) * P],
                                          cc("esel", (4 * x + h) * P, (4 * x + h + 1) * P, rows=8),
                                          row[:, c * P:(c + 1) * P], start=True, stop=True)
                        last.then_inc(bc_done, 1)
                    for x, c, q, bk in both:
                        pe.wait_ge(n_done, g * 6 + (q0 + x + 1))
                        for h in range(H):
                            last = tr(bk[2][:, h * P:(h + 1) * P], q["N"][:, h, :], ident)
                        last.then_inc(n_tr, 1)
                    for lv in range(LEVELS):
                        for x, c, q, bk in both:
                            if lv:
                                b = 2 ** lv
                                pe.wait_ge(u_done, g * 42 + (q0 * 7 + 2 * (lv - 1) + x + 1))
                                if lv == 1:
                                    pe.wait_ge(l_done, g * 6 + (q0 + x + 1))
                                uv = q["U"].rearrange("p h (q t b) -> p h q t b", t=2, b=b)[:, :, :, 1 - x, :]
                                for h in range(H):
                                    last = mm(bk[1][:, h * 64:(h + 1) * 64].rearrange("p (q b) -> p q b", b=b),
                                              q["L"][:, h, :], uv[:, h], start=True, stop=True)
                                last.then_inc(y_done, 1)
                            else:
                                pe.wait_ge(u_done, g * 42 + (q0 * 7 + x + 1))
                        modulate_next(stp, lv, 0)
                        for x, c, q, bk in both:
                            if lv == 0:
                                for h in range(H):
                                    last = tr(bk[0][:, h * P:(h + 1) * P], q["U"][:, h, :], ident)
                                last.then_inc(u_tr, 1)
                                continue
                            b = 2 ** lv
                            pe.wait_ge(t_done, g * 36 + (q0 * 6 + 2 * (lv - 1) + x + 1))
                            pe.wait_ge(y_masked, g * 36 + (q0 * 6 + 2 * (lv - 1) + x + 1))
                            for h in range(H):
                                last = mm(bk[2][:, h * 64:(h + 1) * 64], q["Tm"][:, h, :], q["Ys"][:, h, :],
                                          start=True, stop=True)
                            last.then_inc(du_done, 1)
                        modulate_next(stp, lv, 1)
                        if 1 <= lv < LEVELS - 1:
                            for x, c, q, bk in both:
                                pe.wait_ge(u_done, g * 42 + (q0 * 7 + 2 * lv + x + 1))
                                for h in range(H):
                                    last = tr(bk[0][:, h * P:(h + 1) * P], q["U"][:, h, :], ident)
                                last.then_inc(u_tr, 1)
                    pe.wait_ge(mod_read, g * 3 + (5 + stp + 1))
                    for x, c, q, bk in both:
                        if stp:
                            if stp == 1 and x == 0:
                                pe.wait_ge(state_loaded, g * 16 + 16)
                            for h in range(H):
                                last = mm(bank[6 + x][:, h * P:(h + 1) * P], kT[:, h, c * P:(c + 1) * P],
                                          S[:, x, h, :], start=True, stop=True)
                            last.then_inc(ks_done, 1)
                    for x, c, q, bk in both:
                        pe.wait_ge(u_done, g * 42 + (q0 * 7 + 12 + x + 1))
                        pe.wait_ge(quad_pool, g * 6 + (q0 + x + 1))
                        if stp:
                            pe.wait_ge(r_done, g * 4 + (q0 - 2 + x + 1))
                        R = q["Tm"] if stp else q["vb"]
                        for h in range(H):
                            last = mm(bk[1][:, h * P:(h + 1) * P], q["U"][:, h, :], R[:, h, :], start=True,
                                      stop=True)
                        last.then_inc(vnew_done, 1)
                    for x, c, q, bk in both:
                        pe.wait_ge(v_read, g * 6 + (q0 + x + 1))
                        for h in range(H):
                            dst = bk[2][:, h * P:(h + 1) * P]
                            if stp:
                                mm(dst, S[:, x, h, :], q["qe"][:, h, :], start=True, stop=False)
                            last = mm(dst, q["L"][:, h, :], q["QK"][:, h, :], start=not stp, stop=True)
                        last.then_inc(o_done, 1)
                        if stp < 2:
                            for h in range(H):
                                last = mm(bk[0][:, h * P:(h + 1) * P], q["kdec"][:, h, :], q["L"][:, h, :],
                                          start=True, stop=True)
                            last.then_inc(ds_done, 1)
                pe.wait_ge(osq, g + 1)
                for h in range(H):
                    last = mm(bank[h][:, 0:T], ones, kT[:, h, :], start=True, stop=True)
                last.then_inc(oms, 1)
                pe.wait_ge(group_done, g + 1)

            pe.wait_ge(omix, HG)
            for m in range(KD):
                n = m % RING
                pe.wait_ge(loaded[n], 16 * (BASE["about"][n] + 1 + m // RING))
                if m >= 2:
                    pe.wait_ge(out_read, m - 1)
                w = slots[n].rearrange("p (k c) -> p k c", k=2 * KD)
                for k in range(2 * KD):
                    last = mm(bank[m % 2][:, 0:T], w[:, k, :], mix[:, k, :], start=(k == 0), stop=(k == 2 * KD - 1))
                    if k == 0 and m:
                        last.then_inc(free[(m - 1) % RING], 1)
                last.then_inc(out_done, 1)
            mean_square(1, free[(KD - 1) % RING])

            def experts(layer):
                pe.wait_ge(h_ready, 2 * layer + 2)
                for t in range(NT):
                    for k in range(KD):
                        last = mm(bank[7][:, t * E:(t + 1) * E], hT[:, k, t * P:(t + 1) * P], rw[:, k, :],
                                  start=(k == 0), stop=(k == KD - 1))
                last.then_inc(router_done, 1)
                for t in range(NT):
                    for half in range(2):
                        for j in range(4):
                            last = tr(bank[2 * t + half][:, j * P:(j + 1) * P],
                                      hT[:, 4 * half + j, t * P:(t + 1) * P], ident)
                last.then_inc(gathered, 1)
                pe.wait_ge(routed, 2 * layer + 1)
                for t in range(NT):
                    for u in range(t + 1):
                        mm(bank[7][:, 64 + t * E:64 + (t + 1) * E], upper if u == t else ones, rt_m[:, u, :],
                           start=(u == 0), stop=(u == t))
                for t in range(NT):
                    last = mm(bank[7][:, 64 + NT * E:64 + (NT + 1) * E], ones, rt_m[:, t, :], start=(t == 0),
                              stop=(t == NT - 1))
                last.then_inc(router_done, 1)
                pe.wait_ge(gather_read, 35 * layer + 1)
                pe.wait_ge(routed, 2 * layer + 2)
                full = pe.value_load(flag[0:1, 0:1])
                with pe.If(full < 1):
                    picked(layer)
                with pe.If(full >= 1):
                    dense(layer)

            def picked(layer):
                phase, o = f"moe{layer}", 48 * layer

                def gather(half, nxt):
                    for m in range(4):
                        for t in range(NT):
                            f = 4 * half + m
                            last = mm(bank[1 - half][:, m * CAP:(m + 1) * CAP], htok[:, t, f * P:(f + 1) * P],
                                      sel[:, t, :], start=(t == 0), stop=(t == NT - 1))
                            if nxt is not None and half + m + t == 0:
                                last.then_inc(nxt, 1)
                    last.then_inc(gathered, 1)

                pe.wait_ge(sel_done, 33 * layer + 1)
                gather(0, None)
                gather(1, None)
                with pe.Fori(0, E // 2) as ep:
                    for n in range(2):
                        so = n * RING
                        pe.wait_ge(gather_read, ep * 4 + (35 * layer + 1 + 2 * n + 2))
                        for kind, done in enumerate((gate_done, up_done)):
                            for k in range(KD):
                                i = so + 2 * kind + k // 4
                                if k % 4 == 0:
                                    pe.wait_ge(loaded[i], ep * 16 + 16 * (BASE[phase][i] + 1))
                                w = slots[i].rearrange("p (k f) -> p k f", k=4)
                                last = mm(bank[2 + kind][:], xg[:, k, :], w[:, k % 4, :], start=(k == 0),
                                          stop=(k == KD - 1))
                                if k == 3:
                                    last.then_inc(free[i], 1)
                                if kind == 1 and k == 0:
                                    last.then_inc(free[so + 1], 1)
                            last.then_inc(done, 1)
                        pe.wait_ge(sel_done, ep * 4 + (33 * layer + 2 * n + 2))
                        gather(0, free[so + 3])
                        pe.wait_ge(hid_done, ep * 2 + (o + n + 1))
                        for j in range(DE // P):
                            last = tr(bank[4][:, j * P:(j + 1) * P], hid1[:, j * P:(j + 1) * P], ident)
                        last.then_inc(htr_done, 1)
                        pe.wait_ge(comb_read, ep * 16 + (128 * layer + 8 * n + 1))
                        gather(1, None)
                        pe.wait_ge(sel_done, ep * 4 + (33 * layer + 2 * n + 3))
                        for t in range(NT):
                            last = tr(bank[7][:, t * P:(t + 1) * P], gsel[:, t, :], ident)
                        last.then_inc(down_done, 1)
                        for i in (4, 5):
                            pe.wait_ge(loaded[so + i], ep * 16 + 16 * (BASE[phase][so + i] + 1))
                        pe.wait_ge(hidT_done, ep * 2 + (o + n + 1))
                        for half in range(2):
                            for j in range(DE // P):
                                w = slots[so + 4 + j // 2].rearrange("p (k d) -> p k d", k=2)
                                last = mm(bank[5 + half][:], hidT1[:, j * P:(j + 1) * P],
                                          w[:, j % 2, half * 512:(half + 1) * 512], start=(j == 0), stop=(j == 3))
                                if half == 1 and j == 1:
                                    last.then_inc(free[so + 4], 1)
                            last.then_inc(down_done, 1)
                        pe.wait_ge(selT_read, ep * 2 + (16 * layer + n + 1))
                        for m in range(KD):
                            if m % 4 == 0:
                                pe.wait_ge(y_read, ep * 4 + (32 * layer + 2 * n + m // 4 + 1))
                            if m == 4:
                                pe.sem_inc(free[so + 5], 1)
                            if m >= 4:
                                pe.wait_ge(comb_read, ep * 16 + (128 * layer + 8 * n + m - 2))
                            mm(bank[COMBINE[m % 4]][:, 0:T], yo[:, m * P:(m + 1) * P], selT, start=True, stop=True)\
                                .then_inc(comb_done, 1)
                        pe.wait_ge(comb_read, ep * 16 + (128 * layer + 8 * n + 7))
                pe.wait_ge(comb_read, 128 * (layer + 1) + 1)
                for signal in (gate_done, up_done, htr_done):
                    pe.sem_inc(signal, 32)
                pe.sem_inc(acc_tr, 6)

            def dense(layer):
                phase, o = f"moe{layer}", 48 * layer
                with pe.Fori(0, E // 2) as ep:
                    def turn(n):
                        pe.wait_ge(hid_done, ep * 6 + (o + n + 1))
                        for j in range(DE // P):
                            last = tr(bank[4][:, j * P:(j + 1) * P], hid[n % 2][:, j * P:(j + 1) * P], ident)
                        last.then_inc(htr_done, 1)

                    def down(n):
                        so, t = n // 3 * RING, n % 3
                        if t == 0:
                            for i in (4, 5):
                                pe.wait_ge(loaded[so + i], ep * 16 + 16 * (BASE[phase][so + i] + 1))
                        pe.wait_ge(hidT_done, ep * 6 + (o + n + 1))
                        pe.wait_ge(acc_done, ep * 6 + (49 * layer + n + 1))
                        for half in range(2):
                            for j in range(DE // P):
                                w = slots[so + 4 + j // 2].rearrange("p (k d) -> p k d", k=2)
                                last = mm(bank[5 + half][:], hidT[n % 2][:, j * P:(j + 1) * P],
                                          w[:, j % 2, half * 512:(half + 1) * 512], start=(j == 0), stop=(j == 3))
                                if half == 1 and j == 1 and t == 2:
                                    last.then_inc(free[so + 4], 1)
                        last.then_inc(down_done, 1)

                    for n in range(6):
                        so, t = n // 3 * RING, n % 3
                        for kind, (bk, done) in enumerate(((n % 2, gate_done), (2 + n % 2, up_done))):
                            for k in range(KD):
                                i = so + 2 * kind + k // 4
                                if t == 0 and k % 4 == 0:
                                    pe.wait_ge(loaded[i], ep * 16 + 16 * (BASE[phase][i] + 1))
                                w = slots[i].rearrange("p (k f) -> p k f", k=4)
                                last = mm(bank[bk][:], hT[:, k, t * P:(t + 1) * P], w[:, k % 4, :],
                                          start=(k == 0), stop=(k == KD - 1))
                                if t == 2 and k == 3:
                                    last.then_inc(free[i], 1)
                                if t == 2 and kind == 1 and k == 0:
                                    last.then_inc(free[so + 1], 1)
                            last.then_inc(done, 1)
                            if n and kind == 0:
                                turn(n - 1)
                            if n and kind == 1:
                                down(n - 1)
                    turn(5)
                    down(5)
                pe.wait_ge(acc_done, 49 * layer + 49)
                for n in range(2 * NT):
                    if n >= 2:
                        pe.wait_ge(acc_added, 6 * layer + n - 1)
                    for j in range(4):
                        m = n % 2 * 4 + j
                        last = tr(bank[n % 2][:, j * P:(j + 1) * P], accf[:, n // 2, m * P:(m + 1) * P], ident)
                    last.then_inc(acc_tr, 1)
                pe.wait_ge(acc_added, 6 * layer + 6)
                pe.sem_inc(gathered, 34)
                pe.sem_inc(comb_done, 128)

            def gla():
                pe.wait_ge(h_ready, 3)
                pe.wait_ge(tail2_loaded, 32)
                for k in range(KD):
                    last = mm(bank[7][:, 0:T], tw2[:, k, :], hT[:, k, :], start=(k == 0), stop=(k == KD - 1))
                last.then_inc(glr_done, 1)
                pe.wait_ge(glr_copied, 1)
                for n in range(8):
                    if n >= 4:
                        pe.wait_ge(gpre_act, n - 3)
                        pe.wait_ge(gpre_dve, n - 3)
                    d, h = n // 4, n % 4
                    mm(bank[n % 4][:, 0:T], w2sb[32 * d:32 * d + 32, h * P:(h + 1) * P], lrT[32 * d:32 * d + 32, :],
                       start=True, stop=True).then_inc(gpre_done, 1)
                pe.wait_ge(gpre_act, 8)
                pe.wait_ge(gpre_dve, 8)
                with pe.Fori(0, 2) as g:
                    for hh in range(2):
                        so = 3 * hh
                        for i in range(2):
                            pe.wait_ge(loaded[so + i], g * 16 + 16 * (BASE["gla"][so + i] + 1))
                            w = slots[so + i].rearrange("p (m k c) -> p m k c", m=2, k=KD)
                            for m in range(2):
                                for k in range(KD):
                                    last = mm(bank[2 * i + m][:, 0:T], w[:, m, k, :], hT[:, k, :], start=(k == 0),
                                              stop=(k == KD - 1))
                                    if i == 1 and m == 0 and k == 0:
                                        last.then_inc(free[so], 1)
                                last.then_inc(gproj_done, 1)
                        pe.wait_ge(loaded[so + 2], g * 16 + 16 * (BASE["gla"][so + 2] + 1))
                        w = slots[so + 2].rearrange("p (k c) -> p k c", k=KD)
                        for t in range(NT):
                            for k in range(KD):
                                last = mm(bank[4 + t // 2][:, t % 2 * 256:t % 2 * 256 + 256],
                                          hT[:, k, t * P:(t + 1) * P], w[:, k, :], start=(k == 0), stop=(k == KD - 1))
                                if t == 0 and k == 0:
                                    last.then_inc(free[so + 1], 1)
                        last.then_inc(gproj_done, 1)
                        pe.wait_ge(gproj_read, g * 10 + (5 * hh + 5))
                        pe.sem_inc(free[so + 2], 1)
                        def scores(q, b, bk):
                            pe.wait_ge(gmul, g * 12 + (q + 1))
                            for i in range(4):
                                last = mm(bk[0][:, i * SUB:(i + 1) * SUB], b["ex"][:, i, :], b["qx"][:, i, :],
                                          start=True, stop=True)
                            last.then_inc(gA_done, 1)
                            tr(bk[1][:, 0:P], b["kd"], ident).then_inc(gkd_tr, 1)

                        for d in range(2):
                            scores(6 * hh + d, glp[d], bank[d::2])
                        for stp in range(NT):
                            chunk = (stp, (0, 2, 1)[stp])
                            q0 = 6 * hh + 2 * stp
                            for d in range(2):
                                b, bk, c = glp[2 * stp + d], bank[d::2], chunk[d]
                                pe.wait_ge(gA_read, g * 12 + (q0 + d + 1))
                                if stp < 2:
                                    pe.wait_ge(gkd_done, g * 8 + (4 * hh + 2 * stp + d + 1))
                                    scores(q0 + 2 + d, glp[2 * stp + 2 + d], bk)
                                if stp == 1 and d == 0:
                                    pe.wait_ge(gs_loaded, g * 32 + (16 * hh + 16))
                                if stp:
                                    pe.wait_ge(go_read, g * 12 + (q0 - 2 + d + 1))
                                    pe.wait_ge(gs_done, g * 8 + (4 * hh + 2 * (stp - 1) + d + 1))
                                for j in range(2):
                                    dst = bk[2][:, j * P:(j + 1) * P]
                                    if stp:
                                        mm(dst, gS2[:, d, j * P:(j + 1) * P], b["qe"], start=True, stop=False)
                                    last = mm(dst, gv[:, c, j * P:(j + 1) * P], b["AT"], start=not stp, stop=True)
                                last.then_inc(go_done, 1)
                                if stp < 2:
                                    mm(bk[3][:, 0:GLA_V], b["kdT"], gv[:, c, :], start=True, stop=True)\
                                        .then_inc(gds_done, 1)
                        pe.wait_ge(gosq, g * 2 + (hh + 1))
                        for j in range(2):
                            last = mm(bank[0][:, 0:T], ones, gsq[:, j, :], start=(j == 0), stop=(j == 1))
                        last.then_inc(goms, 1)
                        pe.wait_ge(gorstd, g * 2 + (hh + 1))
                pe.wait_ge(gomix, 4)
                for m in range(KD):
                    n = m // 2
                    if m % 2 == 0:
                        pe.wait_ge(loaded[n], 16 * (BASE["glaout"][n] + 1))
                    if m >= 2:
                        pe.wait_ge(out_read, KD + m - 1)
                    w = slots[n].rearrange("p (m k c) -> p m k c", m=2, k=KD)
                    for k in range(KD):
                        last = mm(bank[m % 2][:, 0:T], w[:, m % 2, k, :], mix[:, k, :], start=(k == 0),
                                  stop=(k == KD - 1))
                        if k == 0 and m % 2 == 0 and m:
                            last.then_inc(free[n - 1], 1)
                    last.then_inc(out_done, 1)

            experts(0)
            mean_square(2)
            gla()
            mean_square(3, free[3])
            experts(1)
            mean_square(4)

        @block.scalar
        def _(act):
            A = act.activation
            act.wait_ge(const_loaded, 48)
            A(cs.rearrange("p a b -> p (a b)"), v("c"), ACT.Silu).then_inc(prep_exp, 1)
            A(z2, v("lam"), ACT.Abs).then_inc(prep_exp, 1)
            act.wait_ge(prep_exp, 2)
            A(z1, z2, ACT.Exp, scale=-1.0).then_inc(prep_exp, 1)
            A(hba.rearrange("p a b -> p (a b)"), v("lba"), ACT.Copy, scale=0.5).then_inc(prep_exp, 1)
            A(hbx.rearrange("p a b -> p (a b)"), v("lbx"), ACT.Copy, scale=0.5).then_inc(prep_exp, 1)

            def norm(n):
                if n == 0:
                    act.wait_ge(x_loaded, 16)
                elif n % 2 == 0:
                    act.wait_ge(x_ready, n)
                for k in range(KD):
                    if n % 2:
                        act.wait_ge(out_read, KD * (n // 2) + k + 1)
                    A(squares[:, k, :], xT[:, k, :], ACT.Square).then_inc(sq_done, 1)
                act.wait_ge(ms_done, n + 1)
                A(rstd, bank[6][:, 0:T], ACT.Ln, scale=1.0 / D, bias=cc("eps")).then_inc(ln_done, 1)
                act.wait_ge(ln_done, (1, 4, 5, 10, 11)[n])
                A(rstd, rstd, ACT.Exp, scale=-0.5).then_inc(rstd_done, 1)

            norm(0)
            link = step_counter(act, tail_act)
            link(A(arow, v("arow"), ACT.Exp))
            act.wait_ge(tail_done, 1)
            link(A(tu, bank[7][:, 0:T], ACT.Identity, scale=cc("sgn"), bias=v("trow")))
            link(A(tabs, tu, ACT.Abs))
            link(A(tabs, tabs, ACT.Exp, scale=-1.0))
            link(A(tabs, tabs, ACT.Ln, bias=1.0))
            act.sem_inc(proj_read, 2)

            with act.Fori(0, HG) as g:
                def load_gate_weights(i):
                    if i >= 2:
                        act.wait_ge(gates_done, g * 4 + (i - 1))
                    act.dma_start(lruw[:, i % 2], lruw_in[g * 4 + i])\
                        .then_inc((lruw0_loaded, lruw1_loaded)[i % 2], 16)

                def lru_gates(i):
                    act.wait_ge(gates_done, g * 4 + (i + 1))
                    if i:
                        act.wait_ge(lru_done, g * 4 + i)
                    for d in range(2):
                        A(rt[:, d, :], bank[2 + 2 * d][:, 0:T], ACT.Tanh, scale=0.5, bias=hba4(i, d, "a"))
                    for d in range(2):
                        last = A(it_[:, d, :], bank[3 + 2 * d][:, 0:T], ACT.Tanh, scale=0.5, bias=hba4(i, d, "x"))
                    last.then_inc(lru_tanh, 1)
                    act.wait_ge(lru_tanh, g * 4 + (i + 1))
                    for d in range(2):
                        n4 = gp[:, 0, i, d:d + 1]
                        A(aa[:, d, :], rt[:, d, :], ACT.Exp, scale=n4, bias=n4)
                    for d in range(2):
                        p4 = gp[:, 1, i, d:d + 1]
                        last = A(th[:, d, :], rt[:, d, :], ACT.Tanh, scale=p4, bias=p4)
                    last.then_inc(lru_mid, 1)

                def hba4(i, d, kind):
                    return gp[:, 2 if kind == "a" else 3, i, d:d + 1]

                act.wait_ge(group_start, g + 1)
                load_gate_weights(0)
                load_gate_weights(1)
                for b in range(28):
                    if b < 24:
                        act.wait_ge(proj_done, g * 24 + (b + 1))
                        src = bank[b % 2][:, 0:T]
                        if b < 16:
                            if b >= 2:
                                act.wait_ge(conv_done, g * 16 + (b - 1))
                            A(pad[b % 2][:, 2:2 + T_PROMPT], src[:, 0:T_PROMPT], ACT.Copy)
                            A(pad[b % 2][:, 133:133 + T_SAMPLE], src[:, T_PROMPT:T], ACT.Copy)\
                                .then_inc(proj_read, 1)
                        elif b < 20:
                            A(mix[:, g * 4 + (KD + b - 16), :], src, ACT.Silu).then_inc(proj_read, 1)
                        else:
                            if b >= 22:
                                act.wait_ge(y_mixed, g * 4 + (b - 21))
                            A(gy[b % 2], src, ACT.Gelu_apprx_tanh).then_inc(proj_read, 1)
                    if 5 <= b < 17:
                        n = b - 5
                        act.wait_ge(conv_done, g * 16 + (b - 1 + 1))
                        if n >= 10:
                            act.wait_ge(tr_done, g * 8 + (n - 4 - 2 + 1))
                        dst = qT[:, n, :] if n < 4 else kT[:, n - 4, :] if n < 8 else vT[n % 2]
                        A(dst, cv[(b - 1) % 2], ACT.Silu).then_inc(silu_done, 1)
                    if b in LRU_SCANS:
                        act.wait_ge(lru_u, g * 4 + (LRU_SCANS.index(b) + 1))
                        A(rt, th, ACT.Sqrt, scale=0.25).then_inc(lru_sqrt, 1)
                    if b in LRU_GATES:
                        lru_gates(LRU_GATES.index(b))
                        if b in LRU_GATES[:2]:
                            load_gate_weights(LRU_GATES.index(b) + 2)
                    if b == 10:
                        act.wait_ge(ss_done, g * 8 + 4)
                        A(rowQ, bank[7][0:8, 0:T], ACT.Ln, bias=cc("eps", rows=8)).then_inc(lnr_done, 1)
                    if b == 14:
                        act.wait_ge(ss_done, g * 8 + 8)
                        A(rowK, bank[7][0:8, 0:T], ACT.Ln, bias=cc("eps", rows=8)).then_inc(lnr_done, 1)
                act.wait_ge(silu_done, g * 12 + 12)
                act.wait_ge(proj_read, g * 24 + 26)
                act.sem_inc(half_act, 1)

                for c in range(NT):
                    for n, dst in enumerate((Gs, Qs)):
                        act.wait_ge(gram_done, g * 6 + (2 * c + n + 1))
                        if c == 0 and n == 0:
                            act.wait_ge(half_dve, g + 1)
                            act.wait_ge(half_pool, g + 1)
                        A(dst[:, c].rearrange("p h t -> p (h t)"), bank[2 * c + n][:], ACT.Copy)\
                            .then_inc(gram_read, 1)
                act.wait_ge(cols_copied, g + 1)
                A(ecols[:, 1:4].rearrange("p a b c -> p (a b c)"), cols[:, 1:4].rearrange("p a b c -> p (a b c)"),
                  ACT.Exp)
                A(egl.rearrange("p a b -> p (a b)"), bank[7][:, 0:8 * NT], ACT.Exp).then_inc(cols_exp, 1)
                for stp in range(NT):
                    q0 = stp * 2
                    for x in range(2):
                        q, bk = quad[x], bank[3 * x:3 * x + 3]
                        act.wait_ge(arg_done, g * 6 + (q0 + x + 1))
                        A(q["N"], q["N"], ACT.Exp)
                        A(q["QK"], q["QK"], ACT.Exp)
                        A(q["qe"].rearrange("p a b -> p (a b)"), bk[1][:], ACT.Exp).then_inc(exp_done, 1)
                    for x in range(2):
                        q, bk = quad[x], bank[3 * x:3 * x + 3]
                        act.wait_ge(n_tr, g * 6 + (q0 + x + 1))
                        A(q["L"].rearrange("p a b -> p (a b)"), bk[2][:], ACT.Copy).then_inc(l_done, 1)
                    for lv in range(LEVELS - 1):
                        for x in range(2):
                            q, bk = quad[x], bank[3 * x:3 * x + 3]
                            act.wait_ge(u_tr, g * 36 + (q0 * 6 + 2 * lv + x + 1))
                            A(q["Tm"].rearrange("p a b -> p (a b)"), bk[0][:], ACT.Copy).then_inc(t_done, 1)
                    for x in range(2):
                        q, bk = quad[x], bank[3 * x:3 * x + 3]
                        act.wait_ge(vnew_done, g * 6 + (q0 + x + 1))
                        A(q["L"].rearrange("p a b -> p (a b)"), bk[1][:], ACT.Copy).then_inc(v_read, 1)
                act.wait_ge(oms, g + 1)
                for h in range(H):
                    last = A(qT[:, h, :], bank[h][:, 0:T], ACT.Ln, scale=1.0 / DK, bias=cc("eps"))
                last.then_inc(ln_done, 1)
                act.wait_ge(ln_done, g + 2)
                A(qT, qT, ACT.Exp, scale=-0.5).then_inc(orstd, 1)
            norm(1)

            def experts(layer):
                act.wait_ge(router_done, 2 * layer + 1)
                A(rt_s.rearrange("p a b -> p (a b)"), bank[7][:, 0:NT * E], ACT.Sigmoid).then_inc(router_sig, 1)
                act.wait_ge(gathered, 35 * layer + 1)
                for t in range(NT):
                    for half in range(2):
                        last = A(htok[:, t, half * 512:(half + 1) * 512], bank[2 * t + half][:], ACT.Copy)
                last.then_inc(gather_read, 1)
                act.wait_ge(routed, 2 * layer + 2)
                full = act.value_load(flag[0:1, 0:1])
                with act.If(full < 1):
                    picked(layer)
                with act.If(full >= 1):
                    dense(layer)

            def picked(layer):
                o = 48 * layer

                def take_gathered(half, count):
                    act.wait_ge(gathered, count)
                    A(xg[:, 4 * half:4 * half + 4, :].rearrange("p a b -> p (a b)"), bank[1 - half][:], ACT.Copy)\
                        .then_inc(gather_read, 1)

                for half in range(2):
                    take_gathered(half, 35 * layer + 2 + half)
                with act.Fori(0, E // 2) as ep:
                    for n in range(2):
                        act.wait_ge(gate_done, ep * 2 + (o + n + 1))
                        A(sg1, bank[2][:], ACT.Silu).then_inc(sg_done, 1)
                        take_gathered(0, ep * 4 + (35 * layer + 2 * n + 4))
                        act.wait_ge(htr_done, ep * 2 + (o + n + 1))
                        A(hidT1, bank[4][:], ACT.Copy).then_inc(hidT_done, 1)
                        take_gathered(1, ep * 4 + (35 * layer + 2 * n + 5))
                        for half in range(2):
                            act.wait_ge(down_done, ep * 6 + (o + 3 * n + half + 2))
                            A(yo[:, half * 512:(half + 1) * 512], bank[5 + half][:], ACT.Copy).then_inc(y_read, 1)
                act.wait_ge(y_read, 32 * (layer + 1))
                act.sem_inc(sg_done, 32)
                act.sem_inc(hidT_done, 32)

            def dense(layer):
                o = 48 * layer
                with act.Fori(0, E // 2) as ep:
                    def turned(n):
                        act.wait_ge(htr_done, ep * 6 + (o + n + 1))
                        A(hidT[n % 2], bank[4][:], ACT.Copy).then_inc(hidT_done, 1)

                    for n in range(6):
                        act.wait_ge(gate_done, ep * 6 + (o + n + 1))
                        A(sg[n % 2], bank[n % 2][:], ACT.Silu).then_inc(sg_done, 1)
                        if n:
                            turned(n - 1)
                    turned(5)
                act.wait_ge(hidT_done, o + 48)
                act.sem_inc(gather_read, 34)
                act.sem_inc(y_read, 32)

            def gla():
                act.wait_ge(glr_done, 1)
                A(lrT, bank[7][:, 0:T], ACT.Copy).then_inc(glr_copied, 1)
                for n in range(8):
                    act.wait_ge(gpre_done, n + 1)
                    A(gabs[:, n, :], bank[n % 4][:, 0:T], ACT.Abs, bias=v("glb", n, n + 1)).then_inc(gpre_act, 1)
                act.wait_ge(gpre_act, 8)
                A(gabs, gabs, ACT.Exp, scale=-1.0).then_inc(gexp, 1)
                act.wait_ge(gexp, 1)
                A(gabs, gabs, ACT.Ln, bias=1.0).then_inc(gexp, 1)
                with act.Fori(0, 2) as g:
                    for hh in range(2):
                        for stp in range(NT):
                            chunk = (stp, (0, 2, 1)[stp])
                            q0 = 6 * hh + 2 * stp
                            for d in range(2):
                                b, c = glp[2 * stp + d], chunk[d]
                                gc = gch[:, d, c * P:(c + 1) * P]
                                gl = gc[:, P - 1:P] if d == 0 else gc[:, 0:1]
                                act.wait_ge(gargs, g * 24 + (2 * (q0 + d) + 2))
                                A(b["ex"], b["ex"], ACT.Exp, scale=-1.0)
                                A(b["qx"], b["qx"], ACT.Exp)
                                A(b["qe"], gc, ACT.Exp)
                                A(b["egl"], gl, ACT.Exp)
                                A(b["kd"], gc, ACT.Exp, scale=-1.0, bias=gl).then_inc(gexps, 1)
                        n0 = 5 * hh
                        act.wait_ge(gproj_done, g * 10 + (n0 + 1))
                        if hh == 0:
                            act.wait_ge(ghead, g * 2 + 1)
                        A(gq, bank[0][:, 0:T], ACT.Copy, scale=DK ** -0.5).then_inc(gproj_read, 1)
                        act.wait_ge(gproj_done, g * 10 + (n0 + 2))
                        A(gk, bank[1][:, 0:T], ACT.Copy).then_inc(gproj_read, 1)
                        for j in range(2):
                            act.wait_ge(gproj_done, g * 10 + (n0 + 3 + j))
                            A(mix[:, g * 4 + (2 * hh + j), :], bank[2 + j][:, 0:T], ACT.Silu).then_inc(gproj_read, 1)
                        act.wait_ge(gproj_done, g * 10 + (n0 + 5))
                        A(gv[:, 0:2].rearrange("p a b -> p (a b)"), bank[4][:], ACT.Copy)
                        A(gv[:, 2], bank[5][:, 0:GLA_V], ACT.Copy).then_inc(gproj_read, 1)
                        for stp in range(2):
                            q0 = 6 * hh + 2 * stp
                            for d in range(2):
                                act.wait_ge(gkd_tr, g * 12 + (q0 + d + 1))
                                A(glp[2 * stp + d]["kdT"], bank[d::2][1][:, 0:P], ACT.Copy).then_inc(gkd_done, 1)
                        act.wait_ge(goms, g * 2 + (hh + 1))
                        act.dma_start(gS2, s_gla[g * 2 + (hh + 1)]).then_inc(gs_loaded, 16)
                        A(grstd, bank[0][:, 0:T], ACT.Ln, scale=1.0 / GLA_V, bias=cc("eps")).then_inc(ln_done, 1)
                        act.wait_ge(ln_done, g * 2 + (hh + 6))
                        A(grstd, grstd, ACT.Exp, scale=-0.5).then_inc(gorstd, 1)

            experts(0)
            norm(2)
            gla()
            norm(3)
            experts(1)
            norm(4)

        @block.gpsimd
        def _(pool):
            TT = pool.tensor_tensor
            pool.wait_ge(rows_ready, 1)
            with pool.Fori(0, HG) as g:
                pool.wait_ge(group_start, g + 1)
                for j in range(8):
                    pool.wait_ge(silu_done, g * 12 + (j + 1))
                    if j >= 2:
                        pool.wait_ge(ss_done, g * 8 + (j - 1))
                    src = qT[:, j, :] if j < 4 else kT[:, j - 4, :]
                    TT(sqb[j % 2], src, src, ALU.mult).then_inc(sq_pool, 1)
                pool.wait_ge(sq_pool, g * 8 + 8)
                pool.sem_inc(half_pool, 1)
                pool.wait_ge(cols_exp, g + 1)
                for stp in range(NT):
                    chunk = (stp, (0, 2, 1)[stp])
                    q0 = stp * 2
                    for x in range(2):
                        q, c = quad[x], chunk[x]
                        if stp:
                            pool.wait_ge(o_read, g * 6 + (q0 - 2 + x + 1))
                            pool.wait_ge(s_done, g * 4 + (q0 - 2 + x + 1))
                        TT(q["kdec"], kTok[:, c], bc3(ecols[:, 3, c, 4 * x:4 * x + 4], P), ALU.mult)
                        TT(q["vb"], vTok[:, c], bc3(ecols[:, 1, c, 4 * x:4 * x + 4], P), ALU.mult)
                        pool.wait_ge(exp_done, g * 6 + (q0 + x + 1))
                        TT(q["QK"], q["QK"], Qs[:, c], ALU.mult)
                        TT(q["qe"], q["qe"], qT[:, :, c * P:(c + 1) * P], ALU.mult).then_inc(quad_pool, 1)
                pool.wait_ge(quad_pool, g * 6 + 6)

            with pool.Fori(0, 2) as g:
                for hh in range(2):
                    pool.wait_ge(gproj_read, g * 10 + (5 * hh + 2))
                    for stp in range(NT):
                        chunk = (stp, (0, 2, 1)[stp])
                        q0 = 6 * hh + 2 * stp
                        for d in range(2):
                            b, sl = glp[2 * stp + d], slice(chunk[d] * P, (chunk[d] + 1) * P)
                            pool.wait_ge(gexps, g * 12 + (q0 + d + 1))
                            TT(b["ex"], b["ex"], bcm(gk[:, sl], 4), ALU.mult)
                            TT(b["qx"].rearrange("p a b -> p (a b)"), b["qx"].rearrange("p a b -> p (a b)"), gq[:, sl],
                               ALU.mult)
                            TT(b["qe"], b["qe"], gq[:, sl], ALU.mult)
                            TT(b["kd"], b["kd"], gk[:, sl], ALU.mult).then_inc(gmul, 1)

        @block.vector
        def _(dve):
            V = nc.vector
            TT, TS, STT = V.tensor_tensor, V.tensor_scalar, V.scalar_tensor_tensor
            dve.wait_ge(const_loaded, 48)
            link = line = step_counter(dve, prep)
            dve.wait_ge(prep_exp, 5)
            link(TS(z3, z1, 2.0, None, ALU.add))
            link(V.reciprocal(z4, z3))
            link(TT(z2, z1, z4, ALU.mult))
            link(TT(z3, z2, z2, ALU.mult))
            link(TS(z4, z3, 1.0 / 15, 1.0 / 13, ALU.mult, ALU.add))
            for m in (11, 9, 7, 5, 3, 1):
                link(TT(z4, z4, z3, ALU.mult))
                link(TS(z4, z4, 1.0 / m, None, ALU.add))
            link(TT(z4, z4, z2, ALU.mult))
            link(TS(z4, z4, 2.0, None, ALU.mult))
            link(TS(z3, v("lam"), -1.0, 0.0, ALU.mult, ALU.max))
            spf = sp.rearrange("p a b -> p (a b)")
            link(TT(spf, z4, z3, ALU.add))
            link(TS(nsp4.rearrange("p a b -> p (a b)"), spf, -4.0, None, ALU.mult))
            link(TS(psp4.rearrange("p a b -> p (a b)"), spf, 4.0, None, ALU.mult))
            dve.sem_inc(lru_prep, 1)

            def copy_of(dst, src):
                return TT(dst, src, src, ALU.max)

            def modulation(layer, src, first, n):
                TT(mod[layer][:, bass.ds(first, n), :], src[:, 0:2 * n].rearrange("p (a b) -> p a b", b=2),
                   bc3(vecs[:, bass.ds(first + (VC["ada_b"][0] + 48 * layer), n)], 2), ALU.add).then_inc(mod_read, 1)

            def norm(n, permuted=False):
                layer, second = n // 2, n % 2
                dve.wait_ge(rstd_done, n + 1)
                m = mod[layer]
                sc, sh = m[:, 24 * second + 8:24 * second + 16, :], m[:, 24 * second:24 * second + 8, :]
                gn = v("n2" if second else "n1", 8 * layer, 8 * layer + 8)
                TS(gain, sc, 1.0, None, ALU.add).then_inc(normed_done, 1)
                dve.wait_ge(normed_done, 3 * n + 1)
                TT(gain, gain, bc3(gn, 2), ALU.mult).then_inc(normed_done, 1)
                TT(normed, xT[:], bcm(rstd, KD), ALU.mult).then_inc(normed_done, 1)
                dve.wait_ge(normed_done, 3 * n + 3)
                for k in range(KD):
                    for q, t0, tn in SEGS:
                        src, dst = normed[:, k, t0:t0 + tn], hT[:, k, t0:t0 + tn]
                        if permuted and q:
                            src = src.rearrange("p (r w) -> p w r", w=GRID_W)
                            dst = dst.rearrange("p (w r) -> p w r", w=GRID_W)
                        last = TS(dst, src, gain[:, k, q:q + 1], sh[:, k, q:q + 1], ALU.mult, ALU.add)
                last.then_inc(h_ready, 1)

            dve.sem_inc(mod_read, 1)
            with dve.Fori(0, 2) as r:
                for half in range(2):
                    dve.wait_ge(free[RING - 1], r * 2 + (BASE["ada0"][RING - 1] + 2 + half))
                    for n in range(3):
                        last = V.tensor_copy(mrow[half][:, n * 512:(n + 1) * 512], bank[3 * half + n][0:2, :])
                    last.then_inc(mod_rows, 1)
                    dve.wait_ge(mod_turned, r * 2 + (half + 1))
                    modulation(0, bank[7], r * 24 + 12 * half, 12)
            dve.wait_ge(mod_read, 5)
            norm(0)
            dve.wait_ge(tail_act, 5)
            link(STT(tv_, tu, 0.0, tabs, ALU.max, ALU.add))
            link(TS(tv_, tv_, arow, -1.0, ALU.mult, ALU.mult))
            for g in range(HG):
                V.tensor_copy(gR[:, g, :], tv_[32 * g:32 * g + 8, :])
                link(V.tensor_copy(lbR[:, g, :], tv_[64 + 32 * g:64 + 32 * g + 8, :]))
            for g in range(HG):
                for c in range(NT):
                    sl = slice(c * P, (c + 1) * P)
                    link(V.tensor_tensor_scan(psR[:, g, sl], cc("ones", rows=8), gR[:, g, sl], 0.0, ALU.mult,
                                              ALU.add))
            for g in range(HG):
                p3 = psR[:, g, :].rearrange("p (c t) -> p c t", t=P)
                g3 = gR[:, g, :].rearrange("p (c t) -> p c t", t=P)
                t3 = pt[:, g, :].rearrange("p (c t) -> p c t", t=P)
                link(V.tensor_copy(glR[:, g, :], p3[:, :, P - 1]))
                link(TT(t3, g3, bc3(glR[:, g, :], P), ALU.add))
                link(STT(pt[:, g, :], psR[:, g, :], -2.0, pt[:, g, :], ALU.mult, ALU.add))
                link(STT(gcR[:, g, :], pt[:, g, :], cc("bwd", rows=8), psR[:, g, :], ALU.mult, ALU.add))
            dve.sem_inc(rows_ready, 1)

            with dve.Fori(0, HG) as g:
                for n, src in enumerate((nsp4, psp4, hba, hbx)):
                    V.tensor_copy(gp[:, n], src[:, bass.ds(g * 4, 4), :])
                V.tensor_copy(gpx[:, 0:16], vecs[:, bass.ds(g * 16 + VC["lcw"][0], 16)])
                V.tensor_copy(gpx[:, 16:20], vecs[:, bass.ds(g * 4 + VC["lcb"][0], 4)])
                for n in range(3):
                    V.tensor_copy(gpx[:, 20 + 16 * n:36 + 16 * n],
                                  vecs[:, bass.ds(g * 16 + (VC["gcw"][0] + 32 * n), 16)])
                    V.tensor_copy(gpx[:, 68 + 4 * n:72 + 4 * n],
                                  vecs[:, bass.ds(g * 4 + (VC["gcb"][0] + 8 * n), 4)])
                V.tensor_copy(gpx[:, 80:88], vecs[:, bass.ds(g * 8 + VC["h0"][0], 8)])
                for n in range(2):
                    V.memset(pad[n][:, 0:2], 0.0)
                    V.memset(pad[n][:, 130:133], 0.0)
                    last = V.memset(pad[n][:, 389:390], 0.0)
                last.then_inc(group_start, 1)
                dve.wait_ge(group_start, g + 1)

                link = step_counter(dve, conv_step)
                CONV = 3 * 16

                def conv(b):
                    kind, i = b // 4, b % 4
                    w = gpx[:, 4 * i:4 * i + 4] if kind == 0 else \
                        gpx[:, 20 + 16 * (kind - 1) + 4 * i:24 + 16 * (kind - 1) + 4 * i]
                    bias = gpx[:, 16 + i:17 + i] if kind == 0 else gpx[:, 64 + 4 * kind + i:65 + 4 * kind + i]
                    x, dst = pad[b % 2], (xc[:, i, :] if kind == 0 else cv[b % 2])
                    dve.wait_ge(proj_read, g * 24 + (b + 3))
                    link(TS(acc, x[:, 0:387], w[:, 0:1], bias, ALU.mult, ALU.add), g * CONV)
                    for n in range(1, 3):
                        link(STT(acc, x[:, n:n + 387], w[:, n:n + 1], acc, ALU.mult, ALU.add), g * CONV)
                    if b >= 6:
                        dve.wait_ge(silu_done, g * 12 + (b - 6 + 1))
                    STT(dst[:, 0:T_PROMPT], x[:, 3:3 + T_PROMPT], w[:, 3:4], acc[:, 0:T_PROMPT], ALU.mult, ALU.add)
                    STT(dst[:, T_PROMPT:T], x[:, 134:134 + T_SAMPLE], w[:, 3:4], acc[:, 131:387], ALU.mult,
                        ALU.add).then_inc(conv_done, 1)
                    dve.wait_ge(conv_done, g * 16 + (b + 1))

                def lru_factors(i):
                    dve.wait_ge(lru_mid, g * 4 + (i + 1))
                    TT(rt, aa, aa, ALU.mult).then_inc(lru_b, 1)
                    STT(it_, it_, 1.0, xc[:, i, :].unsqueeze(1).to_broadcast([P, 2, T]), ALU.add, ALU.mult)
                    dve.wait_ge(lru_b, g * 24 + (6 * i + 1))
                    STT(th, rt, 1.0, th, ALU.add, ALU.mult).then_inc(lru_u, 1)

                def lru_scan(i):
                    dve.wait_ge(lru_sqrt, g * 4 + (i + 1))
                    TT(it_, it_, rt, ALU.mult).then_inc(lru_b, 1)
                    dve.wait_ge(lru_b, g * 24 + (6 * i + 2))
                    scan = V.tensor_tensor_scan
                    h0f, h0b = gpx[:, 80 + 2 * i:81 + 2 * i], gpx[:, 81 + 2 * i:82 + 2 * i]
                    scan(hf[:, 0:128], aa[:, 0, 0:128], it_[:, 0, 0:128], 0.0, ALU.mult, ALU.add)
                    scan(hf[:, 128:T], aa[:, 0, 128:T], it_[:, 0, 128:T], h0f, ALU.mult, ALU.add)
                    scan(hb[:, 0:128][:, ::-1], aa[:, 1, 0:128][:, ::-1], it_[:, 1, 0:128][:, ::-1], 0.0, ALU.mult,
                         ALU.add)
                    scan(hb[:, 128:T][:, ::-1], aa[:, 1, 128:T][:, ::-1], it_[:, 1, 128:T][:, ::-1], h0b,
                         ALU.mult, ALU.add).then_inc(lru_b, 1)
                    dve.wait_ge(lru_b, g * 24 + (6 * i + 3))
                    copy_of(lru_st[:, bass.ds(g * 4 + i, 1), 0], hf[:, 127:128]).then_inc(lru_b, 1)
                    copy_of(lru_st[:, bass.ds(g * 4 + i, 1), 1], hb[:, 0:1]).then_inc(lru_b, 1)
                    TT(mix[:, g * 4 + i, :], hf, hb, ALU.add).then_inc(lru_b, 1)
                    dve.wait_ge(lru_b, g * 24 + (6 * i + 6))
                    dve.sem_inc(lru_done, 1)

                for b in range(26):
                    if 11 <= b < 19:
                        j = b - 11
                        dve.wait_ge(tr_done, g * 8 + (j + 1))
                        dst = (kTok if j < 4 else vTok)[:, :, j % 4, :]
                        V.tensor_copy(dst, bank[6][:, 0:T].rearrange("p (c t) -> p c t", t=P))\
                            .then_inc(tr_read, 1)
                    if b < 16:
                        conv(b)
                    if b in LRU_SCANS:
                        lru_scan(LRU_SCANS.index(b))
                    if b in LRU_GATES:
                        lru_factors(LRU_GATES.index(b))
                    if b >= 22:
                        i = b - 22
                        dve.wait_ge(proj_read, g * 24 + (20 + i + 3))
                        m = mix[:, g * 4 + i, :]
                        TT(m, m, gy[i % 2], ALU.mult).then_inc(y_mixed, 1)
                link = step_counter(dve, rows_dve)
                RW = 7
                dve.wait_ge(lnr_done, g * 2 + 2)
                gc = gcR[:, g, :]
                link(STT(negC, rowK, -0.5, gc, ALU.mult, ALU.subtract), g * RW)
                link(STT(rowA, rowK, -0.5, gc, ALU.mult, ALU.add), g * RW)
                link(TT(rowA, rowA, lbR[:, g, :], ALU.add), g * RW)
                link(STT(rowQ, rowQ, -0.5, gc, ALU.mult, ALU.add), g * RW)
                link(TS(rowQ, rowQ, float(np.log(DK ** -0.5)), None, ALU.add), g * RW)
                link(TT(rowK.rearrange("p (c t) -> p c t", t=P), negC.rearrange("p (c t) -> p c t", t=P),
                        bc3(glR[:, g, :], P), ALU.add), g * RW)
                link(copy_of(lbS, lbR[:, g, :]), g * RW)
                assert link.n[0] == RW
                dve.wait_ge(y_mixed, g * 4 + 4)
                dve.wait_ge(tr_read, g * 8 + 8)
                dve.sem_inc(half_dve, 1)

                dve.wait_ge(cols_done, g + 1)
                V.tensor_copy(cols.rearrange("p a b c -> p (a b c)"), bank[6][:, 0:4 * NT * 8])\
                    .then_inc(cols_copied, 1)
                dve.wait_ge(cols_exp, g + 1)
                dve.wait_ge(cols_copied, g + 1)
                dve.wait_ge(gram_read, g * 6 + 6)
                TS(ecols[:, 2].rearrange("p a b -> p (a b)"), ecols[:, 2].rearrange("p a b -> p (a b)"), -1.0, None,
                   ALU.mult)
                for stp in range(NT):
                    chunk = (stp, (0, 2, 1)[stp])
                    q0 = stp * 2
                    both = [(x, chunk[x], quad[x], bank[3 * x:3 * x + 3]) for x in range(2)]
                    for x, c, q, bk in both:
                        dve.wait_ge(bc_done, g * 6 + (q0 + x + 1))
                        for h in range(H):
                            nc_ = cols[:, 0, c, 4 * x + h:4 * x + h + 1]
                            STT(q["N"][:, h, :], bk[0][:, h * P:(h + 1) * P], nc_,
                                cc("neg_strict", x * P, x * P + P), ALU.add, ALU.add)
                            last = STT(q["QK"][:, h, :], bk[1][:, h * P:(h + 1) * P], nc_,
                                       cc("neg_incl", x * P, x * P + P), ALU.add, ALU.add)
                        last.then_inc(arg_done, 1)
                    for x, c, q, bk in both:
                        dve.wait_ge(exp_done, g * 6 + (q0 + x + 1))
                        TT(q["N"], q["N"], Gs[:, c], ALU.mult).then_inc(n_done, 1)
                        dve.wait_ge(n_done, g * 6 + (q0 + x + 1))
                        TT(q["U"], q["N"], bcm(cc("pair", x * P, x * P + P), H), ALU.mult).then_inc(u_init, 1)
                        dve.wait_ge(u_init, g * 6 + (q0 + x + 1))
                        TT(q["U"], bcm(ident, H), q["U"], ALU.subtract).then_inc(u_done, 1)
                    for lv in range(1, LEVELS):
                        b = 2 ** lv
                        n0 = q0 * 6 + 2 * (lv - 1)
                        for x, c, q, bk in both:
                            dve.wait_ge(y_done, g * 36 + (n0 + x + 1))
                            mk = cc("lev", x * 384 + (lv - 1) * 64, x * 384 + lv * 64)
                            TT(q["Ys"], bk[1][:, 0:256].rearrange("p (h c) -> p h c", h=H), bcm(mk, H), ALU.mult)\
                                .then_inc(y_masked, 1)
                        if lv == 5:
                            n = (12 + 4 * stp + 3) % RING
                            dve.wait_ge(free[n], g * 4 + (BASE["ab"][n] + 2 + (12 + 4 * stp + 3) // RING))
                            for n in range(2):
                                last = V.tensor_copy(mrow1[:, n * 512:(n + 1) * 512], bank[6 + n][0:2, :])
                            last.then_inc(mod_rows, 1)
                        for x, c, q, bk in both:
                            dve.wait_ge(du_done, g * 36 + (n0 + x + 1))
                            uv = q["U"].rearrange("p h (q t b) -> p h q t b", t=2, b=b)[:, :, :, 1 - x, :]
                            TT(uv, uv, bk[2][:, 0:256].rearrange("p (h q b) -> p h q b", h=H, b=b), ALU.subtract)\
                                .then_inc(u_done, 1)
                    dve.wait_ge(mod_turned, g * 3 + (4 + stp + 1))
                    modulation(1, bank[6], g * 24 + 8 * stp, 8)
                    for x, c, q, bk in both:
                        if stp:
                            dve.wait_ge(ks_done, g * 4 + (q0 - 2 + x + 1))
                            dve.wait_ge(quad_pool, g * 6 + (q0 + x + 1))
                            for h in range(H):
                                last = STT(q["Tm"][:, h, :], bank[6 + x][:, h * P:(h + 1) * P],
                                           ecols[:, 2, c, 4 * x + h:4 * x + h + 1], q["vb"][:, h, :], ALU.mult,
                                           ALU.add)
                            last.then_inc(r_done, 1)
                    for x, c, q, bk in both:
                        dve.wait_ge(o_done, g * 6 + (q0 + x + 1))
                        o = oT[:, :, c * P:(c + 1) * P]
                        first = stp + x == 0 or stp == 1
                        po = bk[2][:].rearrange("p (h t) -> p h t", h=H)
                        if first:
                            V.tensor_copy(o, po).then_inc(o_read, 1)
                        else:
                            TT(o, o, po, ALU.add).then_inc(o_read, 1)
                        dve.wait_ge(o_read, g * 6 + (q0 + x + 1))
                        if stp < 2:
                            dve.wait_ge(ds_done, g * 4 + (q0 + x + 1))
                            if stp == 0:
                                V.tensor_copy(S[:, x].rearrange("p a b -> p (a b)"), bk[0][:]).then_inc(s_done, 1)
                            else:
                                for h in range(H):
                                    last = STT(S[:, x, h, :], S[:, x, h, :], egl[:, 4 * x + h, c:c + 1],
                                               bk[0][:, h * P:(h + 1) * P], ALU.mult, ALU.add)
                                last.then_inc(s_done, 1)
                TT(kT, oT, oT, ALU.mult).then_inc(osq, 1)
                dve.wait_ge(orstd, g + 1)
                STT(oT, oT, v("gng"), qT, ALU.mult, ALU.mult).then_inc(group_done, 1)
                dve.wait_ge(group_done, g + 1)
                m = mix[:, bass.ds(g * 4 + KD, 4), :]
                TT(m, m, oT, ALU.mult).then_inc(omix, 1)
                dve.wait_ge(omix, g + 1)

            dve.wait_ge(mod_read, 11)
            for m in range(KD):
                dve.wait_ge(out_done, m + 1)
                for q, t0, tn in SEGS:
                    xs = xT[:, m, t0:t0 + tn]
                    last = STT(xs, bank[m % 2][:, t0:t0 + tn], mod[0][:, 16 + m, q:q + 1], xs, ALU.mult, ALU.add)
                last.then_inc(out_read, 1)
            dve.wait_ge(out_read, KD)
            dve.sem_inc(x_ready, 1)
            norm(1)

            def route(layer):
                L = line
                flat = lambda a: a.rearrange("p a b -> p (a b)")
                dve.wait_ge(router_sig, layer + 1)
                L(TT(rt_sel, rt_s, bcm(v("rb"), NT), ALU.add))
                four = flat(rt_sel).rearrange("p (g e) -> p g e", e=4)
                L(TT(rt_mx, four[:, :, 0::2], four[:, :, 1::2], ALU.max))
                L(TT(rt_mn, four[:, :, 0::2], four[:, :, 1::2], ALU.min))
                L(TT(rt_t, rt_mx[:, :, 0], rt_mx[:, :, 1], ALU.max))
                L(TT(rt_u, rt_mx[:, :, 0], rt_mx[:, :, 1], ALU.min))
                L(TT(rt_g, rt_mn[:, :, 0], rt_mn[:, :, 1], ALU.max))
                L(TT(rt_u, rt_u, rt_g, ALU.max))
                L(TT(rt_t, rt_t, rt_u, ALU.add))
                g3 = lambda a: a.rearrange("p (t g) -> p t g", g=4)
                L(V.tensor_reduce(rt_k, g3(rt_t), AX.X, ALU.max))
                L(TT(g3(rt_g), g3(rt_t), bc3(rt_k, 4), ALU.is_ge))
                L(TT(g3(rt_g), g3(rt_g), bcm(cc("i4"), NT), ALU.mult))
                L(V.tensor_reduce(rt_k, g3(rt_g), AX.X, ALU.min))
                L(TT(g3(rt_h), bc3(rt_k, 4), bcm(cc("i4"), NT), ALU.is_equal))
                member = rt_h.unsqueeze(2).to_broadcast([P, 12, 4])
                m4 = flat(rt_m).rearrange("p (g e) -> p g e", e=4)
                L(TT(m4, four, member, ALU.mult))
                L(TS(rt_u, rt_h, BIG, -BIG, ALU.mult, ALU.add))
                L(TT(m4, m4, rt_u.unsqueeze(2).to_broadcast([P, 12, 4]), ALU.add))
                for first, hot in ((True, rt_o1), (False, rt_o2)):
                    L(V.tensor_reduce(rt_k, rt_m, AX.X, ALU.max))
                    L(TT(rt_a, rt_m, bc3(rt_k, E), ALU.is_ge))
                    L(TT(rt_a, rt_a, bcm(cc("i16"), NT), ALU.mult))
                    L(V.tensor_reduce(rt_k, rt_a, AX.X, ALU.min))
                    L(TT(hot, bc3(rt_k, E), bcm(cc("i16"), NT), ALU.is_equal))
                    if first:
                        L(STT(flat(rt_m), flat(hot), -2.0 * BIG, flat(rt_m), ALU.mult, ALU.add))
                TT(rt_m, rt_o1, rt_o2, ALU.add).then_inc(routed, 1)
                dve.wait_ge(routed, 2 * layer + 1)
                L(TT(rt_a, rt_m, rt_s, ALU.mult))
                L(V.tensor_reduce(rt_k, rt_a, AX.X, ALU.add))
                L(V.reciprocal(rt_k, rt_k))
                L(TT(gates_, rt_a, bc3(rt_k, E), ALU.mult))
                dve.wait_ge(router_done, 2 * layer + 2)
                L(TT(rank[:, :, 0:E], bank[7][:, 64:64 + NT * E].rearrange("p (t e) -> p t e", t=NT), rt_m, ALU.mult))
                L(V.tensor_reduce(rt_k[:, 0:1], bank[7][:, 64 + NT * E:64 + (NT + 1) * E], AX.X, ALU.max))
                TS(flag[:, 0:1], rt_k[:, 0:1], CAP + 0.5, None, ALU.is_ge).then_inc(routed, 1)

            def experts(layer):
                dve.wait_ge(h_ready, 2 * layer + 2)
                TS(upper, cc("neg_incl", 0, P), -1.0, None, ALU.is_ge)
                V.memset(rank, 0.0)
                line(V.tensor_tensor_scan(places, ones, ones, 0.0, ALU.mult, ALU.add))
                route(layer)
                dve.wait_ge(routed, 2 * layer + 2)
                full = dve.value_load(flag[0:1, 0:1])
                with dve.If(full < 1):
                    picked(layer)
                with dve.If(full >= 1):
                    dense(layer)

            def picked(layer):
                o, c0 = 48 * layer, 128 * layer

                def choose(expert):
                    for t in range(NT):
                        last = TS(sel[:, t, :], places, rank[:, t, expert], None, ALU.is_equal)
                    last.then_inc(sel_done, 1)

                choose(slice(0, 1))
                with dve.Fori(0, E // 2) as ep:
                    for n in range(2):
                        dve.wait_ge(gathered, ep * 4 + (35 * layer + 2 * n + 3))
                        choose(bass.ds(ep * 2 + (n + 1), 1))
                        for t in range(NT):
                            last = TS(gsel[:, t, :], places, rank[:, t, bass.ds(ep * 2 + n, 1)],
                                      gates_[:, t, bass.ds(ep * 2 + n, 1)], ALU.is_equal, ALU.mult)
                        last.then_inc(sel_done, 1)
                        dve.wait_ge(sg_done, ep * 2 + (o + n + 1))
                        dve.wait_ge(up_done, ep * 2 + (o + n + 1))
                        TT(hid1, bank[3][:], sg1, ALU.mult).then_inc(hid_done, 1)
                        dve.wait_ge(down_done, ep * 6 + (o + 3 * n + 1))
                        V.tensor_copy(selT, bank[7][:, 0:T]).then_inc(selT_read, 1)
                        dve.wait_ge(comb_read, ep * 16 + (c0 + 8 * n + 1))
                        for m in range(KD):
                            dve.wait_ge(comb_done, ep * 16 + (c0 + 8 * n + m + 1))
                            for q, t0, tn in SEGS:
                                xs = xT[:, m, t0:t0 + tn]
                                last = STT(xs, bank[COMBINE[m % 4]][:, t0:t0 + tn], mod[layer][:, 40 + m, q:q + 1], xs,
                                           ALU.mult, ALU.add)
                            last.then_inc(comb_read, 1)
                dve.wait_ge(comb_read, c0 + 129)
                dve.sem_inc(hid_done, 32)
                dve.sem_inc(acc_done, 49)
                dve.sem_inc(acc_added, 6)

            def dense(layer):
                o = 48 * layer
                V.memset(mix[:, 0:KD, :], 0.0).then_inc(acc_done, 1)
                dve.wait_ge(acc_done, 49 * layer + 1)
                with dve.Fori(0, E // 2) as ep:
                    def add(n):
                        t = n % 3
                        dve.wait_ge(down_done, ep * 6 + (o + n + 1))
                        if t == 2:
                            dve.sem_inc(free[n // 3 * RING + 5], 1)
                        for half in range(2):
                            a = accf[:, t, half * 512:(half + 1) * 512]
                            last = TT(a, a, bank[5 + half][:], ALU.add)
                        last.then_inc(acc_done, 1)

                    for n in range(6):
                        dve.wait_ge(sg_done, ep * 6 + (o + n + 1))
                        dve.wait_ge(up_done, ep * 6 + (o + n + 1))
                        STT(hid[n % 2], bank[2 + n % 2][:], gates_[:, n % 3, bass.ds(ep * 2 + n // 3, 1)], sg[n % 2],
                            ALU.mult, ALU.mult).then_inc(hid_done, 1)
                        if n == 2 or n == 5:
                            dve.sem_inc(free[n // 3 * RING + 3], 1)
                        if n:
                            add(n - 1)
                    add(5)
                for n in range(2 * NT):
                    dve.wait_ge(acc_tr, 6 * layer + n + 1)
                    t, q = n // 2, min(n // 2, 1)
                    for j in range(4):
                        m = n % 2 * 4 + j
                        xs = xT[:, m, t * P:(t + 1) * P]
                        last = STT(xs, bank[n % 2][:, j * P:(j + 1) * P], mod[layer][:, 40 + m, q:q + 1], xs, ALU.mult,
                                   ALU.add)
                    last.then_inc(acc_added, 1)
                dve.wait_ge(acc_added, 6 * layer + 6)
                dve.sem_inc(sel_done, 33)
                dve.sem_inc(selT_read, 16)
                dve.sem_inc(comb_read, 128)

            def gla():
                TS(incl, cc("neg_incl").rearrange("p (a b) -> p a b", a=2), -1.0, None, ALU.is_ge)
                for n in range(8):
                    dve.wait_ge(gpre_act, n + 1)
                    TS(gmin[:, n, :], bank[n % 4][:, 0:T], v("glb", n, n + 1), 0.0, ALU.add, ALU.min)\
                        .then_inc(gpre_dve, 1)
                dve.wait_ge(gexp, 2)
                dve.wait_ge(gpre_dve, 8)
                link = line
                link(TT(gmin, gmin, gabs, ALU.subtract))
                link(TS(gmin, gmin, 1.0 / 16.0, None, ALU.mult))
                for n in range(8):
                    for c in range(NT):
                        src, dst = gmin[:, n, c * P:(c + 1) * P], gabs[:, n, c * P:(c + 1) * P]
                        if n >= 4:
                            src, dst = src[:, ::-1], dst[:, ::-1]
                        last = V.tensor_tensor_scan(dst, ones, src, 0.0, ALU.mult, ALU.add)
                link(last)
                dve.sem_inc(gs_saved, 16)
                with dve.Fori(0, 2) as g:
                    for hh in range(2):
                        for d in range(2):
                            last = copy_of(gch[:, d, :], gabs[:, g * 2 + (4 * d + hh), :])
                        last.then_inc(ghead, 1)
                        dve.wait_ge(ghead, g * 2 + (hh + 1))
                        for stp in range(NT):
                            chunk = (stp, (0, 2, 1)[stp])
                            q0 = 6 * hh + 2 * stp
                            for d in range(2):
                                b, c = glp[2 * stp + d], chunk[d]
                                gc = gch[:, d, c * P:(c + 1) * P]
                                ref = gc[:, SUB // 2 - 1 + d::SUB]
                                TT(b["qx"], gc.rearrange("p (i t) -> p i t", t=SUB), bc3(ref, SUB), ALU.subtract)
                                TT(b["ex"], bcm(gc, 4), bc3(ref, P), ALU.subtract).then_inc(gargs, 1)
                                dve.wait_ge(gargs, g * 24 + (2 * (q0 + d) + 1))
                                TS(b["ex"], b["ex"], -CLAMP, None, ALU.max).then_inc(gargs, 1)
                        def causal(stp, d):
                            dve.wait_ge(gA_done, g * 12 + (6 * hh + 2 * stp + d + 1))
                            TT(glp[2 * stp + d]["AT"], bank[d][:, 0:P], incl[:, d, :], ALU.mult).then_inc(gA_read, 1)

                        for d in range(2):
                            causal(0, d)
                        for stp in range(NT):
                            chunk = (stp, (0, 2, 1)[stp])
                            q0 = 6 * hh + 2 * stp
                            for d in range(2):
                                if stp < 2:
                                    causal(stp + 1, d)
                                b, c = glp[2 * stp + d], chunk[d]
                                dve.wait_ge(go_done, g * 12 + (q0 + d + 1))
                                o = go[:, :, c * P:(c + 1) * P]
                                po = bank[4 + d][:, 0:2 * P].rearrange("p (j t) -> p j t", j=2)
                                if stp + d == 0 or stp == 1:
                                    V.tensor_copy(o, po).then_inc(go_read, 1)
                                else:
                                    TT(o, o, po, ALU.add).then_inc(go_read, 1)
                                dve.wait_ge(go_read, g * 12 + (q0 + d + 1))
                                if stp < 2:
                                    dve.wait_ge(gds_done, g * 8 + (4 * hh + 2 * stp + d + 1))
                                    if stp == 0:
                                        dve.wait_ge(gs_saved, g * 32 + (16 * hh + 16))
                                        V.tensor_copy(gS[:, d, :], bank[6 + d][:, 0:GLA_V]).then_inc(gs_done, 1)
                                    else:
                                        STT(gS2[:, d, :], gS2[:, d, :], b["egl"], bank[6 + d][:, 0:GLA_V], ALU.mult,
                                            ALU.add).then_inc(gs_done, 1)
                        TT(gsq, go, go, ALU.mult).then_inc(gosq, 1)
                        dve.wait_ge(gorstd, g * 2 + (hh + 1))
                        for j in range(2):
                            last = STT(go[:, j, :], go[:, j, :], v("glg", j, j + 1), grstd, ALU.mult, ALU.mult)
                        last.then_inc(gfin, 1)
                        dve.wait_ge(gfin, g * 2 + (hh + 1))
                        m = mix[:, bass.ds(g * 4 + 2 * hh, 2), :]
                        TT(m, m, go, ALU.mult).then_inc(gomix, 1)
                        dve.wait_ge(gomix, g * 2 + (hh + 1))
                for m in range(KD):
                    dve.wait_ge(out_done, KD + m + 1)
                    for q, t0, tn in SEGS:
                        xs, ps = xT[:, m, t0:t0 + tn], bank[m % 2][:, t0:t0 + tn]
                        if q:
                            xs = xs.rearrange("p (r w) -> p w r", w=GRID_W)
                            ps = ps.rearrange("p (w r) -> p w r", w=GRID_W)
                        last = STT(xs, ps, mod[1][:, 16 + m, q:q + 1], xs, ALU.mult, ALU.add)
                    last.then_inc(out_read, 1)
                dve.wait_ge(out_read, 2 * KD)
                dve.sem_inc(x_ready, 1)

            dve.sem_inc(comb_read, 1)
            experts(0)
            dve.sem_inc(x_ready, 1)
            norm(2, permuted=True)
            gla()
            norm(3)
            experts(1)
            dve.sem_inc(x_ready, 1)
            dve.wait_ge(rstd_done, 5)
            TT(normed, xT[:], bcm(rstd, KD), ALU.mult).then_inc(normed_done, 1)
            dve.wait_ge(normed_done, 13)
            for k in range(KD):
                last = TS(hT[:, k, :], normed[:, k, :], v("nf", k, k + 1), None, ALU.mult)
                if k % 2:
                    last.then_inc(y_ready, 1)


def kernel(**inputs):
    import concourse.bacc as bacc
    from concourse.bass_utils import run_bass_kernel_spmd

    a = {k: np.asarray(x) for k, x in inputs.items()}

    def feat(x):
        x = np.moveaxis(x, -1, 0)
        return x.reshape(x.shape[0] // P, P, *x.shape[1:]).swapaxes(0, 1)

    def units_cols(w):
        n = w.shape[1]
        return w.reshape(KD, P, n // 256, 2, P).transpose(2, 1, 3, 0, 4).reshape(n // 256, P, SLOT)

    w_in = a["ab_w_in"][0]
    cols_of = {"y": 0, "x": 1024, "q": 2048, "k": 3072, "v": 4096, "z": 5120}
    ada = [units_cols(a["ada_w"][i]) for i in range(2)]
    ab = [[units_cols(w_in[:, cols_of[n] + 512 * g:cols_of[n] + 512 * g + 512]) for n in "xqkvzy"]
          + [ada[1][12 * g:12 * g + 12]] for g in range(HG)]
    about = a["ab_w_out"][0].reshape(2 * KD, P, KD, P).transpose(2, 1, 0, 3).reshape(KD, P, SLOT)

    def moe(i):
        out = []
        for e in range(E):
            for w in (a["moe_w_gate"], a["moe_w_up"]):
                out.append(w[i, e].reshape(2, 4, P, DE).transpose(0, 2, 1, 3).reshape(2, P, SLOT))
            out.append(a["moe_w_down"][i, e].reshape(2, 2, P, D).transpose(0, 2, 1, 3).reshape(2, P, SLOT))
        return out

    gw = a["gla_w_in"][0]
    gla = []
    for h in range(GLA_H):
        gla.append(units_cols(np.concatenate([gw[:, 128 * h:128 * h + 128], gw[:, 512 + 128 * h:640 + 128 * h]], 1)))
        gla.append(units_cols(gw[:, 2048 + 256 * h:2304 + 256 * h]))
        gla.append(gw[:, 1024 + 256 * h:1280 + 256 * h].reshape(KD, P, 256).transpose(1, 0, 2).reshape(1, P, SLOT))
    parts = {"ada0": [ada[0]], "ab": sum(ab, []), "about": [about],
             "moe0": moe(0), "gla": gla, "glaout": [units_cols(a["gla_w_out"][0])], "moe1": moe(1)}
    ws = np.concatenate([u for name, _ in PHASES for u in parts[name]])
    assert ws.shape == (N_UNITS, P, SLOT), ws.shape

    x = np.concatenate([a["x_prompt"][0], a["x_sample"][0]])
    xT = np.ascontiguousarray(feat(x))
    vec = np.zeros((P, NV), np.float32)

    def put(name, val):
        s, e = VC[name]
        vec[:val.shape[0], s:e] = val.reshape(val.shape[0], -1)

    put("c", feat(np.stack([a["c_ctx"], a["c"][0]])))
    put("ada_b", feat(a["ada_b"]).swapaxes(1, 2))
    put("n1", feat(a["norm1_g"]).swapaxes(1, 2))
    put("n2", feat(a["norm2_g"]).swapaxes(1, 2))
    put("nf", feat(a["final_norm_g"]))
    put("lcw", feat(a["lru_conv_w"][0]))
    put("lcb", feat(a["lru_conv_b"][0]))
    put("lba", feat(a["lru_ba"][0]))
    put("lbx", feat(a["lru_bx"][0]))
    put("lam", feat(a["lru_lam"][0]))
    put("gcw", feat(a["gdn_conv_w"][0]))
    put("gcb", feat(a["gdn_conv_b"][0]))
    put("gng", a["gdn_norm_g"][0][:, None])
    put("h0", feat(a["state_lru"][0, 0]))
    put("glb", feat(a["gla_b2"][0]).swapaxes(1, 2))
    put("glg", feat(a["gla_norm_g"][0]))
    put("rb", np.broadcast_to(a["router_b"], (P, E)))
    rows = np.zeros((2, 4, 32), np.float32)
    for g in range(HG):
        for n, name in enumerate(("gdn_a_log", "gdn_dt_bias")):
            rows[n, g, 0:8] = a[name][0][:, 4 * g:4 * g + 4].reshape(8)
    put("arow", rows[0].reshape(P, 1))
    put("trow", rows[1].reshape(P, 1))

    tail = np.zeros((D, 4, 32), np.float32)
    for n, off in enumerate((6144, 6160)):
        part = w_in[:, off:off + 16].reshape(D, 2, HG, H)
        for g in range(HG):
            tail[:, 2 * n + g, 0:8] = part[:, :, g, :].reshape(D, 8)
    tail = tail.reshape(KD, P, P).transpose(1, 0, 2)
    tail2 = np.zeros((D, 4, 32), np.float32)
    tail2[:, 0:2, 0:16] = gw[:, 3072:3104].reshape(D, 2, 16)
    tail2 = tail2.reshape(KD, P, P).transpose(1, 0, 2)
    w2 = np.zeros((2, 32, 512), np.float32)
    w2[:, 0:16] = a["gla_w2"][0]
    lruw = np.stack([a["lru_wa"][0, 0], a["lru_wx"][0, 0], a["lru_wa"][0, 1], a["lru_wx"][0, 1]])
    lruw = lruw.transpose(1, 2, 0, 3)
    s_gdn = a["state_gdn"][0, 0].reshape(2, HG, H, DK, P).transpose(1, 3, 0, 2, 4)
    s_gla = np.zeros((GLA_H + 1, DK, 2, GLA_V), np.float32)
    s_gla[:GLA_H] = a["state_gla"][0, 0].reshape(2, GLA_H, DK, GLA_V).transpose(1, 2, 0, 3)
    arrays = {"ws": ws, "vec": vec, "const": constants(), "x_in": xT, "rw_in": feat(a["router_w"].T),
              "tail_in": tail, "tail2_in": tail2, "w2_in": w2.reshape(64, 512), "lruw_in": lruw, "s_gdn": s_gdn,
              "s_gla": s_gla}
    arrays = {k: np.ascontiguousarray(x, dtype=np.float32) for k, x in arrays.items()}
    outs = {"y_out": (P, KD, T), "st_lru": (P, 8, 2), "st_gdn": (HG, 2, P, H, P), "st_gla": (GLA_H, P, 2, GLA_V)}
    nc = bacc.Bacc("TRN2", target_bir_lowering=False, num_devices=1)
    args = {k: nc.dram_tensor(k, x.shape, mybir.dt.float32, kind="ExternalInput").ap() for k, x in arrays.items()}
    st = {k: nc.dram_tensor(k, sh, mybir.dt.float32, kind="ExternalOutput").ap() for k, sh in outs.items()}
    build(nc, *args.values(), *[st[k] for k in ("y_out", "st_lru", "st_gdn", "st_gla")])
    r = run_bass_kernel_spmd(nc, [arrays], core_ids=[0]).results[0]
    y = r["y_out"].transpose(2, 1, 0).reshape(T, D)
    return (y[None, 0:T_PROMPT], y[None, T_PROMPT:],
            r["st_lru"].transpose(2, 1, 0).reshape(1, 1, 2, D),
            r["st_gdn"].transpose(1, 0, 3, 2, 4).reshape(1, 1, 2, HG * H, DK, P),
            r["st_gla"].transpose(2, 0, 1, 3).reshape(1, 1, 2, GLA_H, DK, GLA_V))
```
